# Optimizing a Trainium2 kernel written in Bass

```python
import numpy as np
import jax
import jax.numpy as jnp
from jax import lax

D_MODEL = 1024
BATCH = 1
SEQ = 512
DEPTH = 2

GRID_W = 64
CTX_LEN = 256
HEAD_DIM = 64
MIX_WIDTH = D_MODEL
ATT_WIDTH = MIX_WIDTH // 2
RET_WIDTH = MIX_WIDTH // 4
FOURIER_WIDTH = MIX_WIDTH - ATT_WIDTH - RET_WIDTH
ATT_Q_HEADS = ATT_WIDTH // HEAD_DIM
ATT_KV_HEADS = ATT_Q_HEADS // 4
ATT_GROUP = ATT_Q_HEADS // ATT_KV_HEADS
KV_WIDTH = ATT_KV_HEADS * HEAD_DIM
WINDOW = 128
BLOCK = 128
RET_HEADS = RET_WIDTH // HEAD_DIM
RET_CHUNK = 128
FOURIER_GROUPS = 4
FOURIER_DIM = FOURIER_WIDTH // FOURIER_GROUPS
PROJ_SIZES = (ATT_WIDTH, KV_WIDTH, KV_WIDTH, RET_WIDTH, RET_WIDTH, RET_WIDTH, RET_WIDTH, RET_WIDTH, FOURIER_WIDTH)
PROJ_WIDTH = ATT_WIDTH + 2 * KV_WIDTH + 5 * RET_WIDTH + FOURIER_WIDTH
D_FF = 4 * D_MODEL
N_MOD = 6
ROPE_BASE = 10000.0
EPS = 1e-6
NEG_INF = -1e30

kernel_name = 'hybrid_parallel_heads_dit_block'

def rms_norm(x, g):
    xf = x.astype(jnp.float32)
    y = xf * lax.rsqrt(jnp.mean(xf * xf, axis=-1, keepdims=True) + EPS)
    return (y * g.astype(jnp.float32)).astype(x.dtype)

def modulate(x, g, shift, scale):
    return rms_norm(x, g) * (1 + scale) + shift

def rope_table(pos, dim):
    half = dim // 2
    freqs = ROPE_BASE ** (-jnp.arange(half, dtype=jnp.float32) / half)
    ang = pos.astype(jnp.float32)[:, None] * freqs[None, :]
    return jnp.cos(ang)[:, None, :], jnp.sin(ang)[:, None, :]

def rope_rotate(x, cos, sin):
    cos = cos.astype(x.dtype)
    sin = sin.astype(x.dtype)
    x1, x2 = jnp.split(x, 2, axis=-1)
    return jnp.concatenate([x1 * cos - x2 * sin, x2 * cos + x1 * sin], axis=-1)

def axial_rope(x, row_tab, col_tab):
    xr, xc = jnp.split(x, 2, axis=-1)
    return jnp.concatenate([rope_rotate(xr, *row_tab), rope_rotate(xc, *col_tab)], axis=-1)

def split_heads(t, n_heads):
    return t.reshape(t.shape[0], t.shape[1], n_heads, -1)

def split_proj(p):
    offsets = np.cumsum(PROJ_SIZES)[:-1].tolist()
    return jnp.split(p, offsets, axis=-1)

def window_attention_latent(q, k, v, k_ctx, v_ctx, sink):
    b, s, _, d = q.shape
    nb = s // BLOCK
    lc = k_ctx.shape[1]
    qb = q.reshape(b, nb, BLOCK, ATT_KV_HEADS, ATT_GROUP, d)

    def band(t):
        tp = jnp.pad(t, ((0, 0), (BLOCK, BLOCK), (0, 0), (0, 0))).reshape(b, nb + 2, BLOCK, ATT_KV_HEADS, d)
        return jnp.concatenate([tp[:, :-2], tp[:, 1:-1], tp[:, 2:]], axis=2)

    kb, vb = band(k), band(v)
    scale = d ** -0.5
    s_band = jnp.einsum('bnqhgd,bnkhd->bnhgqk', qb, kb).astype(jnp.float32) * scale
    s_ctx = jnp.einsum('bnqhgd,bkhd->bnhgqk', qb, k_ctx).astype(jnp.float32) * scale
    qi = jnp.arange(BLOCK)
    kj = jnp.arange(3 * BLOCK)
    kpos = jnp.arange(nb)[:, None] * BLOCK - BLOCK + kj[None, :]
    in_window = jnp.abs(kj[None, :] - BLOCK - qi[:, None]) <= WINDOW
    valid = in_window[None] & ((kpos >= 0) & (kpos < s))[:, None, :]
    s_band = jnp.where(valid[None, :, None, None], s_band, NEG_INF)
    s_sink = jnp.broadcast_to(
        sink.astype(jnp.float32).reshape(1, 1, ATT_KV_HEADS, ATT_GROUP, 1, 1), s_band.shape[:-1] + (1,))
    p = jax.nn.softmax(jnp.concatenate([s_band, s_ctx, s_sink], axis=-1), axis=-1)
    p_band = p[..., :3 * BLOCK].astype(v.dtype)
    p_ctx = p[..., 3 * BLOCK:3 * BLOCK + lc].astype(v.dtype)
    o = (jnp.einsum('bnhgqk,bnkhd->bnqhgd', p_band, vb)
         + jnp.einsum('bnhgqk,bkhd->bnqhgd', p_ctx, v_ctx))
    return o.reshape(b, s, ATT_Q_HEADS * d)

def context_attention(q, k, v, sink):
    b, l, _, d = q.shape
    qg = q.reshape(b, l, ATT_KV_HEADS, ATT_GROUP, d)
    s = jnp.einsum('bqhgd,bkhd->bhgqk', qg, k).astype(jnp.float32) * d ** -0.5
    s_sink = jnp.broadcast_to(
        sink.astype(jnp.float32).reshape(1, ATT_KV_HEADS, ATT_GROUP, 1, 1), s.shape[:-1] + (1,))
    p = jax.nn.softmax(jnp.concatenate([s, s_sink], axis=-1), axis=-1)
    o = jnp.einsum('bhgqk,bkhd->bqhgd', p[..., :l].astype(v.dtype), v)
    return o.reshape(b, l, ATT_Q_HEADS * d)

def retention_scan(q, k, v, log_gamma, state0):
    b, l, h, _ = q.shape
    n = l // RET_CHUNK
    idx = jnp.arange(RET_CHUNK, dtype=jnp.float32)
    diff = idx[:, None] - idx[None, :]
    inner_decay = jnp.where(diff[None] >= 0,
                            jnp.exp(jnp.maximum(diff, 0.0)[None] * log_gamma[:, None, None]), 0.0)
    xi = jnp.exp((idx[:, None] + 1.0) * log_gamma[None, :])
    zeta = jnp.exp((RET_CHUNK - 1.0 - idx)[:, None] * log_gamma[None, :])
    chunk_decay = jnp.exp(RET_CHUNK * log_gamma)

    def to_chunks(t):
        return t.reshape(b, n, RET_CHUNK, h, t.shape[-1]).swapaxes(0, 1)

    def step(state, inp):
        qc, kc, vc = inp
        sc = jnp.einsum('bihd,bjhd->bhij', qc, kc) * inner_decay[None]
        inner = jnp.einsum('bhij,bjhe->bihe', sc, vc)
        cross = jnp.einsum('bihd,bhde->bihe', qc, state) * xi[None, :, :, None]
        new_state = (state * chunk_decay[None, :, None, None]
                     + jnp.einsum('bjhd,bjhe->bhde', kc * zeta[None, :, :, None], vc))
        return new_state, inner + cross

    final, out = lax.scan(step, state0, (to_chunks(q), to_chunks(k), to_chunks(v)))
    return out.swapaxes(0, 1).reshape(b, l, h, v.shape[-1]), final

def head_group_norm(o, g):
    mu = jnp.mean(o, axis=-1, keepdims=True)
    var = jnp.mean(jnp.square(o - mu), axis=-1, keepdims=True)
    y = (o - mu) * lax.rsqrt(var + EPS)
    return y.reshape(o.shape[0], o.shape[1], -1) * g.astype(jnp.float32)

def fourier_mix(u, w):
    b, l, _ = u.shape
    uf = u.astype(jnp.float32).reshape(b, l, FOURIER_GROUPS, FOURIER_DIM)
    y = jnp.fft.fft2(uf, axes=(1, 3), norm='ortho').real
    return jnp.einsum('blgc,gcd->blgd', y, w.astype(jnp.float32)).reshape(b, l, FOURIER_WIDTH).astype(u.dtype)

def sq_relu_mlp(h, w1, w2):
    return jnp.square(jax.nn.relu(h @ w1)) @ w2

def token_mixers(a_lat, a_ctx, w_in, w_out, q_g, k_g, sink, decay_logit, gn_g, four_w,
                 row_tab, col_tab, t_tab, need_ctx):
    aq, ak, av, rq, rk, rv, rgf, rgb, fu = split_proj(a_lat @ w_in)
    cq, ck, cv, crq, crk, crv, crgf, crgb, cfu = split_proj(a_ctx @ w_in)

    q = axial_rope(rms_norm(split_heads(aq, ATT_Q_HEADS), q_g), row_tab, col_tab)
    k = axial_rope(rms_norm(split_heads(ak, ATT_KV_HEADS), k_g), row_tab, col_tab)
    v = split_heads(av, ATT_KV_HEADS)
    kc = rms_norm(split_heads(ck, ATT_KV_HEADS), k_g)
    vc = split_heads(cv, ATT_KV_HEADS)
    att_lat = window_attention_latent(q, k, v, kc, vc, sink)

    log_gamma = -jax.nn.softplus(-decay_logit.astype(jnp.float32))

    def ret_qkv(tq, tk, tv):
        return (split_heads(tq, RET_HEADS).astype(jnp.float32),
                split_heads(tk, RET_HEADS).astype(jnp.float32) * HEAD_DIM ** -0.5,
                split_heads(tv, RET_HEADS).astype(jnp.float32))

    lq, lk, lv = ret_qkv(rq, rk, rv)
    lq = rope_rotate(lq, *t_tab)
    lk = rope_rotate(lk, *t_tab)
    xq, xk, xv = ret_qkv(crq, crk, crv)
    zero = jnp.zeros((a_lat.shape[0], RET_HEADS, HEAD_DIM, HEAD_DIM), jnp.float32)

    def flip(t):
        return jnp.flip(t, axis=1)

    oc_f, st_f = retention_scan(xq, xk, xv, log_gamma[0], zero)
    oc_b, st_b = retention_scan(flip(xq), flip(xk), flip(xv), log_gamma[1], zero)
    ol_f, _ = retention_scan(lq, lk, lv, log_gamma[0], st_f)
    ol_b, _ = retention_scan(flip(lq), flip(lk), flip(lv), log_gamma[1], st_b)

    def ret_out(o_f, o_b, gf, gb):
        y = (head_group_norm(o_f, gn_g) * jax.nn.silu(gf.astype(jnp.float32))
             + head_group_norm(o_b, gn_g) * jax.nn.silu(gb.astype(jnp.float32)))
        return y.astype(gf.dtype)

    ret_lat = ret_out(ol_f, flip(ol_b), rgf, rgb)

    four_lat = fourier_mix(fu, four_w)

    m_lat = jnp.concatenate([att_lat, ret_lat, four_lat], axis=-1) @ w_out
    if not need_ctx:
        return m_lat, None

    qc = rms_norm(split_heads(cq, ATT_Q_HEADS), q_g)
    att_ctx = context_attention(qc, kc, vc, sink)
    ret_ctx = ret_out(oc_f, flip(oc_b), crgf, crgb)
    four_ctx = fourier_mix(cfu, four_w)
    m_ctx = jnp.concatenate([att_ctx, ret_ctx, four_ctx], axis=-1) @ w_out
    return m_lat, m_ctx

def setup_inputs(seed: int = 0) -> dict:
    key = jax.random.key(seed)
    ks = jax.random.split(key, 20)
    f32 = jnp.float32

    def nrm(k, shape, scale):
        return jax.random.normal(k, shape, f32) * scale

    base_logit = jnp.asarray(np.log(2.0 ** (5 + np.arange(RET_HEADS)) - 1.0), f32)
    return {
        'x': nrm(ks[0], (BATCH, SEQ, D_MODEL), 1.0),
        'c': nrm(ks[1], (BATCH, D_MODEL), 1.0),
        'ctx': nrm(ks[2], (BATCH, CTX_LEN, D_MODEL), 1.0),
        'c_ctx': nrm(ks[3], (D_MODEL,), 1.0),
        'w_mod': nrm(ks[4], (DEPTH, D_MODEL, N_MOD * D_MODEL), 0.5 * D_MODEL ** -0.5),
        'b_mod': nrm(ks[5], (DEPTH, N_MOD * D_MODEL), 0.01),
        'norm1_g': 1.0 + nrm(ks[6], (DEPTH, D_MODEL), 0.01),
        'norm2_g': 1.0 + nrm(ks[7], (DEPTH, D_MODEL), 0.01),
        'w_in': nrm(ks[8], (DEPTH, D_MODEL, PROJ_WIDTH), D_MODEL ** -0.5),
        'w_out': nrm(ks[9], (DEPTH, MIX_WIDTH, D_MODEL), MIX_WIDTH ** -0.5),
        'q_norm_g': 1.0 + nrm(ks[10], (DEPTH, HEAD_DIM), 0.01),
        'k_norm_g': 1.0 + nrm(ks[11], (DEPTH, HEAD_DIM), 0.01),
        'attn_sink': nrm(ks[12], (DEPTH, ATT_Q_HEADS), 0.5),
        'ret_decay_logit': base_logit[None, None, :] + nrm(ks[13], (DEPTH, 2, RET_HEADS), 0.1),
        'ret_gn_g': 1.0 + nrm(ks[14], (DEPTH, RET_WIDTH), 0.01),
        'fourier_w': nrm(ks[15], (DEPTH, FOURIER_GROUPS, FOURIER_DIM, FOURIER_DIM), FOURIER_DIM ** -0.5),
        'w_ff1': nrm(ks[16], (DEPTH, D_MODEL, D_FF), D_MODEL ** -0.5),
        'w_ff2': nrm(ks[17], (DEPTH, D_FF, D_MODEL), D_FF ** -0.5),
    }

def reference(x, c, ctx, c_ctx, w_mod, b_mod, norm1_g, norm2_g, w_in, w_out, q_norm_g, k_norm_g,
              attn_sink, ret_decay_logit, ret_gn_g, fourier_w, w_ff1, w_ff2):
    s = x.shape[1]
    rows = s // GRID_W
    rr, cc = jnp.meshgrid(jnp.arange(rows), jnp.arange(GRID_W), indexing='ij')
    row_tab = rope_table(rr.reshape(-1), HEAD_DIM // 2)
    col_tab = rope_table(cc.reshape(-1), HEAD_DIM // 2)
    t_tab = rope_table(jnp.arange(s), HEAD_DIM)
    silu_c = jax.nn.silu(c)
    silu_cc = jax.nn.silu(c_ctx)
    h = ctx
    for l in range(DEPTH):
        need_ctx = l < DEPTH - 1
        mod_lat = jnp.split((silu_c @ w_mod[l] + b_mod[l])[:, None, :], N_MOD, axis=-1)
        mod_ctx = jnp.split((silu_cc @ w_mod[l] + b_mod[l])[None, None, :], N_MOD, axis=-1)
        a_lat = modulate(x, norm1_g[l], mod_lat[0], mod_lat[1])
        a_ctx = modulate(h, norm1_g[l], mod_ctx[0], mod_ctx[1])
        m_lat, m_ctx = token_mixers(a_lat, a_ctx, w_in[l], w_out[l], q_norm_g[l], k_norm_g[l], attn_sink[l],
                                    ret_decay_logit[l], ret_gn_g[l], fourier_w[l],
                                    row_tab, col_tab, t_tab, need_ctx)
        x = x + mod_lat[2] * m_lat
        x = x + mod_lat[5] * sq_relu_mlp(modulate(x, norm2_g[l], mod_lat[3], mod_lat[4]), w_ff1[l], w_ff2[l])
        if need_ctx:
            h = h + mod_ctx[2] * m_ctx
            h = h + mod_ctx[5] * sq_relu_mlp(modulate(h, norm2_g[l], mod_ctx[3], mod_ctx[4]), w_ff1[l], w_ff2[l])
    return x


_drawn_inputs = setup_inputs


def setup_inputs(seed=0):
    import zlib

    import numpy as np

    out = dict(_drawn_inputs(seed))
    spreads = {}
    factors = {'norm1_g': 8.0,
     'norm2_g': 8.0,
     'q_norm_g': 8.0,
     'k_norm_g': 8.0,
     'attn_sink': 8.0,
     'ret_gn_g': 8.0}
    for name, (base, spread) in spreads.items():
        noise = np.random.default_rng([zlib.crc32(name.encode()), seed]).standard_normal(out[name].shape)
        drawn = base * np.exp(spread * noise) if base else spread * noise
        out[name] = jnp.asarray(drawn.astype(out[name].dtype))
    for name, factor in factors.items():
        out[name] = (out[name] * factor).astype(out[name].dtype)
    return out
```

```python
import concourse.bass as bass
from concourse import mybir
from contextlib import ExitStack

P = 128
D, DEPTH, LAT, CTX = 1024, 2, 512, 256
KT = D // P
NT, NL = (LAT + CTX) // P, LAT // P
COLS = LAT + CTX
HD = 64
PROJ = 2304
GROUPS = [(0, 512), (512, 512), (1024, 512), (1536, 512), (2048, 256)]
DFF = 4096
CHUNK = 4
NCHUNK = DFF // P // CHUNK
UE = 1024
UP, UO, UF = 18, 8, 64
UL = UP + UO + UF
NMOD = 48
EPS = 1e-6
T_ID, T_MPREV, T_MNEXT, T_BLOCK, T_ROPE = 0, 128, 256, 384, 512
T_TMP = T_ROPE + NL * 256
TMP_DPOS, TMP_DNEG, TMP_MPOS, TMP_MNEG, TMP_C, TMP_S, TMP_IDX = 0, 128, 256, 384, 512, 640, 768
TMP_W = 772
TABLE = T_TMP + TMP_W


def proj_tiles(layer):
    out = []
    for g, (_, n) in enumerate(GROUPS):
        for t in range(NT):
            if layer == DEPTH - 1 and t >= NL and g in (0, 3, 4):
                continue
            out.append((g, t, 256 if (layer == DEPTH - 1 and t >= NL and g == 1) else n))
    return out


def build(nc, a):
    fp32, f32r, bf16 = mybir.dt.float32, mybir.dt.float32r, mybir.dt.bfloat16
    ALU, ACT, AX = mybir.AluOpType, mybir.ActivationFunctionType, mybir.AxisListType.X
    stack = ExitStack()

    def sb(name, shape, dt=fp32):
        return stack.enter_context(nc.sbuf_tensor(name, shape, dt))

    def overlay(*plans):
        got = []
        for n, plan in enumerate(plans):
            inner = ExitStack()
            target = stack if n == len(plans) - 1 else inner
            got.append([target.enter_context(nc.sbuf_tensor(*p)) for p in plan])
            inner.close()
        return got

    X = sb("X", [P, KT, COLS])
    (rs,), (Ahi, Alo) = overlay(
        [("ret_scratch", [P, 6, 512], fp32)],
        [("Ahi", [P, KT, COLS], f32r), ("Alo", [P, KT, COLS], f32r)])
    (Xin, rows, maskf), (Zs, Zc), (SD,), (Pb, PTs, AO), (Hhi, Hlo, tmpt), (Pq, Pk, Pr, Pg, Pu) = overlay(
        [("Xin", [P, NT, D], fp32), ("rows", [P, 2, P], fp32), ("maskf", [P, 2, P], fp32)],
        [("Zs", [P, 2, 2, LAT], fp32), ("Zc", [P, 2, 2, CTX], fp32)],
        [("SD", [P, 2, NT, 2, P], fp32)],
        [("Pb", [P, 2, 640], fp32), ("PTs", [P, 2, 640], fp32), ("AO", [P, 512], fp32)],
        [("Hhi", [P, 2, CHUNK, COLS], f32r), ("Hlo", [P, 2, CHUNK, COLS], f32r), ("tmpt", [P, 1536], fp32)],
        [("Pq", [P, NT, 512], fp32), ("Pk", [P, NT, 512], fp32), ("Pr", [P, NT, 512], fp32),
         ("Pg", [P, NT, 512], fp32), ("Pu", [P, NT, 256], fp32)])
    PG = [Pq, Pk, Pr, Pg, Pu]
    (Rt, Tb, Ab, sqb), (outs,), (_, _, scr), (qT, kT, rqT, rkT) = overlay(
        [("Rt", [P, COLS], fp32), ("Tb", [P, 2, COLS], fp32), ("Ab", [P, 2, COLS], fp32), ("sqb", [P, 2, COLS], fp32)],
        [("outs", [P, NL, D], fp32)],
        [("skip_q", [P, 4, COLS], fp32), ("skip_k", [P, COLS], fp32), ("scr", [P, 3, 512], fp32)],
        [("qT", [P, 4, COLS], fp32), ("kT", [P, COLS], fp32), ("rqT", [P, 2, COLS], fp32), ("rkT", [P, 2, COLS], fp32)])
    raw = sb("raw", [P, 2, UE])
    modraw = sb("modraw", [P, 2, UE])
    Whi = sb("Whi", [P, 2, UE], f32r)
    Wlo = sb("Wlo", [P, 2, UE], f32r)
    ident = sb("ident", [P, P])
    ones = sb("ones", [P, P])
    identb = sb("identb", [P, P], bf16)
    maskb = sb("maskb", [P, 2, P], bf16)
    block = sb("blockmask", [P, P])
    rope = sb("rope", [P, NL, 4, HD])
    ropeg = sb("ropeg", [P, NL, 4, HD])
    decay = sb("decay", [P, 2, 4, P])
    WCS = sb("WCS", [P, 2, 2, P])
    bmodT = sb("bmodT", [P, DEPTH, NMOD])
    parT = sb("parT", [P, 48])
    csil = sb("csil", [P, KT, 2])
    modT = sb("modT", [P, DEPTH, NMOD, 2])
    gs = sb("gs", [P, DEPTH, 2, KT, 2])
    qkg = sb("qkg", [P, DEPTH, 2, HD])
    gng = sb("gng", [P, DEPTH, 256])
    sinkb = sb("sinkb", [P, DEPTH, 8])
    nsink = sb("nsink", [P, DEPTH, 8])
    dlog = sb("dlog", [P, DEPTH, 8])
    lgt = sb("lgt", [P, 4, 16])
    XI = sb("XI", [P, 2, 4])
    ZE = sb("ZE", [P, 2, 4])
    CDa = sb("CDa", [P, 8])
    CD = sb("CD", [P, 2, 2])
    fw = tmpt[:, TMP_W:TMP_W + 2 * HD].rearrange("p (q d) -> p q d", q=2)
    ssq = sb("ssq", [P, NT, 10])
    srt = sb("srt", [P, NT, 10])
    mx = sb("mx", [P, 2])
    nm = sb("nm", [P, 2, 8])
    den = sb("den", [P, 2, 8])
    esi = sb("esi", [P, 8])
    es = sb("es", [P, 8])
    gst = sb("gst", [P, 4, 8])
    epst = sb("epst", [P, 1])

    def pb(name, n):
        return stack.enter_context(nc.psum_tensor(name, [P, n], fp32))

    psA, psB, psS = pb("psA", 1024), pb("psB", 1024), pb("psS", 1024)
    pair = [psA, psB]
    ps6, ps7 = pb("ps6", 512), pb("ps7", 512)
    tokbank = [psA[:, 0:512], psA[:, 512:1024], psB[:, 0:512], psB[:, 512:1024], psS[:, 0:512], psS[:, 512:1024]]

    names = """consts_in x_in tmp_in stored rows_T par_ready csil_ready mod_used mod_evac xT_ready x_ready
        stat_sq stat_used rt_sqrt dve a_full a_hi a_ready hi_done lo_done unit_done proj_ready p_ready qk_var qk_sqrt
        q_ready k_ready rq_ready rk_ready tr_ready tr_evac za_evac zb_evac zc_evac y_ready y_hi y_lo
        kz_ready kv_ready st_ready sc_ready md_ready ret_ready g_cent g_sq g_var g_sqrt ro_ready rT_ready rT_hi rT_lo
        s_ready s_max s_exp pt_ready pt_evac pv_ready es_in es_out ao_ready aoT_ready aoT_hi aoT_lo
        lin_ready relu_done h_full h_hi h_lo resid_done prep_lg prep_e prep_act prep_w prep_wd out_T out_a out_d
        act pool_init mask_ready""".split()
    S = {n: stack.enter_context(nc.semaphore(n)) for n in names}
    raw_in = [stack.enter_context(nc.semaphore(f"raw_in{i}")) for i in range(2)]
    mod_in = [stack.enter_context(nc.semaphore(f"mod_in{i}")) for i in range(2)]

    evac_index, n = {}, 0
    for l in range(DEPTH):
        for g, t, _ in proj_tiles(l):
            n += 2 if g == 2 else 1
            evac_index[l, g, t] = n
    TT = [NT, NL]
    CW = [COLS, LAT]
    SPLITS = [[(0, 512), (512, 256)], [(0, 512)]]
    MOD_FIRST = [[0, 16], [53]]
    DFT_FIRST = [48, 101]
    HPOS = [0, 2, 1, 3]
    LT = UO + 32 + 64
    trs = []
    for l in range(DEPTH):
        trs.append([("q", t) for t in range(TT[l])] + [("k", 0)] + [(k, p) for k in ("rq", "rk") for p in range(2)])
    TR_FIRST = [0, len(trs[0])]
    WALK = [[4, 5, 0, 1, 2, 3], [5, 4, 3, 2, 1, 0]]
    ITEMS = []
    for l in range(DEPTH):
        for b in range(TT[l]):
            for k in range(8):
                ITEMS.append((l, b, k // 2 + 4 * (k % 2), k))
    ITEM_FIRST = [0, 8 * TT[0]]

    def band(b):
        if b >= NL:
            return [], None, None
        ks = list(range(max(0, b - 1), min(NL, b + 2)))
        return ks, (0 if b > 0 else None), (len(ks) - 1 if b < NL - 1 else None)

    def unit_through(u):
        l, j = u // UL, u % UL
        if j < UP:
            return "unit_done", UP * l + j + 1
        j -= UP
        if j < UO:
            return "lin_ready", LT * l + j + 1
        j -= UO
        if j < 4:
            return "lin_ready", LT * l + UO + j + 1
        c, k = (j - 4) // 8, (j - 4) % 8
        if c == NCHUNK - 1:
            k += 4
        return "lin_ready", LT * l + UO + 4 + 12 * c + (k + 1 if k < 4 else 4 * (c < NCHUNK - 1) + 2 * (k - 3))

    def proj_signal(l, g, t):
        here = [tt for gg, tt, _ in proj_tiles(l) if gg == g]
        if t == here[-1]:
            return "unit_done", UP * l + (4 * g + 4 if g < 4 else UP)
        n = sum(len(proj_tiles(x)) - len(GROUPS) for x in range(l))
        for gg in range(g):
            n += sum(1 for x, _, _ in proj_tiles(l) if x == gg) - 1
        return "proj_ready", n + here.index(t) + 1

    blk = stack.enter_context(nc.Block())

    @blk.sync
    def _(sp):
        def w_load(u, slot, dst, src, first):
            if not first:
                sp.wait_ge(S["lo_done"], u - 1)
            sp.dma_start(dst, src).then_inc(raw_in[slot], 16)

        def m_load(w, slot, dst, src, first=False):
            if not first:
                sp.wait_ge(S["mod_used"], w - 1)
            sp.dma_start(dst, src).then_inc(mod_in[slot], 16)

        r8 = lambda slot: raw[:, slot, :].rearrange("p (k n) -> p k n", k=8)
        r2 = lambda slot: raw[:, slot, :].rearrange("p (k n) -> p k n", k=2)
        r4 = lambda slot: raw[:, slot, :].rearrange("p (k n) -> p k n", k=4)
        m8 = lambda slot: modraw[:, slot, :].rearrange("p (k n) -> p k n", k=8)

        def mod_src(l, tile):
            return a["w_mod"][l].rearrange("(k p) n -> p k n", p=P)[:, :, bass.ds(tile * P, P)]

        def proj_src(l, u):
            g, part = u // 4, u % 4
            c0, n = GROUPS[g]
            k = 2 if n == 512 else 4
            v = a["w_in"][l].rearrange("(k p) n -> p k n", p=P)
            return v[:, part * k:(part + 1) * k, c0:c0 + n]

        def ff1_src(l, f):
            return a["w_ff1"][l].rearrange("(k p) n -> p k n", p=P)[:, :, bass.ds(f * P, P)]

        def ff2_src(l, c, o):
            return a["w_ff2"][l].rearrange("(k p) n -> p k n", p=P)[:, bass.ds(c * CHUNK, CHUNK), o * 256:(o + 1) * 256]

        def tmp_load(l):
            sp.dma_start(tmpt[:, 0:TMP_W], a["table"][:, T_TMP:TABLE]).then_inc(S["tmp_in"], 16)
            for pp in range(2):
                sp.dma_start(fw[:, pp, :], a["fourier_w"][l, 2 * pp:2 * pp + 2].rearrange("g c d -> (g c) d"))\
                    .then_inc(S["tmp_in"], 16)

        con = S["consts_in"]
        sp.dma_start(ident[:, :], a["table"][:, T_ID:T_ID + P]).then_inc(con, 16)
        sp.dma_start(rows[0:96, 0, :], a["b_mod"].rearrange("l (t p) -> (l t) p", p=P)).then_inc(con, 16)
        for i, nme in enumerate(("norm1_g", "norm2_g")):
            sp.dma_start(rows[16 * i:16 * i + 16, 1, :], a[nme].rearrange("l (t p) -> (l t) p", p=P)).then_inc(con, 16)
        sp.dma_start(rows[32:40, 1, :], a["c"].rearrange("o (t p) -> (o t) p", p=P)).then_inc(con, 16)
        sp.dma_start(rows[40:48, 1, :], a["c_ctx"].rearrange("(t p) -> t p", p=P)).then_inc(con, 16)
        for w in range(2):
            m_load(w, w % 2, m8(w % 2), mod_src(0, w), True)
        sp.dma_start(maskf[:, :, :], a["table"][:, T_MPREV:T_MPREV + 2 * P].rearrange("p (a b) -> p a b", a=2)).then_inc(con, 16)
        sp.dma_start(block[:, :], a["table"][:, T_BLOCK:T_BLOCK + P]).then_inc(con, 16)
        sp.dma_start(rope[:, :, :, :].rearrange("p a b c -> p (a b c)"), a["table"][:, T_ROPE:T_TMP]).then_inc(con, 16)
        for i, nme in enumerate(("q_norm_g", "k_norm_g")):
            sp.dma_start(qkg[:, :, i, :], a[nme].partition_broadcast(P)).then_inc(con, 16)
        sp.dma_start(gng[:, :, :], a["ret_gn_g"].partition_broadcast(P)).then_inc(con, 16)
        sp.dma_start(sinkb[:, :, :], a["attn_sink"].partition_broadcast(P)).then_inc(con, 16)
        sp.dma_start(dlog[:, :, :], a["ret_decay_logit"].rearrange("l a h -> l (a h)").partition_broadcast(P)).then_inc(con, 16)
        tmp_load(0)
        for t in range(NT):
            src = a["x"][0, t * P:(t + 1) * P, :] if t < NL else a["ctx"][0, (t - NL) * P:(t - NL + 1) * P, :]
            sp.dma_start(Xin[:, t, :], src).then_inc(S["x_in"], 16)
        for w in range(2, 16):
            m_load(w, w % 2, m8(w % 2), mod_src(0, w))

        for l in range(DEPTH):
            u0 = l * UL
            for u in range(UP):
                dst = (r2 if u < 16 else r4)((u0 + u) % 2)
                w_load(u0 + u, (u0 + u) % 2, dst, proj_src(l, u), u0 + u < 2)
                if l == 0 and u < 16:
                    for w in (16 + 2 * u, 17 + 2 * u):
                        m_load(w, w % 2, m8(w % 2), mod_src(0, w))
            wo = a["w_out"][l].rearrange("(k p) n -> p k n", p=P)
            for u in range(2):
                w_load(u0 + UP + u, (u0 + UP + u) % 2, r8((u0 + UP + u) % 2), wo[:, :, u * P:(u + 1) * P], False)
            for k in range(NL):
                w = DFT_FIRST[l] + k
                m_load(w, w % 2, modraw[:, w % 2, :], a["dft_lat"][k])
            if l == 0:
                w = DFT_FIRST[l] + NL
                m_load(w, w % 2, modraw[:, w % 2, :], a["dft_ctx"])
            for u in range(2, UO):
                w_load(u0 + UP + u, (u0 + UP + u) % 2, r8((u0 + UP + u) % 2), wo[:, :, u * P:(u + 1) * P], False)
            uf = u0 + UP + UO
            if l == 0:
                sp.wait_ge(S["lin_ready"], UO)
                tmp_load(1)

            def mlp_mod(base, first_tile, k):
                if l == 0 and k < 6:
                    w = base + k
                    m_load(w, (MOD_FIRST[1][0] + k) % 2, m8((MOD_FIRST[1][0] + k) % 2), mod_src(1, first_tile + k))

            def half(c, par):
                for k in range(8):
                    mlp_mod(MOD_FIRST[1][0] + 6 + c * 6, 6 + c * 6, k)
                    u = uf + 4 + c * 8 + k
                    slot = (uf + k) % 2
                    if k < 4:
                        w_load(u, slot, r8(slot), ff1_src(l, (c + 1) * 4 + k), False)
                    else:
                        w_load(u, slot, r4(slot), ff2_src(l, c, k - 4), False)

            for k in range(4):
                mlp_mod(MOD_FIRST[1][0], 0, k)
                w_load(uf + k, (uf + k) % 2, r8((uf + k) % 2), ff1_src(l, k), False)
            for k in range(4, 6):
                mlp_mod(MOD_FIRST[1][0], 0, k)
            with sp.Fori(0, 7) as c:
                half(c, 0)
            for k in range(4):
                u = uf + 60 + k
                w_load(u, u % 2, r4(u % 2), ff2_src(l, NCHUNK - 1, k), False)
        for t in range(NL):
            sp.wait_ge(S["out_a"] if t % 2 == 0 else S["out_d"], t // 2 + 1)
            sp.dma_start(a["out"][0, t * P:(t + 1) * P, :], outs[:, t, :]).then_inc(S["stored"], 16)
        sp.wait_ge(S["stored"], 16 * NL)

    @blk.gpsimd
    def _(pool):
        nc.gpsimd.memset(WCS[:, :, :, :], 0.0).then_inc(S["pool_init"], 1)
        nc.gpsimd.memset(ones[:, :], 1.0 / D).then_inc(S["pool_init"], 1)
        nc.gpsimd.memset(epst[:, :], EPS).then_inc(S["pool_init"], 1)
        with pool.Fori(0, DEPTH * UL // 2) as i:
            for s in range(2):
                pool.wait_ge(S["hi_done"], i * 2 + s + 1)
                nc.gpsimd.tensor_tensor(Wlo[:, s, :], raw[:, s, :], Whi[:, s, :], ALU.subtract).then_inc(S["lo_done"], 1)

    @blk.scalar
    def _(act):
        def hi(slot, round_, sem, value):
            act.wait_ge(raw_in[slot], round_ * 16 + 16)
            if sem is not None:
                act.wait_ge(S[sem], value)
            nc.scalar.activation(Whi[:, slot, :], raw[:, slot, :], ACT.Copy).then_inc(S["hi_done"], 1)

        def hi_static(u):
            if u < DEPTH * UL:
                sem, value = unit_through(u - 2) if u >= 2 else (None, 0)
                hi(u % 2, u // 2, sem, value)

        act_count = [0]

        def link(ins):
            ins.then_inc(S["act"], 1)
            act_count[0] += 1
            act.wait_ge(S["act"], act_count[0])

        def stat_squares(n, m, cols, ready, value):
            s = 8 * n + m
            act.wait_ge(ready, value)
            if s >= 2:
                act.wait_ge(S["stat_used"], s - 1)
            nc.scalar.activation(sqb[:, m % 2, 0:cols], X[:, m, 0:cols], ACT.Square).then_inc(S["stat_sq"], 1)

        def norm(n, cols):
            act.wait_ge(S["stat_used"], 8 * n + 8)
            nc.scalar.activation(Rt[:, 0:cols], psS[:, 0:cols], ACT.Sqrt, bias=epst[:, 0:1]).then_inc(S["rt_sqrt"], 1)
            for k in range(KT):
                act.wait_ge(S["a_full"], 8 * n + k + 1)
                nc.scalar.activation(Ahi[:, k, 0:cols], Ab[:, k % 2, 0:cols], ACT.Copy).then_inc(S["a_hi"], 1)

        def prep(l):
            act.wait_ge(S["prep_lg"], 2 * l + 1)
            link(nc.scalar.activation(lgt[:, 1, 0:8], lgt[:, 0, 0:8], ACT.Exp, scale=-1.0))
            nc.scalar.activation(lgt[:, 2, 0:8], lgt[:, 1, 0:8], ACT.Ln, bias=1.0).then_inc(S["prep_e"], 1)
            act.wait_ge(S["prep_lg"], 2 * l + 2)
            act.wait_ge(S["tmp_in"], 48 * (l + 1))
            lg = lgt[:, 3, 0:8]
            for d in range(2):
                dist = tmpt[:, (TMP_DPOS, TMP_DNEG)[d]:(TMP_DPOS, TMP_DNEG)[d] + P]
                for h in range(4):
                    last = nc.scalar.activation(decay[:, d, HPOS[h], :], dist, ACT.Exp, scale=lgt[:, 3, 4 * d + h:4 * d + h + 1])
                    last.then_inc(S["prep_act"], 1)
                i = TMP_IDX + 2 * d
                nc.scalar.activation(XI[:, d, :], lg[:, 4 * d:4 * d + 4], ACT.Exp, scale=tmpt[:, i:i + 1]).then_inc(S["prep_act"], 1)
                nc.scalar.activation(ZE[:, d, :], lg[:, 4 * d:4 * d + 4], ACT.Exp, scale=tmpt[:, i + 1:i + 2]).then_inc(S["prep_act"], 1)
            nc.scalar.activation(CDa[:, :], lg, ACT.Exp, scale=128.0).then_inc(S["prep_act"], 1)

        act.wait_ge(S["pool_init"], 3)
        act.wait_ge(S["par_ready"], 2)
        nc.scalar.activation(csil[:, :, :], parT[:, 32:48].rearrange("p (s k) -> p k s", s=2), ACT.Silu).then_inc(S["csil_ready"], 1)
        prep(0)
        for m in range(KT):
            stat_squares(0, m, COLS, S["x_ready"], m + 1)
        hi_static(0)
        hi_static(1)

        for l in range(DEPTH):
            u0, uf = l * UL, l * UL + UP + UO
            norm(2 * l, COLS)
            tiles = proj_tiles(l)
            for u in range(UP):
                last_of_group = (u % 4 == 3) if u < 16 else (u == 17)
                if last_of_group:
                    g = u // 4
                    for j, (gg, t, w) in enumerate(tiles):
                        if gg != g:
                            continue
                        sem, value = proj_signal(l, g, t)
                        act.wait_ge(S[sem], value)
                        dst, src = PG[g][:, t, 0:w], tokbank[t][:, 0:w]
                        if g == 0:
                            dst = dst.rearrange("p (j a d) -> p a j d", j=4, a=2)
                            src = src.rearrange("p (a j d) -> p a j d", a=2, j=4)
                        if g == 2:
                            nc.scalar.activation(dst[:, 0:256], src[:, 0:256], ACT.Copy, scale=HD ** -0.5).then_inc(S["p_ready"], 1)
                            nc.scalar.activation(dst[:, 256:512], src[:, 256:512], ACT.Copy).then_inc(S["p_ready"], 1)
                        else:
                            nc.scalar.activation(dst, src, ACT.Silu if g == 3 else ACT.Copy).then_inc(S["p_ready"], 1)
                hi_static(u0 + u + 2)
                if u == 10:
                    act.wait_ge(S["qk_var"], l + 1)
                    nc.scalar.activation(srt[:, :, :], ssq[:, :, :], ACT.Sqrt).then_inc(S["qk_sqrt"], 1)
            for j, (kind, i) in enumerate(trs[l]):
                act.wait_ge(S["tr_ready"], TR_FIRST[l] + j + 1)
                src = pair[(TR_FIRST[l] + j) % 2]
                if kind == "q":
                    dst, src = qT[:, :, i * P:(i + 1) * P], src[:, 0:512].rearrange("p (a b) -> p a b", a=4)
                elif kind == "k":
                    dst, src = kT[:, :], src[:, 0:COLS]
                else:
                    dst, src = (rqT if kind == "rq" else rkT)[:, i, 0:CW[l]], src[:, 0:CW[l]]
                nc.scalar.activation(dst, src, ACT.Copy).then_inc(S["tr_evac"], 1)
            act.wait_ge(S["mod_used"], DFT_FIRST[l] + NL)
            nc.scalar.activation(Zs[:, 0, :, :].rearrange("p a b -> p (a b)"), psA[:, :], ACT.Copy).then_inc(S["za_evac"], 1)
            if l == 0:
                act.wait_ge(S["mod_used"], DFT_FIRST[0] + NL + 1)
                nc.scalar.activation(Zc[:, :, :, :].rearrange("p a b c -> p (a b c)"), psS[:, :], ACT.Copy).then_inc(S["zc_evac"], 1)
            act.wait_ge(S["y_ready"], 2 * l + 1)
            nc.scalar.activation(Ahi[:, 6:8, 0:LAT], psA[:, :].rearrange("p (a b) -> p a b", a=2), ACT.Copy).then_inc(S["y_hi"], 1)
            if l == 0:
                act.wait_ge(S["y_ready"], 2)
                nc.scalar.activation(Ahi[:, 6:8, LAT:COLS], psB[:, 0:512].rearrange("p (a b) -> p a b", a=2), ACT.Copy).then_inc(S["y_hi"], 1)
            for j in range(TT[l]):
                r = l * NT + j
                act.wait_ge(S["g_cent"], r + 1)
                nc.scalar.activation(rs[:, 4, :], rs[:, 3, :], ACT.Square).then_inc(S["g_sq"], 1)
                act.wait_ge(S["g_var"], r + 1)
                nc.scalar.activation(gst[:, 2, :], gst[:, 1, :], ACT.Sqrt).then_inc(S["g_sqrt"], 1)
                act.wait_ge(S["rT_ready"], r + 1)
                nc.scalar.activation(Ahi[:, 4:6, j * P:(j + 1) * P], ps7[:, 0:256].rearrange("p (a b) -> p a b", a=2), ACT.Copy).then_inc(S["rT_hi"], 1)
            n_items = 8 * TT[l]
            for s in range(n_items + 7):
                if s < n_items:
                    it = ITEM_FIRST[l] + s
                    _, b, h, k = ITEMS[it]
                    ks, _, _ = band(b)
                    w = (len(ks) + 2) * P
                    q = b % 2
                    act.wait_ge(S["s_max"], it + 1)
                    if it >= 2:
                        act.wait_ge(S["pt_ready"], it - 1)
                    nc.scalar.activation(Pb[:, it % 2, 0:w], pair[it % 2][:, 0:w], ACT.Exp, bias=nm[:, q, h:h + 1],
                                         scale=HD ** -0.5, accum_out=den[:, q, h:h + 1]).then_inc(S["s_exp"], 1)
                    if k == 7:
                        act.wait_ge(S["es_in"], l * NT + b + 1)
                        nc.scalar.activation(es[:, :], esi[:, :], ACT.Exp).then_inc(S["es_out"], 1)
                if s >= 14 and (s - 14) % 8 == 0 and (s - 14) // 8 < TT[l]:
                    b = (s - 14) // 8
                    act.wait_ge(S["aoT_ready"], l * NT + b + 1)
                    nc.scalar.activation(Ahi[:, 0:4, b * P:(b + 1) * P], ps7[:, :].rearrange("p (a b) -> p a b", a=4), ACT.Copy).then_inc(S["aoT_hi"], 1)
            for u in range(UO):
                hi_static(u0 + UP + u + 2)
                if u >= 1:
                    stat_squares(2 * l + 1, u - 1, CW[l], S["resid_done"], 72 * l + u)
            stat_squares(2 * l + 1, 7, CW[l], S["resid_done"], 72 * l + 8)
            norm(2 * l + 1, CW[l])

            def relu(f, hpar, p, k, before):
                act.wait_ge(S["lin_ready"], before + 1)
                nc.scalar.activation(Tb[:, k % 2, 0:CW[l]], pair[p][:, 0:CW[l]], ACT.Relu).then_inc(S["relu_done"], 1)
                act.wait_ge(S["h_full"], f + 1)
                nc.scalar.activation(Hhi[:, hpar, k, 0:CW[l]], Ab[:, k % 2, 0:CW[l]], ACT.Copy).then_inc(S["h_hi"], 1)

            lin0 = 104 * l + 8
            for k in range(4):
                hi_static(uf + k + 2)
                relu(32 * l + k, 0, k % 2, k, lin0 + k)
            if l == 0:
                prep(1)

            def half(c, par):
                for k in range(8):
                    hi((uf + k) % 2, (uf + 6 + k) // 2 + c * 4, "lin_ready",
                       lin0 + 4 + c * 12 + (k + 1 if k < 4 else 4 + 2 * (k - 3)))
                    if k < 4:
                        relu(32 * l + 4 + c * 4 + k, 1 - par, k % 2, k, lin0 + 4 + c * 12 + k)

            with act.Fori(0, 3) as cc:
                half(cc * 2, 0)
                half(cc * 2 + 1, 1)
            half(6, 0)
            for k in range(4):
                hi_static(uf + 62 + k)
                if l == 0:
                    for m in (2 * k, 2 * k + 1):
                        stat_squares(2, m, COLS, S["resid_done"], 64 + m + 1)
        for t in (0, 2):
            act.wait_ge(S["out_T"], t + 1)
            nc.scalar.activation(outs[:, t, :], pair[0][:, :], ACT.Copy).then_inc(S["out_a"], 1)

    @blk.vector
    def _(dve):
        V = nc.vector
        counts = {}

        def link(ins, sem="dve"):
            counts[sem] = counts.get(sem, 0) + 1
            ins.then_inc(S[sem], 1)
            dve.wait_ge(S[sem], counts[sem])

        def bc(ap, axis, shape):
            return ap.unsqueeze(axis).to_broadcast(shape)

        def mod_evac(l, t0, n, psum_first):
            link(V.tensor_tensor(modT[:, l, bass.ds(t0, n), :],
                                 ps6[:, 2 * psum_first:2 * (psum_first + n)].rearrange("p (t s) -> p t s", s=2),
                                 bc(bmodT[:, l, bass.ds(t0, n)], 2, [P, n, 2]), ALU.add), "mod_evac")

        def gain(l, k):
            g = parT[:, 16 * k + 8 * l:16 * k + 8 * l + 8]
            link(V.scalar_tensor_tensor(out=gs[:, l, k, :, :], in0=modT[:, l, 24 * k + 8:24 * k + 16, :], scalar=1.0,
                                        in1=bc(g, 2, [P, 8, 2]), op0=ALU.add, op1=ALU.mult))

        def norm(l, k, cols):
            n = 2 * l + k
            dve.wait_ge(S["rt_sqrt"], n + 1)
            link(V.reciprocal(Rt[:, 0:cols], Rt[:, 0:cols]))

            def low(j):
                dve.wait_ge(S["a_hi"], 8 * n + j + 1)
                V.tensor_tensor(Alo[:, j, 0:cols], Ab[:, j % 2, 0:cols], Ahi[:, j, 0:cols], ALU.subtract).then_inc(S["a_ready"], 1)

            for j in range(KT):
                link(V.tensor_tensor(Tb[:, j % 2, 0:cols], X[:, j, 0:cols], Rt[:, 0:cols], ALU.mult))
                if cols > LAT:
                    link(V.tensor_scalar(Ab[:, j % 2, LAT:cols], Tb[:, j % 2, LAT:cols], gs[:, l, k, j, 1:2],
                                         modT[:, l, 24 * k + j, 1:2], ALU.mult, ALU.add))
                V.tensor_scalar(Ab[:, j % 2, 0:LAT], Tb[:, j % 2, 0:LAT], gs[:, l, k, j, 0:1],
                                modT[:, l, 24 * k + j, 0:1], ALU.mult, ALU.add).then_inc(S["a_full"], 1)
                if j:
                    low(j - 1)
            low(KT - 1)

        def prep(l):
            for i in range(2):
                g = qkg[:, l, i, :]
                link(V.tensor_tensor(ropeg[:, :, 2 * i, :], rope[:, :, 0, :], bc(g, 1, [P, NL, HD]), ALU.mult))
                for f in range(2):
                    gsw = g.rearrange("p (r f i) -> p r f i", r=2, f=2)[:, :, 1 - f, :]
                    o = ropeg[:, :, 2 * i + 1, :].rearrange("p t (r f i) -> p t r f i", r=2, f=2)
                    s = rope[:, :, 1, :].rearrange("p t (r f i) -> p t r f i", r=2, f=2)
                    for r in range(2):
                        link(V.tensor_tensor(o[:, :, r, f, :], s[:, :, r, f, :], bc(gsw[:, r, :], 1, [P, NL, 16]), ALU.mult))
            x = dlog[:, l, :]
            link(V.tensor_scalar(lgt[:, 0, 8:16], x, -1.0, None, ALU.mult))
            link(V.tensor_tensor(lgt[:, 0, 0:8], x, lgt[:, 0, 8:16], ALU.max), "prep_lg")
            link(V.tensor_scalar(lgt[:, 3, 8:16], x, 0.0, None, ALU.min))
            dve.wait_ge(S["prep_e"], l + 1)
            link(V.tensor_tensor(lgt[:, 3, 0:8], lgt[:, 3, 8:16], lgt[:, 2, 0:8], ALU.subtract), "prep_lg")
            dve.wait_ge(S["prep_act"], 13 * (l + 1))
            for d in range(2):
                m = tmpt[:, (TMP_MPOS, TMP_MNEG)[d]:(TMP_MPOS, TMP_MNEG)[d] + P]
                link(V.tensor_tensor(decay[:, d, :, :], decay[:, d, :, :], bc(m, 1, [P, 4, P]), ALU.mult))
            for s in range(2):
                src = CDa[64 * s:64 * s + 64, :].rearrange("p (d q s) -> p d q s", d=2, s=2)
                link(V.tensor_copy(CD[64 * s:64 * s + 64, :, :], src[:, :, :, s]))
            dve.wait_ge(S["prep_w"], l + 1)
            for s in range(2):
                q = slice(64 * s, 64 * s + 64)
                link(V.tensor_copy(WCS[q, :, :, 64 * s:64 * s + 64],
                                   ps7[q, 0:256].rearrange("p (a b c) -> p a b c", a=2, b=2)), "prep_wd")

        dve.wait_ge(S["pool_init"], 3)
        dve.wait_ge(S["rows_T"], 2)
        link(V.tensor_copy(bmodT[:, :, :].rearrange("p a b -> p (a b)"), ps7[:, 0:96]), "par_ready")
        link(V.tensor_copy(parT[:, :], ps7[:, 96:144]), "par_ready")
        link(V.tensor_copy(identb[:, :], ident[:, :]), "mask_ready")
        link(V.tensor_copy(maskb[:, :, :], maskf[:, :, :]), "mask_ready")
        link(V.tensor_scalar(nsink[:, :, :], sinkb[:, :, :], -1.0, None, ALU.mult))
        prep(0)
        for m in range(KT):
            dve.wait_ge(S["xT_ready"], m + 1)
            V.tensor_copy(X[:, m, :], pair[m % 2][:, 0:COLS]).then_inc(S["x_ready"], 1)
        dve.wait_ge(S["mod_used"], 16)
        mod_evac(0, 0, 16, 0)
        gain(0, 0)

        def resid(l, chunk, m, p, value):
            dve.wait_ge(S["lin_ready"], value)
            w = CW[l]
            if w > LAT:
                V.scalar_tensor_tensor(out=X[:, m, LAT:w], in0=pair[p][:, LAT:w], scalar=modT[:, l, 8 * chunk + m, 1:2],
                                       in1=X[:, m, LAT:w], op0=ALU.mult, op1=ALU.add)
            V.scalar_tensor_tensor(out=X[:, m, 0:LAT], in0=pair[p][:, 0:LAT], scalar=modT[:, l, 8 * chunk + m, 0:1],
                                   in1=X[:, m, 0:LAT], op0=ALU.mult, op1=ALU.add).then_inc(S["resid_done"], 1)

        y_n = 0
        for l in range(DEPTH):
            norm(l, 0, COLS)
            for t in range(NT):
                if t < TT[l]:
                    dve.wait_ge(S["p_ready"], evac_index[l, 0, t])
                    link(V.tensor_tensor(scr[:, 0, :], Pq[:, t, :], Pq[:, t, :], ALU.mult))
                    link(V.reduce_sum(ssq[:, t, 0:8], scr[:, 0, :].rearrange("p (h d) -> p h d", h=8), axis=AX))
                else:
                    link(V.memset(ssq[:, t, 0:8], 1.0))
            for t in range(NT):
                dve.wait_ge(S["p_ready"], evac_index[l, 1, t])
                link(V.tensor_tensor(scr[:, 0, 0:P], Pk[:, t, 0:P], Pk[:, t, 0:P], ALU.mult))
                link(V.reduce_sum(ssq[:, t, 8:10], scr[:, 0, 0:P].rearrange("p (h d) -> p h d", h=2), axis=AX))
            link(V.tensor_scalar(ssq[:, :, :], ssq[:, :, :], 1.0 / HD, EPS, ALU.mult, ALU.add), "qk_var")
            dve.wait_ge(S["qk_sqrt"], l + 1)
            link(V.reciprocal(srt[:, :, :], srt[:, :, :]))

            def rotate(v, nh, C, Sn, r, out_sem):
                n, i = nh * HD, HD // (2 * r)
                v3 = v.rearrange("p (h d) -> p h d", h=nh)
                link(V.tensor_tensor(scr[:, 1, 0:n].rearrange("p (h d) -> p h d", h=nh), v3, bc(C, 1, [P, nh, HD]), ALU.mult))
                vs = v.rearrange("p (h r f i) -> p h r f i", h=nh, r=r, f=2)
                os = scr[:, 2, 0:n].rearrange("p (h r f i) -> p h r f i", h=nh, r=r, f=2)
                ss = Sn.rearrange("p (r f i) -> p r f i", r=r, f=2)
                for f in range(2):
                    for q in range(r):
                        link(V.tensor_tensor(os[:, :, q, f, :], vs[:, :, q, 1 - f, :], bc(ss[:, q, f, :], 1, [P, nh, i]), ALU.mult))
                link(V.tensor_tensor(v, scr[:, 1, 0:n], scr[:, 2, 0:n], ALU.add), out_sem)

            for t in range(NT):
                for v, nh, c0, i, sem in ((Pq[:, t, :], 8, 0, 0, "q_ready"), (Pk[:, t, 0:P], 2, 8, 1, "k_ready")):
                    if i == 0 and t >= TT[l]:
                        continue
                    v3 = v.rearrange("p (h d) -> p h d", h=nh)
                    link(V.tensor_tensor(v3, v3, bc(srt[:, t, c0:c0 + nh], 2, [P, nh, HD]), ALU.mult))
                    if t < NL:
                        rotate(v, nh, ropeg[:, t, 2 * i, :], ropeg[:, t, 2 * i + 1, :], 2, sem)
                    else:
                        link(V.tensor_tensor(v3, v3, bc(qkg[:, l, i, :], 1, [P, nh, HD]), ALU.mult), sem)
            for t in range(NL):
                rotate(Pk[:, t, 256:512], 4, rope[:, t, 2, :], rope[:, t, 3, :], 1, "rq_ready")
            for t in range(NL):
                dve.wait_ge(S["p_ready"], evac_index[l, 2, t])
                rotate(Pr[:, t, 0:256], 4, rope[:, t, 2, :], rope[:, t, 3, :], 1, "rk_ready")
            if l == 0:
                dve.wait_ge(S["mod_used"], NMOD)
                mod_evac(0, 16, 32, 16)
                gain(0, 1)
            dve.wait_ge(S["mod_used"], DFT_FIRST[l] + NL)
            V.tensor_copy(Zs[:, 1, :, :].rearrange("p a b -> p (a b)"), psB[:, :]).then_inc(S["zb_evac"], 1)
            dve.wait_ge(S["y_hi"], 2 * l + 1)
            V.tensor_tensor(Alo[:, 6:8, 0:LAT], psA[:, :].rearrange("p (a b) -> p a b", a=2), Ahi[:, 6:8, 0:LAT], ALU.subtract).then_inc(S["y_lo"], 1)
            if l == 0:
                dve.wait_ge(S["y_hi"], 2)
                V.tensor_tensor(Alo[:, 6:8, LAT:COLS], psB[:, 0:512].rearrange("p (a b) -> p a b", a=2), Ahi[:, 6:8, LAT:COLS], ALU.subtract).then_inc(S["y_lo"], 1)
            for d in range(2):
                link(V.memset(SD[:, d, 0, :, :], 0.0), "st_ready")
            for j in range(NT - 1):
                for d in range(2):
                    t = WALK[d][j]
                    e = (l * (NT - 1) + j) * 2 + d
                    if t >= NL:
                        dve.wait_ge(S["p_ready"], evac_index[l, 2, t])
                    k3 = Pr[:, t, 0:256].rearrange("p (h d) -> p h d", h=4)
                    if e >= 1:
                        dve.wait_ge(S["kv_ready"], e)
                    link(V.tensor_tensor(rs[:, 0, 0:256].rearrange("p (h d) -> p h d", h=4), k3, bc(ZE[:, d, :], 2, [P, 4, HD]), ALU.mult), "kz_ready")
                    dve.wait_ge(S["kv_ready"], e + 1)
                    link(V.tensor_tensor(rs[:, 1, 0:256].rearrange("p (a b) -> p a b", a=2), ps7[:, 0:256].rearrange("p (a b) -> p a b", a=2), bc(block[:, :], 1, [P, 2, P]), ALU.mult))
                    for q in range(2):
                        link(V.scalar_tensor_tensor(out=SD[:, d, j + 1, q, :], in0=SD[:, d, j, q, :], scalar=CD[:, d, q:q + 1],
                                                    in1=rs[:, 1, q * P:(q + 1) * P], op0=ALU.mult, op1=ALU.add), "st_ready")
            for t in range(TT[l]):
                r = l * NT + t
                dve.wait_ge(S["sc_ready"], r + 1)
                for d in range(2):
                    link(V.tensor_tensor(rs[:, 1 + d, :].rearrange("p (s n) -> p s n", s=2), psA[:, :].rearrange("p (s n) -> p s n", s=2)[:, :, 0:256],
                                         decay[:, d, :, :].rearrange("p (s q) n -> p s (q n)", s=2), ALU.mult), "md_ready")
                dve.wait_ge(S["ret_ready"], 2 * r + 1)
                link(V.tensor_tensor(rs[:, 3, :].rearrange("p (h d) -> p h d", h=8), psS[:, 0:512].rearrange("p (h d) -> p h d", h=8),
                                     bc(XI[:, :, :].rearrange("p a b -> p (a b)"), 2, [P, 8, HD]), ALU.mult))
                dve.wait_ge(S["ret_ready"], 2 * r + 2)
                link(V.tensor_tensor(rs[:, 3, :], rs[:, 3, :], psS[:, 512:1024], ALU.add), "ro_ready")
                o3 = rs[:, 3, :].rearrange("p (h d) -> p h d", h=8)
                link(V.reduce_sum(gst[:, 0, :], o3, axis=AX))
                link(V.tensor_scalar(gst[:, 0, :], gst[:, 0, :], -1.0 / HD, None, ALU.mult))
                link(V.tensor_tensor(o3, o3, bc(gst[:, 0, :], 2, [P, 8, HD]), ALU.add), "g_cent")
                dve.wait_ge(S["g_sq"], r + 1)
                link(V.reduce_sum(gst[:, 1, :], rs[:, 4, :].rearrange("p (h d) -> p h d", h=8), axis=AX))
                link(V.tensor_scalar(gst[:, 1, :], gst[:, 1, :], 1.0 / HD, EPS, ALU.mult, ALU.add), "g_var")
                link(V.tensor_tensor(Pg[:, t, :].rearrange("p (d n) -> p d n", d=2), Pg[:, t, :].rearrange("p (d n) -> p d n", d=2),
                                     bc(gng[:, l, :], 1, [P, 2, 256]), ALU.mult))
                link(V.tensor_tensor(rs[:, 3, :], rs[:, 3, :], Pg[:, t, :], ALU.mult))
                dve.wait_ge(S["g_sqrt"], r + 1)
                link(V.reciprocal(gst[:, 3, :], gst[:, 2, :]))
                link(V.tensor_tensor(o3, o3, bc(gst[:, 3, :], 2, [P, 8, HD]), ALU.mult))
                link(V.tensor_tensor(rs[:, 5, 0:256], rs[:, 3, 0:256], rs[:, 3, 256:512], ALU.add), "ro_ready")
                dve.wait_ge(S["rT_hi"], r + 1)
                V.tensor_tensor(Alo[:, 4:6, t * P:(t + 1) * P], ps7[:, 0:256].rearrange("p (a b) -> p a b", a=2),
                                Ahi[:, 4:6, t * P:(t + 1) * P], ALU.subtract).then_inc(S["rT_lo"], 1)
            n_items = 8 * TT[l]
            for s in range(n_items + 7):
                if s < n_items:
                    it = ITEM_FIRST[l] + s
                    _, b, h, k = ITEMS[it]
                    w = (len(band(b)[0]) + 2) * P
                    dve.wait_ge(S["s_ready"], it + 1)
                    link(V.reduce_max(mx[:, it % 2:it % 2 + 1], pair[it % 2][:, 0:w], axis=AX))
                    link(V.tensor_scalar(nm[:, b % 2, h:h + 1], mx[:, it % 2:it % 2 + 1], -HD ** -0.5, nsink[:, l, h:h + 1],
                                         ALU.mult, ALU.min), "s_max")
                    if k == 7:
                        if l * NT + b >= 1:
                            dve.wait_ge(S["es_out"], l * NT + b)
                        link(V.tensor_tensor(esi[:, :], nm[:, b % 2, :], sinkb[:, l, :], ALU.add), "es_in")
                if 2 <= s < n_items + 2:
                    it = ITEM_FIRST[l] + s - 2
                    w = (len(band(ITEMS[it][1])[0]) + 2) * P
                    dve.wait_ge(S["pt_ready"], it + 1)
                    if it >= 2:
                        dve.wait_ge(S["pv_ready"], it - 1)
                    V.tensor_copy(PTs[:, it % 2, 0:w], psS[:, 0:w]).then_inc(S["pt_evac"], 1)
                if s >= 11 and (s - 11) % 8 == 0 and (s - 11) // 8 < TT[l]:
                    b = (s - 11) // 8
                    dve.wait_ge(S["es_out"], l * NT + b + 1)
                    link(V.tensor_tensor(es[:, :], es[:, :], den[:, b % 2, :], ALU.add))
                    link(V.reciprocal(es[:, :], es[:, :]))
                    dve.wait_ge(S["pv_ready"], ITEM_FIRST[l] + 8 * b + 8)
                    V.tensor_tensor(AO[:, :].rearrange("p (h d) -> p h d", h=8), ps6[:, :].rearrange("p (h d) -> p h d", h=8),
                                    bc(es[:, :], 2, [P, 8, HD]), ALU.mult).then_inc(S["ao_ready"], 1)
                if s >= 14 and (s - 14) % 8 == 0 and (s - 14) // 8 < TT[l]:
                    b = (s - 14) // 8
                    dve.wait_ge(S["aoT_hi"], l * NT + b + 1)
                    V.tensor_tensor(Alo[:, 0:4, b * P:(b + 1) * P], ps7[:, :].rearrange("p (a b) -> p a b", a=4),
                                    Ahi[:, 0:4, b * P:(b + 1) * P], ALU.subtract).then_inc(S["aoT_lo"], 1)
            for m in range(KT):
                resid(l, 2, m, m % 2, 104 * l + m + 1)
            norm(l, 1, CW[l])
            w = CW[l]

            def hidden(f, hpar, k):
                dve.wait_ge(S["relu_done"], f + 1)
                V.tensor_tensor(Ab[:, k % 2, 0:w], Tb[:, k % 2, 0:w], Tb[:, k % 2, 0:w], ALU.mult).then_inc(S["h_full"], 1)
                dve.wait_ge(S["h_hi"], f + 1)
                V.tensor_tensor(Hlo[:, hpar, k, 0:w], Ab[:, k % 2, 0:w], Hhi[:, hpar, k, 0:w], ALU.subtract).then_inc(S["h_lo"], 1)

            lin0 = 104 * l + 8
            for k in range(4):
                hidden(32 * l + k, 0, k)
            if l == 0:
                dve.wait_ge(S["mod_used"], MOD_FIRST[1][0] + 6)
                mod_evac(1, 0, 6, 0)
                prep(1)

            def half(c, par):
                for k in range(4):
                    hidden(32 * l + 4 + c * 4 + k, 1 - par, k)
                if l == 0:
                    dve.wait_ge(S["mod_used"], c * 6 + MOD_FIRST[1][0] + 12)
                    V.tensor_tensor(modT[:, 1, bass.ds(c * 6 + 6, 6), :], ps6[:, 0:12].rearrange("p (t s) -> p t s", s=2),
                                    bc(bmodT[:, 1, bass.ds(c * 6 + 6, 6)], 2, [P, 6, 2]), ALU.add).then_inc(S["mod_evac"], 1)
                for m in range(KT):
                    resid(l, 5, m, m % 2, lin0 + 4 + c * 12 + 4 + m + 1)

            with dve.Fori(0, 3) as cc:
                half(cc * 2, 0)
                half(cc * 2 + 1, 1)
            half(6, 0)
            for m in range(KT):
                resid(l, 5, m, m % 2, lin0 + 88 + m + 1)
            if l == 0:
                counts["mod_evac"] = 10
                dve.wait_ge(S["mod_evac"], 10)
                gain(1, 0)
                gain(1, 1)
        for t in (1, 3):
            dve.wait_ge(S["out_T"], t + 1)
            V.tensor_copy(outs[:, t, :], pair[1][:, :]).then_inc(S["out_d"], 1)

    @blk.tensor
    def _(pe):
        mm = nc.tensor.matmul

        def tr(out, in_, n=P):
            return nc.tensor.transpose(out, in_, ident[0:n, 0:n])

        def mod_tile(w, slot, round_, col):
            pe.wait_ge(mod_in[slot], round_ * 16 + 16)
            for k in range(KT):
                last = mm(ps6[:, col:col + 2], modraw[:, slot, k * P:(k + 1) * P], csil[:, k, :], start=(k == 0), stop=(k == KT - 1))
            last.then_inc(S["mod_used"], 1)

        def stats(n, m, splits):
            pe.wait_ge(S["stat_sq"], 8 * n + m + 1)
            for c0, w in splits:
                last = mm(psS[:, c0:c0 + w], ones[:, :], sqb[:, m % 2, c0:c0 + w], start=(m == 0), stop=(m == KT - 1))
            last.then_inc(S["stat_used"], 1)

        def fourier_weights(l):
            pe.wait_ge(S["tmp_in"], 48 * (l + 1))
            for s in range(2):
                for q in range(2):
                    last = mm(ps7[:, (2 * s + q) * HD:(2 * s + q + 1) * HD], tmpt[:, TMP_C + s * P:TMP_C + (s + 1) * P], fw[:, q, :], start=True, stop=True)
            last.then_inc(S["prep_w"], 1)

        pe.wait_ge(S["consts_in"], 14 * 16)
        tr(ps7[:, 0:96], rows[0:96, 0, :], 96).then_inc(S["rows_T"], 1)
        tr(ps7[:, 96:144], rows[0:48, 1, :], 48).then_inc(S["rows_T"], 1)
        pe.wait_ge(S["par_ready"], 2)
        fourier_weights(0)
        pe.wait_ge(S["pool_init"], 3)
        pe.wait_ge(S["x_in"], 16 * NT)
        for m in range(KT):
            if m >= 2:
                pe.wait_ge(S["x_ready"], m - 1)
            for t in range(NT):
                last = tr(pair[m % 2][:, t * P:(t + 1) * P], Xin[:, t, m * P:(m + 1) * P])
            last.then_inc(S["xT_ready"], 1)
            if m >= 2:
                stats(0, m - 2, SPLITS[0])
        stats(0, KT - 2, SPLITS[0])
        stats(0, KT - 1, SPLITS[0])
        pe.wait_ge(S["csil_ready"], 1)
        for w in range(16):
            mod_tile(w, w % 2, w // 2, 2 * w)

        pj = 0
        for l in range(DEPTH):
            u0, uf = l * UL, l * UL + UP + UO
            tiles = proj_tiles(l)
            for u in range(UP):
                g = u // 4
                n = GROUPS[g][1]
                nk = 2 if n == 512 else 4
                part = u % 4
                parts = 4 if n == 512 else 2
                uu = u0 + u
                pe.wait_ge(S["lo_done"], uu + 1)
                here = [(t, w) for gg, t, w in tiles if gg == g]
                for t, w in here:
                    if part == 0 and g > 0:
                        prev = max(gg for gg, tt, _ in tiles if tt == t and gg < g) if any(tt == t and gg < g for gg, tt, _ in tiles) else None
                        if prev is not None:
                            pe.wait_ge(S["p_ready"], evac_index[l, prev, t])
                    for kk in range(nk):
                        k = part * nk + kk
                        if t == 0 and g == 0:
                            pe.wait_ge(S["a_ready"], 16 * l + k + 1)
                        if w < n:
                            cs = slice(kk * n, kk * n + w)
                        else:
                            cs = slice(kk * n, (kk + 1) * n)
                        ah, al = Ahi[:, k, t * P:(t + 1) * P], Alo[:, k, t * P:(t + 1) * P]
                        wh, wl = Whi[:, uu % 2, cs], Wlo[:, uu % 2, cs]
                        first, fin = part == 0 and kk == 0, part == parts - 1 and kk == nk - 1
                        out = tokbank[t][:, 0:w]
                        mm(out, ah, wh, start=first, stop=False)
                        mm(out, ah, wl, start=False, stop=False)
                        last = mm(out, al, wh, start=False, stop=fin)
                    if t == here[-1][0]:
                        last.then_inc(S["unit_done"], 1)
                    elif part == parts - 1:
                        last.then_inc(S["proj_ready"], 1)
                if l == 0 and u < 16:
                    for w in (16 + 2 * u, 17 + 2 * u):
                        if w == 16:
                            pe.wait_ge(S["mod_evac"], 1)
                        mod_tile(w, w % 2, w // 2, 2 * w)
            pe.wait_ge(S["p_ready"], max(v for (ll, _, _), v in evac_index.items() if ll == l))
            tb = [[0, 0, 0, 0], [NT, NT, NL, NL]][l]
            for j, (kind, i) in enumerate(trs[l]):
                if TR_FIRST[l] + j >= 2:
                    pe.wait_ge(S["tr_evac"], TR_FIRST[l] + j - 1)
                dst = pair[(TR_FIRST[l] + j) % 2]
                if kind == "q":
                    pe.wait_ge(S["q_ready"], tb[0] + i + 1)
                    for q in range(4):
                        last = tr(dst[:, q * P:(q + 1) * P], Pq[:, i, q * P:(q + 1) * P])
                elif kind == "k":
                    pe.wait_ge(S["k_ready"], tb[1] + NT)
                    for t in range(NT):
                        last = tr(dst[:, t * P:(t + 1) * P], Pk[:, t, 0:P])
                else:
                    pe.wait_ge(S["rq_ready"], tb[2] + NL)
                    pe.wait_ge(S["rk_ready"], tb[3] + NL)
                    for t in range(TT[l]):
                        src = Pk[:, t, 256 + i * P:256 + (i + 1) * P] if kind == "rq" else Pr[:, t, i * P:(i + 1) * P]
                        last = tr(dst[:, t * P:(t + 1) * P], src)
                last.then_inc(S["tr_ready"], 1)
            pe.wait_ge(S["tr_evac"], TR_FIRST[l] + len(trs[l]))
            for k in range(NL):
                w = DFT_FIRST[l] + k
                pe.wait_ge(mod_in[w % 2], 16 * (w // 2 + 1))
                for s in range(2):
                    for c in range(2):
                        last = mm(pair[s][:, c * 512:(c + 1) * 512], Pu[:, k, c * P:(c + 1) * P], modraw[:, w % 2, s * 512:(s + 1) * 512],
                                  start=(k == 0), stop=(k == NL - 1))
                last.then_inc(S["mod_used"], 1)
            if l == 0:
                w = DFT_FIRST[0] + NL
                pe.wait_ge(mod_in[w % 2], 16 * (w // 2 + 1))
                tab = modraw[:, w % 2, :].rearrange("p (s k n) -> p s k n", s=2, k=2)
                for s in range(2):
                    for c in range(2):
                        for k in range(2):
                            last = mm(psS[:, s * 512 + c * 256:s * 512 + (c + 1) * 256], Pu[:, NL + k, c * P:(c + 1) * P], tab[:, s, k, :],
                                      start=(k == 0), stop=(k == 1))
                last.then_inc(S["mod_used"], 1)
            pe.wait_ge(S["za_evac"], l + 1)
            pe.wait_ge(S["zb_evac"], l + 1)
            pe.wait_ge(S["prep_wd"], 2 * l + 2)
            for c in range(2):
                for s in range(2):
                    last = mm(psA[:, c * 512:(c + 1) * 512], WCS[:, s, c, :], Zs[:, s, c, :], start=(s == 0), stop=(s == 1))
            last.then_inc(S["y_ready"], 1)
            if l == 0:
                pe.wait_ge(S["zc_evac"], 1)
                for c in range(2):
                    for s in range(2):
                        last = mm(psB[:, c * 256:(c + 1) * 256], WCS[:, s, c, :], Zc[:, s, c, :], start=(s == 0), stop=(s == 1))
                last.then_inc(S["y_ready"], 1)
            for j in range(NT - 1):
                for d in range(2):
                    t = WALK[d][j]
                    e = (l * (NT - 1) + j) * 2 + d
                    pe.wait_ge(S["kz_ready"], e + 1)
                    for q in range(2):
                        last = mm(ps7[:, q * P:(q + 1) * P], rs[:, 0, q * P:(q + 1) * P], Pr[:, t, 256 + q * P:256 + (q + 1) * P], start=True, stop=True)
                    last.then_inc(S["kv_ready"], 1)
            pe.wait_ge(S["st_ready"], (l + 1) * (2 + 4 * (NT - 1)))
            for t in range(TT[l]):
                r = l * NT + t
                if r >= 1:
                    pe.wait_ge(S["md_ready"], 2 * r)
                tc = slice(t * P, (t + 1) * P)
                for h in range(4):
                    q = slice(64 * (h % 2), 64 * (h % 2) + 64)
                    c0 = 512 * (h % 2) + P * (h // 2)
                    last = mm(psA[:, c0:c0 + P], rkT[q, h // 2, tc], rqT[q, h // 2, tc], start=True, stop=True)
                last.then_inc(S["sc_ready"], 1)
                if r >= 1:
                    pe.wait_ge(S["ro_ready"], 2 * r)
                for d in range(2):
                    for q in range(2):
                        last = mm(psS[:, d * 256 + q * P:d * 256 + (q + 1) * P], rqT[:, q, tc], SD[:, d, WALK[d].index(t), q, :], start=True, stop=True)
                last.then_inc(S["ret_ready"], 1)
                for d in range(2):
                    pe.wait_ge(S["md_ready"], 2 * r + d + 1)
                    for h in range(4):
                        c0 = 512 + d * 256 + h * HD
                        last = mm(psS[:, c0:c0 + HD], rs[:, 1 + d, HPOS[h] * P:(HPOS[h] + 1) * P], Pr[:, t, 256 + h * HD:256 + (h + 1) * HD], start=True, stop=True)
                last.then_inc(S["ret_ready"], 1)
                pe.wait_ge(S["ro_ready"], 2 * r + 2)
                for q in range(2):
                    last = tr(ps7[:, q * P:(q + 1) * P], rs[:, 5, q * P:(q + 1) * P])
                last.then_inc(S["rT_ready"], 1)
            pe.wait_ge(S["rT_lo"], l * NT + TT[l])
            pe.wait_ge(S["y_lo"], 2 * l + (2 if l == 0 else 1))
            n_items = 8 * TT[l]
            for s in range(n_items + 7):
                if s < n_items:
                    it = ITEM_FIRST[l] + s
                    _, b, h, k = ITEMS[it]
                    ks, mprev, mnext = band(b)
                    nb = len(ks)
                    q = slice(64 * (h // 4), 64 * (h // 4) + 64)
                    qv = qT[q, h % 4, b * P:(b + 1) * P]
                    dst = pair[it % 2]
                    if s >= 2:
                        pe.wait_ge(S["s_exp"], it - 1)
                    if nb:
                        mm(dst[:, 0:nb * P], qv, kT[q, ks[0] * P:(ks[-1] + 1) * P], start=True, stop=(mprev is None and mnext is None))
                        for i, mt in ((0, mprev), (1, mnext)):
                            if mt is not None:
                                mm(dst[:, mt * P:(mt + 1) * P], identb[:, :], maskb[:, i, :], start=False, stop=(i == 1 or mnext is None))
                    for i in range(2):
                        c0 = (nb + i) * P
                        last = mm(dst[:, c0:c0 + P], qv, kT[q, LAT + i * P:LAT + (i + 1) * P], start=True, stop=True)
                    last.then_inc(S["s_ready"], 1)
                if 2 <= s < n_items + 2:
                    it = ITEM_FIRST[l] + s - 2
                    nk = len(band(ITEMS[it][1])[0]) + 2
                    pe.wait_ge(S["s_exp"], it + 1)
                    if s >= 3:
                        pe.wait_ge(S["pt_evac"], it)
                    for i in range(nk):
                        last = tr(psS[:, i * P:(i + 1) * P], Pb[:, it % 2, i * P:(i + 1) * P])
                    last.then_inc(S["pt_ready"], 1)
                if 3 <= s < n_items + 3:
                    it = ITEM_FIRST[l] + s - 3
                    _, b, h, k = ITEMS[it]
                    keys = band(b)[0] + [NL, NL + 1]
                    pe.wait_ge(S["pt_evac"], it + 1)
                    if k == 0 and b > 0:
                        pe.wait_ge(S["ao_ready"], l * NT + b)
                    for i, kt in enumerate(keys):
                        last = mm(ps6[:, h * HD:(h + 1) * HD], PTs[:, it % 2, i * P:(i + 1) * P], Pk[:, kt, P + (h // 4) * HD:P + (h // 4 + 1) * HD],
                                  start=(i == 0), stop=(i == len(keys) - 1))
                    last.then_inc(S["pv_ready"], 1)
                if s >= 13 and (s - 13) % 8 == 0 and (s - 13) // 8 < TT[l]:
                    b = (s - 13) // 8
                    pe.wait_ge(S["ao_ready"], l * NT + b + 1)
                    if b >= 1:
                        pe.wait_ge(S["aoT_lo"], l * NT + b)
                    for q in range(4):
                        last = tr(ps7[:, q * P:(q + 1) * P], AO[:, q * P:(q + 1) * P])
                    last.then_inc(S["aoT_ready"], 1)
            pe.wait_ge(S["aoT_lo"], l * NT + TT[l])

            def tile(dst, slot, offs, hi_, lo_, w, waits=None):
                for i, off in enumerate(offs):
                    if waits is not None:
                        waits(i)
                    wh, wl = Whi[:, slot, off:off + P], Wlo[:, slot, off:off + P]
                    first, fin = i == 0, i == len(offs) - 1
                    for wt, x, f, e in ((wh, hi_, first, False), (wh, lo_, False, False), (wl, hi_, False, fin)):
                        for c0, cn in SPLITS[l]:
                            last = mm(dst[:, c0:c0 + cn], wt, x[:, i, c0:c0 + cn], start=f, stop=e)
                return last

            k8 = [k * P for k in range(KT)]
            for u in range(UO):
                uu = u0 + UP + u
                pe.wait_ge(S["lo_done"], uu + 1)
                if u >= 2:
                    pe.wait_ge(S["resid_done"], 72 * l + u - 1)
                tile(pair[u % 2], uu % 2, k8, Ahi, Alo, CW[l]).then_inc(S["lin_ready"], 1)
                if u >= 2:
                    stats(2 * l + 1, u - 2, SPLITS[l])
            stats(2 * l + 1, 6, SPLITS[l])
            stats(2 * l + 1, 7, SPLITS[l])

            def a_wait(n):
                return lambda k: pe.wait_ge(S["a_ready"], 8 * n + k + 1)

            for k in range(4):
                uu = uf + k
                if l == 0:
                    mod_tile(None, (MOD_FIRST[1][0] + k) % 2, (MOD_FIRST[1][0] + k) // 2, 2 * k)
                pe.wait_ge(S["lo_done"], uu + 1)
                if k >= 2:
                    pe.wait_ge(S["relu_done"], 32 * l + k - 1)
                tile(pair[k % 2], uu % 2, k8, Ahi, Alo, CW[l], a_wait(2 * l + 1) if k == 0 else None).then_inc(S["lin_ready"], 1)
            if l == 0:
                for k in (4, 5):
                    mod_tile(None, (MOD_FIRST[1][0] + k) % 2, (MOD_FIRST[1][0] + k) // 2, 2 * k)
                fourier_weights(1)

            def ff2(c, par, k, uu, slot):
                pe.wait_ge(S["lo_done"], uu + 1)
                for o in range(2):
                    m = 2 * k + o
                    g = c * 8 + m
                    if m < 2:
                        pe.wait_ge(S["relu_done"], 32 * l + c * 4 + 7 + m)
                    else:
                        pe.wait_ge(S["resid_done"], 72 * l + 8 + g - 1)
                    if m == 0:
                        pe.wait_ge(S["h_lo"], 32 * l + c * 4 + 4)
                    offs = [i * 256 + o * P for i in range(CHUNK)]
                    last = tile(pair[m % 2], slot, offs, Hhi[:, par], Hlo[:, par], CW[l])
                    last.then_inc(S["lin_ready"], 1)

            def half(c, par):
                for k in range(8):
                    if l == 0 and k < 6:
                        if k == 0:
                            pe.wait_ge(S["mod_evac"], c + 3)
                        j = MOD_FIRST[1][0] + 6 + k
                        mod_tile(None, j % 2, c * 3 + j // 2, 2 * k)
                    uu = uf + 4 + c * 8 + k
                    slot = (uf + k) % 2
                    if k < 4:
                        f = 32 * l + 4 + c * 4 + k
                        pe.wait_ge(S["lo_done"], uu + 1)
                        pe.wait_ge(S["relu_done"], f - 1)
                        if k < 2:
                            pe.wait_ge(S["resid_done"], 72 * l + 7 + c * 8 + k)
                        tile(pair[k % 2], slot, k8, Ahi, Alo, CW[l]).then_inc(S["lin_ready"], 1)
                    else:
                        ff2(c, par, k - 4, uu, slot)

            with pe.Fori(0, 3) as cc:
                half(cc * 2, 0)
                half(cc * 2 + 1, 1)
            half(6, 0)
            for k in range(4):
                uu = uf + 60 + k
                pe.wait_ge(S["lo_done"], uu + 1)
                for o in range(2):
                    m = 2 * k + o
                    pe.wait_ge(S["resid_done"], 72 * l + 8 + 56 + m - 1)
                    if m == 0:
                        pe.wait_ge(S["h_lo"], 32 * l + 32)
                    offs = [i * 256 + o * P for i in range(CHUNK)]
                    tile(pair[m % 2], uu % 2, offs, Hhi[:, 1], Hlo[:, 1], CW[l]).then_inc(S["lin_ready"], 1)
                    if l == 0 and m >= 2:
                        stats(2, m - 2, SPLITS[0])
            if l == 0:
                stats(2, 6, SPLITS[0])
                stats(2, 7, SPLITS[0])
        pe.wait_ge(S["resid_done"], 144)
        for t in range(NL):
            if t >= 2:
                pe.wait_ge(S["out_a"] if t % 2 == 0 else S["out_d"], t // 2)
            for m in range(KT):
                last = tr(pair[t % 2][:, m * P:(m + 1) * P], X[:, m, t * P:(t + 1) * P])
            last.then_inc(S["out_T"], 1)

    stack.close()


def tables():
    import numpy as np
    f = np.float32
    i = np.arange(P)
    tab = np.zeros((P, TABLE), f)
    tab[:, T_ID:T_ID + P] = np.eye(P)
    q, k = i[:, None], i[None, :]
    tab[:, T_MPREV:T_MPREV + P] = np.where(k >= q, 0.0, -1e30)
    tab[:, T_MNEXT:T_MNEXT + P] = np.where(k <= q, 0.0, -1e30)
    tab[:, T_BLOCK:T_BLOCK + P] = (i[:, None] // HD == i[None, :] // HD)
    tok = np.arange(LAT)

    def cs(pos, half):
        fr = (f(10000.0) ** (-np.arange(half, dtype=f) / f(half))).astype(f)
        ang = (pos.astype(f)[:, None] * fr[None, :]).astype(f).astype(np.float64)
        return np.cos(ang), np.sin(ang)

    rc, rsn = cs(tok // 64, 16)
    cc, csn = cs(tok % 64, 16)
    tc, tsn = cs(tok, 32)
    rope = np.stack([np.concatenate([rc, rc, cc, cc], 1), np.concatenate([-rsn, rsn, -csn, csn], 1),
                     np.concatenate([tc, tc], 1), np.concatenate([-tsn, tsn], 1)], 1)
    tab[:, T_ROPE:T_TMP] = rope.reshape(NL, P, 4 * HD).transpose(1, 0, 2).reshape(P, -1)
    t0 = tab[:, T_TMP:]
    kq = i[None, :] - i[:, None]
    t0[:, TMP_DPOS:TMP_DPOS + P] = np.maximum(kq, 0)
    t0[:, TMP_DNEG:TMP_DNEG + P] = np.maximum(-kq, 0)
    t0[:, TMP_MPOS:TMP_MPOS + P] = kq >= 0
    t0[:, TMP_MNEG:TMP_MNEG + P] = kq <= 0
    j = np.arange(HD)
    ang = 2 * np.pi * (np.outer(j, j) % HD) / HD
    for s, m in enumerate((np.cos(ang), -np.sin(ang))):
        for b in range(2):
            t0[b * HD:(b + 1) * HD, TMP_C + s * P + b * HD:TMP_C + s * P + (b + 1) * HD] = m
    t0[:, TMP_IDX:TMP_IDX + 4] = np.stack([i + 1, P - 1 - i, P - i, i], 1)

    def dft(n):
        w = 2 * np.pi * (np.outer(np.arange(n), np.arange(n)) % n) / n
        return (np.stack([np.cos(w), np.sin(w)]) / np.sqrt(n * HD)).astype(f)

    lat = dft(LAT).reshape(2, NL, P, LAT).transpose(1, 2, 0, 3).reshape(NL, P, 2 * LAT)
    ctx = dft(CTX).reshape(2, 2, P, CTX).transpose(2, 0, 1, 3).reshape(P, 4 * CTX)
    return {"table": tab, "dft_lat": np.ascontiguousarray(lat), "dft_ctx": np.ascontiguousarray(ctx)}


_INS = ["x", "c", "ctx", "c_ctx", "w_mod", "b_mod", "norm1_g", "norm2_g", "w_in", "w_out", "q_norm_g", "k_norm_g",
        "attn_sink", "ret_decay_logit", "ret_gn_g", "fourier_w", "w_ff1", "w_ff2"]


def kernel(**inputs):
    import numpy as _np
    import concourse.bacc as _bacc
    from concourse import mybir as _mybir
    from concourse.bass_utils import run_bass_kernel_spmd as _run

    nc = _bacc.Bacc("TRN2", target_bir_lowering=False, num_devices=1)
    arrays, args = {}, {}
    consts = tables()
    for name in _INS + list(consts):
        v = _np.ascontiguousarray(consts[name] if name in consts else inputs[name])
        arrays[f"in_{name}_dram"] = v
        args[name] = nc.dram_tensor(f"in_{name}_dram", v.shape, _mybir.dt.from_np(v.dtype), kind="ExternalInput").ap()
    args["out"] = nc.dram_tensor("out_0_dram", (1, LAT, D), _mybir.dt.float32, kind="ExternalOutput").ap()
    build(nc, args)
    r = _run(nc, [arrays], core_ids=[0])
    return r.results[0]["out_0_dram"]
```

```python
import concourse.bass as bass
from concourse import mybir
from contextlib import ExitStack

P = 128
D, DEPTH, LAT, CTX = 1024, 2, 512, 256
KT = D // P
NT, NL = (LAT + CTX) // P, LAT // P
COLS = LAT + CTX
HD = 64
PROJ = 2304
GROUPS = [(0, 512), (512, 512), (1024, 512), (1536, 512), (2048, 256)]
DFF = 4096
CHUNK = 4
NCHUNK = DFF // P // CHUNK
UE = 1024
UP, UO, UF = 18, 8, 64
UL = UP + UO + UF
NMOD = 48
MCH = 512
NST = 5
EPS = 1e-6
T_ID, T_MPREV, T_MNEXT, T_BLOCK, T_ROPE = 0, 128, 256, 384, 512
T_TMP = T_ROPE + NL * 256
TMP_DPOS, TMP_DNEG, TMP_MPOS, TMP_MNEG, TMP_C, TMP_S, TMP_IDX = 0, 128, 256, 384, 512, 640, 768
TMP_W = 772
TABLE = T_TMP + TMP_W


def proj_tiles(layer):
    out = []
    for g, (_, n) in enumerate(GROUPS):
        for t in range(NT):
            if layer == DEPTH - 1 and t >= NL and g in (0, 3, 4):
                continue
            out.append((g, t, 256 if (layer == DEPTH - 1 and t >= NL and g == 1) else n))
    return out


def build(nc, a):
    fp32, f32r, bf16 = mybir.dt.float32, mybir.dt.float32r, mybir.dt.bfloat16
    ALU, ACT, AX = mybir.AluOpType, mybir.ActivationFunctionType, mybir.AxisListType.X
    stack = ExitStack()

    def sb(name, shape, dt=fp32):
        return stack.enter_context(nc.sbuf_tensor(name, shape, dt))

    def overlay(*plans):
        got = []
        for n, plan in enumerate(plans):
            inner = ExitStack()
            target = stack if n == len(plans) - 1 else inner
            got.append([target.enter_context(nc.sbuf_tensor(*p)) for p in plan])
            inner.close()
        return got

    X = sb("X", [P, KT, COLS])
    (rs,), (Ahi, Alo) = overlay(
        [("ret_scratch", [P, 6, 512], fp32)],
        [("Ahi", [P, KT, COLS], f32r), ("Alo", [P, KT, COLS], f32r)])
    (Xin, rows, maskf, modst), (Zs, Zc), (SD,), (Pb, PTs, AO, _, qs, kh, kl), (Hhi, Hlo, tmpt), (Pq, Pk, Pr, Pg, Pu) = overlay(
        [("Xin", [P, NT, D], fp32), ("rows", [P, 2, P], fp32), ("maskf", [P, 2, P], fp32),
         ("modst", [P, NST, UE], fp32)],
        [("Zs", [P, 2, 2, LAT], fp32), ("Zc", [P, 2, 2, CTX], fp32)],
        [("SD", [P, 2, NT, 2, P], fp32)],
        [("Pb", [P, 2, 640], fp32), ("PTs", [P, 2, 640], fp32), ("AO", [P, 512], fp32), ("skip_Pk", [P, NT, 512], fp32),
         ("qs", [P, 2, 2, 4, P], f32r), ("kh", [P, 2, COLS], f32r), ("kl", [P, 2, COLS], f32r)],
        [("Hhi", [P, 2, CHUNK, COLS], f32r), ("Hlo", [P, 2, CHUNK, COLS], f32r), ("tmpt", [P, 1536], fp32)],
        [("Pq", [P, NT, 512], fp32), ("Pk", [P, NT, 512], fp32), ("Pr", [P, NT, 512], fp32),
         ("Pg", [P, NT, 512], fp32), ("Pu", [P, NT, 256], fp32)])
    PG = [Pq, Pk, Pr, Pg, Pu]
    (Rt, Tb, Ab, sqb, macc), (outs,), (_, _, scr), (qT, kT, rqT, rkT) = overlay(
        [("Rt", [P, COLS], fp32), ("Tb", [P, 2, COLS], fp32), ("Ab", [P, 2, COLS], fp32), ("sqb", [P, 2, COLS], fp32),
         ("macc", [P, 2, 512], fp32)],
        [("outs", [P, NL, D], fp32)],
        [("skip_q", [P, 4, COLS], fp32), ("skip_k", [P, COLS], fp32), ("scr", [P, 3, 512], fp32)],
        [("qT", [P, 4, COLS], fp32), ("kT", [P, COLS], fp32), ("rqT", [P, 2, COLS], fp32), ("rkT", [P, 2, COLS], fp32)])
    raw = sb("raw", [P, 2, UE])
    modraw = sb("modraw", [P, 2, UE])
    Whi = sb("Whi", [P, 2, UE], f32r)
    Wlo = sb("Wlo", [P, 2, UE], f32r)
    ident = sb("ident", [P, P])
    ones = sb("ones", [P, P])
    identb = sb("identb", [P, P], bf16)
    maskb = sb("maskb", [P, 2, P], bf16)
    block = sb("blockmask", [P, P])
    rope = sb("rope", [P, NL, 4, HD])
    ropeg = sb("ropeg", [P, NL, 4, HD])
    decay = sb("decay", [P, 2, 4, P])
    WCS = sb("WCS", [P, 2, 2, P])
    bmodT = sb("bmodT", [P, DEPTH, NMOD])
    parT = sb("parT", [P, 48])
    csil = sb("csil", [P, KT, 2])
    modT = sb("modT", [P, DEPTH, NMOD, 2])
    gs = sb("gs", [P, DEPTH, 2, KT, 2])
    qkg = sb("qkg", [P, DEPTH, 2, HD])
    gng = sb("gng", [P, DEPTH, 256])
    sinkb = sb("sinkb", [P, DEPTH, 8])
    nsink = sb("nsink", [P, DEPTH, 8])
    dlog = sb("dlog", [P, DEPTH, 8])
    lgt = sb("lgt", [P, 4, 16])
    XI = sb("XI", [P, 2, 4])
    ZE = sb("ZE", [P, 2, 4])
    CDa = sb("CDa", [P, 8])
    CD = sb("CD", [P, 2, 2])
    fw = tmpt[:, TMP_W:TMP_W + 2 * HD].rearrange("p (q d) -> p q d", q=2)
    ssq = sb("ssq", [P, NT, 10])
    srt = sb("srt", [P, NT, 10])
    mx = sb("mx", [P, 2])
    nm = sb("nm", [P, 2, 8])
    den = sb("den", [P, 2, 8])
    esi = sb("esi", [P, 8])
    es = sb("es", [P, 8])
    gst = sb("gst", [P, 4, 8])
    epst = sb("epst", [P, 1])

    def pb(name, n):
        return stack.enter_context(nc.psum_tensor(name, [P, n], fp32))

    psA, psB, psS = pb("psA", 1024), pb("psB", 1024), pb("psS", 1024)
    pair = [psA, psB]
    ps6, ps7 = pb("ps6", 512), pb("ps7", 512)
    tokbank = [psA[:, 0:512], psA[:, 512:1024], psB[:, 0:512], psB[:, 512:1024], psS[:, 0:512], psS[:, 512:1024]]

    names = """consts_in x_in tmp_in stored rows_T par_ready csil_ready mod_used mod_step modp_ready mod_red mod_evac xT_ready x_ready
        stat_sq stat_used rt_sqrt dve a_full a_hi a_ready hi_done lo_done unit_done proj_ready p_ready qk_var qk_sqrt
        q_ready k_ready rq_ready rk_ready tr_ready tr_evac za_evac zb_evac zc_evac y_ready y_hi y_lo
        kz_ready kv_ready st_ready sc_ready md_ready ret_ready g_cent g_sq g_var g_sqrt ro_ready rT_ready rT_hi rT_lo
        kq_hi kq_lo qb_hi qb_lo s_ready s_max s_exp pt_ready pt_evac pv_ready es_in es_out ao_ready aoT_ready aoT_hi aoT_lo
        lin_ready relu_done h_full h_hi h_lo resid_done prep_lg prep_e prep_act prep_w prep_wd out_T out_a out_d
        act pool_init mask_ready""".split()
    S = {n: stack.enter_context(nc.semaphore(n)) for n in names}
    raw_in = [stack.enter_context(nc.semaphore(f"raw_in{i}")) for i in range(2)]
    mod_in = [stack.enter_context(nc.semaphore(f"mod_in{i}")) for i in range(2)]
    modst_in = [stack.enter_context(nc.semaphore(f"modst_in{i}")) for i in range(NST)]

    evac_index, n = {}, 0
    for l in range(DEPTH):
        for g, t, _ in proj_tiles(l):
            n += 2 if g == 2 else 1
            evac_index[l, g, t] = n
    TT = [NT, NL]
    CW = [COLS, LAT]
    SPLITS = [[(0, 512), (512, 256)], [(0, 512)]]
    MOD1 = 53
    DFT_FIRST = [48, 101]
    HPOS = [0, 2, 1, 3]
    LT = UO + 32 + 64
    trs = []
    for l in range(DEPTH):
        trs.append([("q", t) for t in range(TT[l])] + [("k", 0)] + [(k, p) for k in ("rq", "rk") for p in range(2)])
    TR_FIRST = [0, len(trs[0])]
    WALK = [[4, 5, 0, 1, 2, 3], [5, 4, 3, 2, 1, 0]]
    ITEMS = []
    for l in range(DEPTH):
        for b in range(TT[l]):
            for k in range(8):
                ITEMS.append((l, b, k // 2 + 4 * (k % 2), k))
    ITEM_FIRST = [0, 8 * TT[0]]

    def band(b):
        if b >= NL:
            return [], None, None
        ks = list(range(max(0, b - 1), min(NL, b + 2)))
        return ks, (0 if b > 0 else None), (len(ks) - 1 if b < NL - 1 else None)

    def unit_through(u):
        l, j = u // UL, u % UL
        if j < UP:
            return "unit_done", UP * l + j + 1
        j -= UP
        if j < UO:
            return "lin_ready", LT * l + j + 1
        j -= UO
        if j < 4:
            return "lin_ready", LT * l + UO + j + 1
        c, k = (j - 4) // 8, (j - 4) % 8
        if c == NCHUNK - 1:
            k += 4
        return "lin_ready", LT * l + UO + 4 + 12 * c + (k + 1 if k < 4 else 4 * (c < NCHUNK - 1) + 2 * (k - 3))

    def proj_signal(l, g, t):
        here = [tt for gg, tt, _ in proj_tiles(l) if gg == g]
        if t == here[-1]:
            return "unit_done", UP * l + (4 * g + 4 if g < 4 else UP)
        n = sum(len(proj_tiles(x)) - len(GROUPS) for x in range(l))
        for gg in range(g):
            n += sum(1 for x, _, _ in proj_tiles(l) if x == gg) - 1
        return "proj_ready", n + here.index(t) + 1

    blk = stack.enter_context(nc.Block())

    @blk.sync
    def _(sp):
        def w_load(u, slot, dst, src, first):
            if not first:
                sp.wait_ge(S["lo_done"], u - 1)
            sp.dma_start(dst, src).then_inc(raw_in[slot], 16)

        def m_load(w, slot, dst, src):
            sp.wait_ge(S["mod_used"], w - 1)
            sp.dma_start(dst, src).then_inc(mod_in[slot], 16)

        r8 = lambda slot: raw[:, slot, :].rearrange("p (k n) -> p k n", k=8)
        r2 = lambda slot: raw[:, slot, :].rearrange("p (k n) -> p k n", k=2)
        r4 = lambda slot: raw[:, slot, :].rearrange("p (k n) -> p k n", k=4)
        m2 = lambda slot: modraw[:, slot, :].rearrange("p (k n) -> p k n", k=2)

        def mod_src(l, chunk, part):
            return a["w_mod"][l].rearrange("(k p) n -> p k n", p=P)[:, 2 * part:2 * part + 2, bass.ds(chunk * MCH, MCH)]

        def proj_src(l, u):
            g, part = u // 4, u % 4
            c0, n = GROUPS[g]
            k = 2 if n == 512 else 4
            v = a["w_in"][l].rearrange("(k p) n -> p k n", p=P)
            return v[:, part * k:(part + 1) * k, c0:c0 + n]

        def ff1_src(l, f):
            return a["w_ff1"][l].rearrange("(k p) n -> p k n", p=P)[:, :, bass.ds(f * P, P)]

        def ff2_src(l, c, o):
            return a["w_ff2"][l].rearrange("(k p) n -> p k n", p=P)[:, bass.ds(c * CHUNK, CHUNK), o * 256:(o + 1) * 256]

        def tmp_load(l):
            sp.dma_start(tmpt[:, 0:TMP_W], a["table"][:, T_TMP:TABLE]).then_inc(S["tmp_in"], 16)
            for pp in range(2):
                sp.dma_start(fw[:, pp, :], a["fourier_w"][l, 2 * pp:2 * pp + 2].rearrange("g c d -> (g c) d"))\
                    .then_inc(S["tmp_in"], 16)

        con = S["consts_in"]
        sp.dma_start(ident[:, :], a["table"][:, T_ID:T_ID + P]).then_inc(con, 16)
        sp.dma_start(rows[0:96, 0, :], a["b_mod"].rearrange("l (t p) -> (l t) p", p=P)).then_inc(con, 16)
        for i, nme in enumerate(("norm1_g", "norm2_g")):
            sp.dma_start(rows[16 * i:16 * i + 16, 1, :], a[nme].rearrange("l (t p) -> (l t) p", p=P)).then_inc(con, 16)
        sp.dma_start(rows[32:40, 1, :], a["c"].rearrange("o (t p) -> (o t) p", p=P)).then_inc(con, 16)
        sp.dma_start(rows[40:48, 1, :], a["c_ctx"].rearrange("(t p) -> t p", p=P)).then_inc(con, 16)

        def first_mod(w):
            if w >= NST:
                sp.wait_ge(S["mod_used"], w - NST + 1)
            sp.dma_start(modst[:, w % NST, :].rearrange("p (k n) -> p k n", k=2), mod_src(0, w // 4, w % 4)).then_inc(modst_in[w % NST], 16)

        for w in range(NST):
            first_mod(w)
        sp.dma_start(maskf[:, :, :], a["table"][:, T_MPREV:T_MPREV + 2 * P].rearrange("p (a b) -> p a b", a=2)).then_inc(con, 16)
        sp.dma_start(block[:, :], a["table"][:, T_BLOCK:T_BLOCK + P]).then_inc(con, 16)
        sp.dma_start(rope[:, :, :, :].rearrange("p a b c -> p (a b c)"), a["table"][:, T_ROPE:T_TMP]).then_inc(con, 16)
        for i, nme in enumerate(("q_norm_g", "k_norm_g")):
            sp.dma_start(qkg[:, :, i, :], a[nme].partition_broadcast(P)).then_inc(con, 16)
        sp.dma_start(gng[:, :, :], a["ret_gn_g"].partition_broadcast(P)).then_inc(con, 16)
        sp.dma_start(sinkb[:, :, :], a["attn_sink"].partition_broadcast(P)).then_inc(con, 16)
        sp.dma_start(dlog[:, :, :], a["ret_decay_logit"].rearrange("l a h -> l (a h)").partition_broadcast(P)).then_inc(con, 16)
        tmp_load(0)
        for t in range(NT):
            src = a["x"][0, t * P:(t + 1) * P, :] if t < NL else a["ctx"][0, (t - NL) * P:(t - NL + 1) * P, :]
            sp.dma_start(Xin[:, t, :], src).then_inc(S["x_in"], 16)
        for w in range(NST, 16):
            first_mod(w)

        for l in range(DEPTH):
            u0 = l * UL
            for u in range(UP):
                dst = (r2 if u < 16 else r4)((u0 + u) % 2)
                w_load(u0 + u, (u0 + u) % 2, dst, proj_src(l, u), u0 + u < 2)
                if l == 0 and u >= 2:
                    for w in (12 + 2 * u, 13 + 2 * u):
                        m_load(w, w % 2, m2(w % 2), mod_src(0, w // 4, w % 4))
            wo = a["w_out"][l].rearrange("(k p) n -> p k n", p=P)
            for u in range(2):
                w_load(u0 + UP + u, (u0 + UP + u) % 2, r8((u0 + UP + u) % 2), wo[:, :, u * P:(u + 1) * P], False)
            for k in range(NL):
                w = DFT_FIRST[l] + k
                m_load(w, w % 2, modraw[:, w % 2, :], a["dft_lat"][k])
            if l == 0:
                w = DFT_FIRST[l] + NL
                m_load(w, w % 2, modraw[:, w % 2, :], a["dft_ctx"])
            for u in range(2, UO):
                w_load(u0 + UP + u, (u0 + UP + u) % 2, r8((u0 + UP + u) % 2), wo[:, :, u * P:(u + 1) * P], False)
            uf = u0 + UP + UO
            if l == 0:
                sp.wait_ge(S["lin_ready"], UO)
                tmp_load(1)

            def half(c, mod):
                for k in range(8):
                    u = uf + 4 + c * 8 + k
                    slot = (uf + k) % 2
                    if k < 4:
                        w_load(u, slot, r8(slot), ff1_src(l, (c + 1) * 4 + k), False)
                    else:
                        w_load(u, slot, r4(slot), ff2_src(l, c, k - 4), False)
                    if mod:
                        slot = (MOD1 + k) % 2
                        m_load(MOD1 + c * 8 + k, slot, m2(slot), mod_src(1, c * 2 + k // 4, k % 4))

            for k in range(4):
                w_load(uf + k, (uf + k) % 2, r8((uf + k) % 2), ff1_src(l, k), False)
            with sp.Fori(0, 6) as c:
                half(c, l == 0)
            half(6, False)
            for k in range(4):
                u = uf + 60 + k
                w_load(u, u % 2, r4(u % 2), ff2_src(l, NCHUNK - 1, k), False)
        for t in range(NL):
            sp.wait_ge(S["out_a"] if t % 2 == 0 else S["out_d"], t // 2 + 1)
            sp.dma_start(a["out"][0, t * P:(t + 1) * P, :], outs[:, t, :]).then_inc(S["stored"], 16)
        sp.wait_ge(S["stored"], 16 * NL)

    @blk.gpsimd
    def _(pool):
        nc.gpsimd.memset(WCS[:, :, :, :], 0.0).then_inc(S["pool_init"], 1)
        nc.gpsimd.memset(ones[:, :], 1.0 / D).then_inc(S["pool_init"], 1)
        nc.gpsimd.memset(epst[:, :], EPS).then_inc(S["pool_init"], 1)

        def low_parts(u0, u1):
            with pool.Fori(u0 // 2, u1 // 2) as i:
                for s in range(2):
                    pool.wait_ge(S["hi_done"], i * 2 + s + 1)
                    nc.gpsimd.tensor_tensor(Wlo[:, s, :], raw[:, s, :], Whi[:, s, :], ALU.subtract).then_inc(S["lo_done"], 1)

        low_parts(0, UP + 2)
        for l in range(DEPTH):
            low_parts(l * UL + UP + 2, min((l + 1) * UL + UP + 2, DEPTH * UL))

    @blk.scalar
    def _(act):
        def hi(slot, round_, sem, value):
            act.wait_ge(raw_in[slot], round_ * 16 + 16)
            if sem is not None:
                act.wait_ge(S[sem], value)
            nc.scalar.activation(Whi[:, slot, :], raw[:, slot, :], ACT.Copy).then_inc(S["hi_done"], 1)

        def hi_static(u):
            if u < DEPTH * UL:
                sem, value = unit_through(u - 2) if u >= 2 else (None, 0)
                hi(u % 2, u // 2, sem, value)

        act_count = [0]

        def link(ins):
            ins.then_inc(S["act"], 1)
            act_count[0] += 1
            act.wait_ge(S["act"], act_count[0])

        def stat_squares(n, m, cols, ready, value):
            s = 8 * n + m
            act.wait_ge(ready, value)
            if s >= 2:
                act.wait_ge(S["stat_used"], s - 1)
            nc.scalar.activation(sqb[:, m % 2, 0:cols], X[:, m, 0:cols], ACT.Square).then_inc(S["stat_sq"], 1)

        def norm(n, cols):
            act.wait_ge(S["stat_used"], 8 * n + 8)
            nc.scalar.activation(Rt[:, 0:cols], psS[:, 0:cols], ACT.Sqrt, bias=epst[:, 0:1]).then_inc(S["rt_sqrt"], 1)
            for k in range(KT):
                act.wait_ge(S["a_full"], 8 * n + k + 1)
                nc.scalar.activation(Ahi[:, k, 0:cols], Ab[:, k % 2, 0:cols], ACT.Copy).then_inc(S["a_hi"], 1)

        def prep(l):
            act.wait_ge(S["prep_lg"], 2 * l + 1)
            link(nc.scalar.activation(lgt[:, 1, 0:8], lgt[:, 0, 0:8], ACT.Exp, scale=-1.0))
            nc.scalar.activation(lgt[:, 2, 0:8], lgt[:, 1, 0:8], ACT.Ln, bias=1.0).then_inc(S["prep_e"], 1)
            act.wait_ge(S["prep_lg"], 2 * l + 2)
            act.wait_ge(S["tmp_in"], 48 * (l + 1))
            lg = lgt[:, 3, 0:8]
            for d in range(2):
                dist = tmpt[:, (TMP_DPOS, TMP_DNEG)[d]:(TMP_DPOS, TMP_DNEG)[d] + P]
                for h in range(4):
                    last = nc.scalar.activation(decay[:, d, HPOS[h], :], dist, ACT.Exp, scale=lgt[:, 3, 4 * d + h:4 * d + h + 1])
                    last.then_inc(S["prep_act"], 1)
                i = TMP_IDX + 2 * d
                nc.scalar.activation(XI[:, d, :], lg[:, 4 * d:4 * d + 4], ACT.Exp, scale=tmpt[:, i:i + 1]).then_inc(S["prep_act"], 1)
                nc.scalar.activation(ZE[:, d, :], lg[:, 4 * d:4 * d + 4], ACT.Exp, scale=tmpt[:, i + 1:i + 2]).then_inc(S["prep_act"], 1)
            nc.scalar.activation(CDa[:, :], lg, ACT.Exp, scale=128.0).then_inc(S["prep_act"], 1)

        act.wait_ge(S["pool_init"], 3)
        act.wait_ge(S["par_ready"], 2)
        nc.scalar.activation(csil[:, :, :], parT[:, 32:48].rearrange("p (s k) -> p k s", s=2), ACT.Silu).then_inc(S["csil_ready"], 1)
        for m in range(KT):
            act.wait_ge(S["xT_ready"], m + 1)
            nc.scalar.activation(X[:, m, :], pair[m % 2][:, 0:COLS], ACT.Copy).then_inc(S["x_ready"], 1)
            if m:
                stat_squares(0, m - 1, COLS, S["x_ready"], m)
        stat_squares(0, KT - 1, COLS, S["x_ready"], KT)
        hi_static(0)
        hi_static(1)

        for l in range(DEPTH):
            u0, uf = l * UL, l * UL + UP + UO
            norm(2 * l, COLS)
            prep(l)
            tiles = proj_tiles(l)
            for u in range(UP):
                last_of_group = (u % 4 == 3) if u < 16 else (u == 17)
                if last_of_group:
                    g = u // 4
                    if g == 4:
                        act.wait_ge(S["prep_wd"], 2 * l + 2)
                    for j, (gg, t, w) in enumerate(tiles):
                        if gg != g:
                            continue
                        sem, value = proj_signal(l, g, t)
                        act.wait_ge(S[sem], value)
                        dst, src = PG[g][:, t, 0:w], tokbank[t][:, 0:w]
                        if g == 0:
                            dst = dst.rearrange("p (j a d) -> p a j d", j=4, a=2)
                            src = src.rearrange("p (a j d) -> p a j d", a=2, j=4)
                        if g == 2:
                            nc.scalar.activation(dst[:, 0:256], src[:, 0:256], ACT.Copy, scale=HD ** -0.5).then_inc(S["p_ready"], 1)
                            nc.scalar.activation(dst[:, 256:512], src[:, 256:512], ACT.Copy).then_inc(S["p_ready"], 1)
                        else:
                            nc.scalar.activation(dst, src, ACT.Silu if g == 3 else ACT.Copy).then_inc(S["p_ready"], 1)
                hi_static(u0 + u + 2)
                if u == 9:
                    act.wait_ge(S["qk_var"], l + 1)
                    nc.scalar.activation(srt[:, :, :], ssq[:, :, :], ACT.Sqrt).then_inc(S["qk_sqrt"], 1)
            for j, (kind, i) in enumerate(trs[l]):
                act.wait_ge(S["tr_ready"], TR_FIRST[l] + j + 1)
                src = pair[(TR_FIRST[l] + j) % 2]
                if kind == "q":
                    dst, src = qT[:, :, i * P:(i + 1) * P], src[:, 0:512].rearrange("p (a b) -> p a b", a=4)
                elif kind == "k":
                    dst, src = kT[:, :], src[:, 0:COLS]
                else:
                    dst, src = (rqT if kind == "rq" else rkT)[:, i, 0:CW[l]], src[:, 0:CW[l]]
                nc.scalar.activation(dst, src, ACT.Copy).then_inc(S["tr_evac"], 1)
            act.wait_ge(S["mod_used"], DFT_FIRST[l] + NL)
            nc.scalar.activation(Zs[:, 0, :, :].rearrange("p a b -> p (a b)"), psA[:, :], ACT.Copy).then_inc(S["za_evac"], 1)
            if l == 0:
                act.wait_ge(S["mod_used"], DFT_FIRST[0] + NL + 1)
                nc.scalar.activation(Zc[:, :, :, :].rearrange("p a b c -> p (a b c)"), psS[:, :], ACT.Copy).then_inc(S["zc_evac"], 1)
            act.wait_ge(S["y_ready"], 2 * l + 1)
            nc.scalar.activation(Ahi[:, 6:8, 0:LAT], psA[:, :].rearrange("p (a b) -> p a b", a=2), ACT.Copy).then_inc(S["y_hi"], 1)
            if l == 0:
                act.wait_ge(S["y_ready"], 2)
                nc.scalar.activation(Ahi[:, 6:8, LAT:COLS], psB[:, 0:512].rearrange("p (a b) -> p a b", a=2), ACT.Copy).then_inc(S["y_hi"], 1)
            for j in range(TT[l]):
                r = l * NT + j
                act.wait_ge(S["g_cent"], r + 1)
                nc.scalar.activation(rs[:, 4, :], rs[:, 3, :], ACT.Square).then_inc(S["g_sq"], 1)
                act.wait_ge(S["g_var"], r + 1)
                nc.scalar.activation(gst[:, 2, :], gst[:, 1, :], ACT.Sqrt).then_inc(S["g_sqrt"], 1)
                act.wait_ge(S["rT_ready"], r + 1)
                nc.scalar.activation(Ahi[:, 4:6, j * P:(j + 1) * P], ps7[:, 0:256].rearrange("p (a b) -> p a b", a=2), ACT.Copy).then_inc(S["rT_hi"], 1)
            for g in range(2):
                for half_ in range(2):
                    nc.scalar.activation(kh[64 * half_:64 * half_ + 64, g, :], kT[64 * g:64 * g + 64, :], ACT.Copy).then_inc(S["kq_hi"], 1)

            def query_hi(b):
                if b >= 2:
                    act.wait_ge(S["s_ready"], ITEM_FIRST[l] + 8 * (b - 1))
                for g in range(2):
                    q = slice(64 * g, 64 * g + 64)
                    nc.scalar.activation(qs[q, b % 2, g, :, :], qT[q, :, b * P:(b + 1) * P], ACT.Copy).then_inc(S["qb_hi"], 1)

            query_hi(0)
            n_items = 8 * TT[l]
            for s in range(n_items + 5):
                if s < n_items:
                    it = ITEM_FIRST[l] + s
                    _, b, h, k = ITEMS[it]
                    if k == 2 and b + 1 < TT[l]:
                        query_hi(b + 1)
                    ks, _, _ = band(b)
                    w = (len(ks) + 2) * P
                    q = b % 2
                    act.wait_ge(S["s_max"], it + 1)
                    if it >= 2:
                        act.wait_ge(S["pt_ready"], it - 1)
                    nc.scalar.activation(Pb[:, it % 2, 0:w], pair[it % 2][:, 0:w], ACT.Exp, bias=nm[:, q, h:h + 1],
                                         scale=HD ** -0.5, accum_out=den[:, q, h:h + 1]).then_inc(S["s_exp"], 1)
                    if k == 7:
                        act.wait_ge(S["es_in"], l * NT + b + 1)
                        nc.scalar.activation(es[:, :], esi[:, :], ACT.Exp).then_inc(S["es_out"], 1)
                if 2 <= s < n_items + 2:
                    it = ITEM_FIRST[l] + s - 2
                    w = (len(band(ITEMS[it][1])[0]) + 2) * P
                    act.wait_ge(S["pt_ready"], it + 1)
                    if it >= 2:
                        act.wait_ge(S["pv_ready"], it - 1)
                    nc.scalar.activation(PTs[:, it % 2, 0:w], psS[:, 0:w], ACT.Copy).then_inc(S["pt_evac"], 1)
                if s >= 12 and (s - 12) % 8 == 0 and (s - 12) // 8 < TT[l]:
                    b = (s - 12) // 8
                    act.wait_ge(S["aoT_ready"], l * NT + b + 1)
                    nc.scalar.activation(Ahi[:, 0:4, b * P:(b + 1) * P], ps7[:, :].rearrange("p (a b) -> p a b", a=4), ACT.Copy).then_inc(S["aoT_hi"], 1)
            for u in range(UO):
                hi_static(u0 + UP + u + 2)
                if u >= 1:
                    stat_squares(2 * l + 1, u - 1, CW[l], S["resid_done"], 72 * l + u)
            stat_squares(2 * l + 1, 7, CW[l], S["resid_done"], 72 * l + 8)
            norm(2 * l + 1, CW[l])

            def relu(f, hpar, p, k, before):
                act.wait_ge(S["lin_ready"], before + 1)
                nc.scalar.activation(Tb[:, k % 2, 0:CW[l]], pair[p][:, 0:CW[l]], ACT.Relu).then_inc(S["relu_done"], 1)
                act.wait_ge(S["h_full"], f + 1)
                nc.scalar.activation(Hhi[:, hpar, k, 0:CW[l]], Ab[:, k % 2, 0:CW[l]], ACT.Copy).then_inc(S["h_hi"], 1)

            lin0 = 104 * l + 8
            for k in range(4):
                hi_static(uf + k + 2)
                relu(32 * l + k, 0, k % 2, k, lin0 + k)

            def half(c, par):
                for k in range(8):
                    hi((uf + k) % 2, (uf + 6 + k) // 2 + c * 4, "lin_ready",
                       lin0 + 4 + c * 12 + (k + 1 if k < 4 else 4 + 2 * (k - 3)))
                    if k < 4:
                        relu(32 * l + 4 + c * 4 + k, 1 - par, k % 2, k, lin0 + 4 + c * 12 + k)

            with act.Fori(0, 3) as cc:
                half(cc * 2, 0)
                half(cc * 2 + 1, 1)
            half(6, 0)
            for k in range(4):
                hi_static(uf + 62 + k)
                if l == 0:
                    for m in (2 * k, 2 * k + 1):
                        stat_squares(2, m, COLS, S["resid_done"], 64 + m + 1)
        for t in (0, 2):
            act.wait_ge(S["out_T"], t + 1)
            nc.scalar.activation(outs[:, t, :], pair[0][:, :], ACT.Copy).then_inc(S["out_a"], 1)

    @blk.vector
    def _(dve):
        V = nc.vector
        counts = {}

        def link(ins, sem="dve"):
            counts[sem] = counts.get(sem, 0) + 1
            ins.then_inc(S[sem], 1)
            dve.wait_ge(S[sem], counts[sem])

        def bc(ap, axis, shape):
            return ap.unsqueeze(axis).to_broadcast(shape)

        def mod_unit(w, wd, part, src, acc):
            step = 0
            for kk in range(2):
                for s in range(2):
                    new = part == 0 and kk == 0
                    if not new:
                        if kk == 0 and s == 1:
                            dve.wait_ge(S["mod_used"], w)
                        else:
                            dve.wait_ge(S["mod_step"], wd * 3 + (kk and s + 1))
                    col = csil[:, 2 * part + kk, s:s + 1]
                    if new:
                        ins = V.tensor_scalar(acc[:, s, :], src[:, kk * MCH:(kk + 1) * MCH], col, None, ALU.mult)
                    else:
                        ins = V.scalar_tensor_tensor(out=acc[:, s, :], in0=src[:, kk * MCH:(kk + 1) * MCH], scalar=col,
                                                     in1=acc[:, s, :], op0=ALU.mult, op1=ALU.add)
                    step += 1
                    ins.then_inc(S["mod_step"] if step < 4 else S["mod_used"], 1)

        def mod_reduce(l, chunk, g):
            dve.wait_ge(S["modp_ready"], g + 1)
            for s, ps in ((0, ps6), (1, ps7)):
                V.tensor_reduce(modT[:, l, bass.ds(chunk * 4, 4), s], ps[:, :].rearrange("p (t k) -> p t k", t=4),
                                axis=AX, op=ALU.add).then_inc(S["mod_red"], 1)
            dve.wait_ge(S["mod_red"], g * 2 + 2)
            V.tensor_tensor(modT[:, l, bass.ds(chunk * 4, 4), :], modT[:, l, bass.ds(chunk * 4, 4), :],
                            bc(bmodT[:, l, bass.ds(chunk * 4, 4)], 2, [P, 4, 2]), ALU.add).then_inc(S["mod_evac"], 1)

        def gain(l, k):
            g = parT[:, 16 * k + 8 * l:16 * k + 8 * l + 8]
            link(V.scalar_tensor_tensor(out=gs[:, l, k, :, :], in0=modT[:, l, 24 * k + 8:24 * k + 16, :], scalar=1.0,
                                        in1=bc(g, 2, [P, 8, 2]), op0=ALU.add, op1=ALU.mult))

        def norm(l, k, cols):
            n = 2 * l + k
            dve.wait_ge(S["rt_sqrt"], n + 1)
            link(V.reciprocal(Rt[:, 0:cols], Rt[:, 0:cols]))

            def low(j):
                dve.wait_ge(S["a_hi"], 8 * n + j + 1)
                V.tensor_tensor(Alo[:, j, 0:cols], Ab[:, j % 2, 0:cols], Ahi[:, j, 0:cols], ALU.subtract).then_inc(S["a_ready"], 1)

            for j in range(KT):
                link(V.tensor_tensor(Tb[:, j % 2, 0:cols], X[:, j, 0:cols], Rt[:, 0:cols], ALU.mult))
                if cols > LAT:
                    link(V.tensor_scalar(Ab[:, j % 2, LAT:cols], Tb[:, j % 2, LAT:cols], gs[:, l, k, j, 1:2],
                                         modT[:, l, 24 * k + j, 1:2], ALU.mult, ALU.add))
                V.tensor_scalar(Ab[:, j % 2, 0:LAT], Tb[:, j % 2, 0:LAT], gs[:, l, k, j, 0:1],
                                modT[:, l, 24 * k + j, 0:1], ALU.mult, ALU.add).then_inc(S["a_full"], 1)
                if j:
                    low(j - 1)
            low(KT - 1)

        def prep(l):
            for i in range(2):
                g = qkg[:, l, i, :]
                link(V.tensor_tensor(ropeg[:, :, 2 * i, :], rope[:, :, 0, :], bc(g, 1, [P, NL, HD]), ALU.mult))
                for f in range(2):
                    gsw = g.rearrange("p (r f i) -> p r f i", r=2, f=2)[:, :, 1 - f, :]
                    o = ropeg[:, :, 2 * i + 1, :].rearrange("p t (r f i) -> p t r f i", r=2, f=2)
                    s = rope[:, :, 1, :].rearrange("p t (r f i) -> p t r f i", r=2, f=2)
                    for r in range(2):
                        link(V.tensor_tensor(o[:, :, r, f, :], s[:, :, r, f, :], bc(gsw[:, r, :], 1, [P, NL, 16]), ALU.mult))
            x = dlog[:, l, :]
            link(V.tensor_scalar(lgt[:, 0, 8:16], x, -1.0, None, ALU.mult))
            link(V.tensor_tensor(lgt[:, 0, 0:8], x, lgt[:, 0, 8:16], ALU.max), "prep_lg")
            link(V.tensor_scalar(lgt[:, 3, 8:16], x, 0.0, None, ALU.min))
            dve.wait_ge(S["prep_e"], l + 1)
            link(V.tensor_tensor(lgt[:, 3, 0:8], lgt[:, 3, 8:16], lgt[:, 2, 0:8], ALU.subtract), "prep_lg")
            dve.wait_ge(S["prep_act"], 13 * (l + 1))
            for d in range(2):
                m = tmpt[:, (TMP_MPOS, TMP_MNEG)[d]:(TMP_MPOS, TMP_MNEG)[d] + P]
                link(V.tensor_tensor(decay[:, d, :, :], decay[:, d, :, :], bc(m, 1, [P, 4, P]), ALU.mult))
            for s in range(2):
                src = CDa[64 * s:64 * s + 64, :].rearrange("p (d q s) -> p d q s", d=2, s=2)
                link(V.tensor_copy(CD[64 * s:64 * s + 64, :, :], src[:, :, :, s]))
            dve.wait_ge(S["prep_w"], l + 1)
            for s in range(2):
                q = slice(64 * s, 64 * s + 64)
                link(V.tensor_copy(WCS[q, :, :, 64 * s:64 * s + 64],
                                   ps7[q, 0:256].rearrange("p (a b c) -> p a b c", a=2, b=2)), "prep_wd")

        dve.wait_ge(S["pool_init"], 3)
        dve.wait_ge(S["rows_T"], 2)
        link(V.tensor_copy(bmodT[:, :, :].rearrange("p a b -> p (a b)"), ps7[:, 0:96]), "par_ready")
        link(V.tensor_copy(parT[:, :], ps7[:, 96:144]), "par_ready")
        link(V.tensor_copy(identb[:, :], ident[:, :]), "mask_ready")
        link(V.tensor_copy(maskb[:, :, :], maskf[:, :, :]), "mask_ready")
        link(V.tensor_scalar(nsink[:, :, :], sinkb[:, :, :], -1.0, None, ALU.mult))
        dve.wait_ge(S["csil_ready"], 1)
        maccs = [macc[:, :, :], Tb[:, :, 0:MCH]]
        for w in range(16):
            if w % 4 == 0 and w >= 8:
                mod_reduce(0, w // 4 - 2, w // 4 - 2)
            dve.wait_ge(modst_in[w % NST], 16 * (w // NST + 1))
            mod_unit(w, w, w % 4, modst[:, w % NST, :], maccs[w // 4 % 2])
        mod_reduce(0, 2, 2)
        mod_reduce(0, 3, 3)
        dve.wait_ge(S["mod_evac"], 4)
        gain(0, 0)

        def resid(l, chunk, m, p, value):
            dve.wait_ge(S["lin_ready"], value)
            w = CW[l]
            if w > LAT:
                V.scalar_tensor_tensor(out=X[:, m, LAT:w], in0=pair[p][:, LAT:w], scalar=modT[:, l, 8 * chunk + m, 1:2],
                                       in1=X[:, m, LAT:w], op0=ALU.mult, op1=ALU.add)
            V.scalar_tensor_tensor(out=X[:, m, 0:LAT], in0=pair[p][:, 0:LAT], scalar=modT[:, l, 8 * chunk + m, 0:1],
                                   in1=X[:, m, 0:LAT], op0=ALU.mult, op1=ALU.add).then_inc(S["resid_done"], 1)

        y_n = 0
        for l in range(DEPTH):
            norm(l, 0, COLS)
            prep(l)
            def rotate(v, nh, C, Sn, r, out_sem):
                n, i = nh * HD, HD // (2 * r)
                v3 = v.rearrange("p (h d) -> p h d", h=nh)
                link(V.tensor_tensor(scr[:, 1, 0:n].rearrange("p (h d) -> p h d", h=nh), v3, bc(C, 1, [P, nh, HD]), ALU.mult))
                vs = v.rearrange("p (h r f i) -> p h r f i", h=nh, r=r, f=2)
                os = scr[:, 2, 0:n].rearrange("p (h r f i) -> p h r f i", h=nh, r=r, f=2)
                ss = Sn.rearrange("p (r f i) -> p r f i", r=r, f=2)
                for f in range(2):
                    for q in range(r):
                        link(V.tensor_tensor(os[:, :, q, f, :], vs[:, :, q, 1 - f, :], bc(ss[:, q, f, :], 1, [P, nh, i]), ALU.mult))
                link(V.tensor_tensor(v, scr[:, 1, 0:n], scr[:, 2, 0:n], ALU.add), out_sem)

            def q_squares(t):
                if t < TT[l]:
                    dve.wait_ge(S["p_ready"], evac_index[l, 0, t])
                    link(V.tensor_tensor(scr[:, 0, :], Pq[:, t, :], Pq[:, t, :], ALU.mult))
                    link(V.reduce_sum(ssq[:, t, 0:8], scr[:, 0, :].rearrange("p (h d) -> p h d", h=8), axis=AX))
                else:
                    link(V.memset(ssq[:, t, 0:8], 1.0))

            def k_squares():
                for t in range(NT):
                    dve.wait_ge(S["p_ready"], evac_index[l, 1, t])
                    link(V.tensor_tensor(scr[:, 0, 0:P], Pk[:, t, 0:P], Pk[:, t, 0:P], ALU.mult))
                    link(V.reduce_sum(ssq[:, t, 8:10], scr[:, 0, 0:P].rearrange("p (h d) -> p h d", h=2), axis=AX))
                link(V.tensor_scalar(ssq[:, :, :], ssq[:, :, :], 1.0 / HD, EPS, ALU.mult, ALU.add), "qk_var")

            def qk_roots():
                dve.wait_ge(S["qk_sqrt"], l + 1)
                link(V.reciprocal(srt[:, :, :], srt[:, :, :]))

            def qk(t):
                for v, nh, c0, i, sem in ((Pq[:, t, :], 8, 0, 0, "q_ready"), (Pk[:, t, 0:P], 2, 8, 1, "k_ready")):
                    if i == 0 and t >= TT[l]:
                        continue
                    v3 = v.rearrange("p (h d) -> p h d", h=nh)
                    link(V.tensor_tensor(v3, v3, bc(srt[:, t, c0:c0 + nh], 2, [P, nh, HD]), ALU.mult))
                    if t < NL:
                        rotate(v, nh, ropeg[:, t, 2 * i, :], ropeg[:, t, 2 * i + 1, :], 2, sem)
                    else:
                        link(V.tensor_tensor(v3, v3, bc(qkg[:, l, i, :], 1, [P, nh, HD]), ALU.mult), sem)

            def rq(t):
                rotate(Pk[:, t, 256:512], 4, rope[:, t, 2, :], rope[:, t, 3, :], 1, "rq_ready")

            def rk(t):
                dve.wait_ge(S["p_ready"], evac_index[l, 2, t])
                rotate(Pr[:, t, 0:256], 4, rope[:, t, 2, :], rope[:, t, 3, :], 1, "rk_ready")

            work = {6: [(q_squares, t) for t in (0, 1, 2)], 7: [(q_squares, t) for t in (3, 4, 5)], 9: [(k_squares,)],
                    11: [(qk_roots,), (qk, 0)], 12: [(qk, 1)], 13: [(qk, 2)], 14: [(qk, 3)], 15: [(qk, 4)],
                    16: [(qk, 5), (rq, 0)], 17: [(rq, 1), (rq, 2), (rq, 3)]}
            for u in range(2, UP):
                if l == 0:
                    if u % 2 == 0 and u >= 6:
                        mod_reduce(0, u // 2 + 1, u // 2 + 1)
                    for w in (12 + 2 * u, 13 + 2 * u):
                        dve.wait_ge(mod_in[w % 2], 16 * ((w - 16) // 2 + 1))
                        mod_unit(w, w, w % 4, modraw[:, w % 2, :], maccs[w // 4 % 2])
                for f, *args in work.get(u, []):
                    f(*args)
            if l == 0:
                mod_reduce(0, 10, 10)
                mod_reduce(0, 11, 11)
                dve.wait_ge(S["mod_evac"], 12)
                gain(0, 1)
            for t in range(NL):
                rk(t)
            dve.wait_ge(S["mod_used"], DFT_FIRST[l] + NL)
            V.tensor_copy(Zs[:, 1, :, :].rearrange("p a b -> p (a b)"), psB[:, :]).then_inc(S["zb_evac"], 1)
            dve.wait_ge(S["y_hi"], 2 * l + 1)
            V.tensor_tensor(Alo[:, 6:8, 0:LAT], psA[:, :].rearrange("p (a b) -> p a b", a=2), Ahi[:, 6:8, 0:LAT], ALU.subtract).then_inc(S["y_lo"], 1)
            if l == 0:
                dve.wait_ge(S["y_hi"], 2)
                V.tensor_tensor(Alo[:, 6:8, LAT:COLS], psB[:, 0:512].rearrange("p (a b) -> p a b", a=2), Ahi[:, 6:8, LAT:COLS], ALU.subtract).then_inc(S["y_lo"], 1)
            for d in range(2):
                link(V.memset(SD[:, d, 0, :, :], 0.0), "st_ready")
            for j in range(NT - 1):
                for d in range(2):
                    t = WALK[d][j]
                    e = (l * (NT - 1) + j) * 2 + d
                    if t >= NL:
                        dve.wait_ge(S["p_ready"], evac_index[l, 2, t])
                    k3 = Pr[:, t, 0:256].rearrange("p (h d) -> p h d", h=4)
                    if e >= 1:
                        dve.wait_ge(S["kv_ready"], e)
                    link(V.tensor_tensor(rs[:, 0, 0:256].rearrange("p (h d) -> p h d", h=4), k3, bc(ZE[:, d, :], 2, [P, 4, HD]), ALU.mult), "kz_ready")
                    dve.wait_ge(S["kv_ready"], e + 1)
                    link(V.tensor_tensor(rs[:, 1, 0:256].rearrange("p (a b) -> p a b", a=2), ps7[:, 0:256].rearrange("p (a b) -> p a b", a=2), bc(block[:, :], 1, [P, 2, P]), ALU.mult))
                    for q in range(2):
                        link(V.scalar_tensor_tensor(out=SD[:, d, j + 1, q, :], in0=SD[:, d, j, q, :], scalar=CD[:, d, q:q + 1],
                                                    in1=rs[:, 1, q * P:(q + 1) * P], op0=ALU.mult, op1=ALU.add), "st_ready")
            for t in range(TT[l]):
                r = l * NT + t
                dve.wait_ge(S["sc_ready"], r + 1)
                for d in range(2):
                    link(V.tensor_tensor(rs[:, 1 + d, :].rearrange("p (s n) -> p s n", s=2), psA[:, :].rearrange("p (s n) -> p s n", s=2)[:, :, 0:256],
                                         decay[:, d, :, :].rearrange("p (s q) n -> p s (q n)", s=2), ALU.mult), "md_ready")
                dve.wait_ge(S["ret_ready"], 2 * r + 1)
                link(V.tensor_tensor(rs[:, 3, :].rearrange("p (h d) -> p h d", h=8), psS[:, 0:512].rearrange("p (h d) -> p h d", h=8),
                                     bc(XI[:, :, :].rearrange("p a b -> p (a b)"), 2, [P, 8, HD]), ALU.mult))
                dve.wait_ge(S["ret_ready"], 2 * r + 2)
                link(V.tensor_tensor(rs[:, 3, :], rs[:, 3, :], psS[:, 512:1024], ALU.add), "ro_ready")
                o3 = rs[:, 3, :].rearrange("p (h d) -> p h d", h=8)
                link(V.reduce_sum(gst[:, 0, :], o3, axis=AX))
                link(V.tensor_scalar(gst[:, 0, :], gst[:, 0, :], -1.0 / HD, None, ALU.mult))
                link(V.tensor_tensor(o3, o3, bc(gst[:, 0, :], 2, [P, 8, HD]), ALU.add), "g_cent")
                dve.wait_ge(S["g_sq"], r + 1)
                link(V.reduce_sum(gst[:, 1, :], rs[:, 4, :].rearrange("p (h d) -> p h d", h=8), axis=AX))
                link(V.tensor_scalar(gst[:, 1, :], gst[:, 1, :], 1.0 / HD, EPS, ALU.mult, ALU.add), "g_var")
                link(V.tensor_tensor(Pg[:, t, :].rearrange("p (d n) -> p d n", d=2), Pg[:, t, :].rearrange("p (d n) -> p d n", d=2),
                                     bc(gng[:, l, :], 1, [P, 2, 256]), ALU.mult))
                link(V.tensor_tensor(rs[:, 3, :], rs[:, 3, :], Pg[:, t, :], ALU.mult))
                dve.wait_ge(S["g_sqrt"], r + 1)
                link(V.reciprocal(gst[:, 3, :], gst[:, 2, :]))
                link(V.tensor_tensor(o3, o3, bc(gst[:, 3, :], 2, [P, 8, HD]), ALU.mult))
                link(V.tensor_tensor(rs[:, 5, 0:256], rs[:, 3, 0:256], rs[:, 3, 256:512], ALU.add), "ro_ready")
                dve.wait_ge(S["rT_hi"], r + 1)
                V.tensor_tensor(Alo[:, 4:6, t * P:(t + 1) * P], ps7[:, 0:256].rearrange("p (a b) -> p a b", a=2),
                                Ahi[:, 4:6, t * P:(t + 1) * P], ALU.subtract).then_inc(S["rT_lo"], 1)
            for g in range(2):
                dve.wait_ge(S["kq_hi"], 4 * l + 2 * g + 2)
                q = slice(64 * g, 64 * g + 64)
                for half_ in range(2):
                    V.tensor_tensor(kl[64 * half_:64 * half_ + 64, g, :], kT[q, :], kh[q, g, :], ALU.subtract).then_inc(S["kq_lo"], 1)

            def query_lo(b):
                for g in range(2):
                    dve.wait_ge(S["qb_hi"], 2 * (l * NT + b) + g + 1)
                    q, across = slice(64 * g, 64 * g + 64), slice(64 - 64 * g, 128 - 64 * g)
                    V.tensor_tensor(qs[across, b % 2, g, :, :], qT[q, :, b * P:(b + 1) * P], qs[q, b % 2, g, :, :], ALU.subtract).then_inc(S["qb_lo"], 1)

            query_lo(0)
            n_items = 8 * TT[l]
            for s in range(n_items + 5):
                if s >= 11 and (s - 11) % 8 == 0 and (s - 11) // 8 < TT[l]:
                    b = (s - 11) // 8
                    dve.wait_ge(S["es_out"], l * NT + b + 1)
                    link(V.tensor_tensor(es[:, :], es[:, :], den[:, b % 2, :], ALU.add))
                    link(V.reciprocal(es[:, :], es[:, :]))
                    dve.wait_ge(S["pv_ready"], ITEM_FIRST[l] + 8 * b + 8)
                    V.tensor_tensor(AO[:, :].rearrange("p (h d) -> p h d", h=8), ps6[:, :].rearrange("p (h d) -> p h d", h=8),
                                    bc(es[:, :], 2, [P, 8, HD]), ALU.mult).then_inc(S["ao_ready"], 1)
                if s < n_items:
                    it = ITEM_FIRST[l] + s
                    _, b, h, k = ITEMS[it]
                    w = (len(band(b)[0]) + 2) * P
                    dve.wait_ge(S["s_ready"], it + 1)
                    link(V.reduce_max(mx[:, it % 2:it % 2 + 1], pair[it % 2][:, 0:w], axis=AX))
                    link(V.tensor_scalar(nm[:, b % 2, h:h + 1], mx[:, it % 2:it % 2 + 1], -HD ** -0.5, nsink[:, l, h:h + 1],
                                         ALU.mult, ALU.min), "s_max")
                    if k == 7:
                        if l * NT + b >= 1:
                            dve.wait_ge(S["es_out"], l * NT + b)
                        link(V.tensor_tensor(esi[:, :], nm[:, b % 2, :], sinkb[:, l, :], ALU.add), "es_in")
                    if k == 2 and b + 1 < TT[l]:
                        query_lo(b + 1)
                if s >= 12 and (s - 12) % 8 == 0 and (s - 12) // 8 < TT[l]:
                    b = (s - 12) // 8
                    dve.wait_ge(S["aoT_hi"], l * NT + b + 1)
                    V.tensor_tensor(Alo[:, 0:4, b * P:(b + 1) * P], ps7[:, :].rearrange("p (a b) -> p a b", a=4),
                                    Ahi[:, 0:4, b * P:(b + 1) * P], ALU.subtract).then_inc(S["aoT_lo"], 1)
            for m in range(KT):
                resid(l, 2, m, m % 2, 104 * l + m + 1)
            norm(l, 1, CW[l])
            w = CW[l]

            def hidden(f, hpar, k):
                dve.wait_ge(S["relu_done"], f + 1)
                V.tensor_tensor(Ab[:, k % 2, 0:w], Tb[:, k % 2, 0:w], Tb[:, k % 2, 0:w], ALU.mult).then_inc(S["h_full"], 1)
                dve.wait_ge(S["h_hi"], f + 1)
                V.tensor_tensor(Hlo[:, hpar, k, 0:w], Ab[:, k % 2, 0:w], Hhi[:, hpar, k, 0:w], ALU.subtract).then_inc(S["h_lo"], 1)

            lin0 = 104 * l + 8
            for k in range(4):
                hidden(32 * l + k, 0, k)

            def half(c, par, mod):
                def m(*ks):
                    for k in ks:
                        if mod:
                            w = c * 8 + MOD1 + k
                            dve.wait_ge(mod_in[(MOD1 + k) % 2], c * 64 + 16 * ((MOD1 + k - 16) // 2 + 1))
                            mod_unit(w, c * 8 + NMOD + k, k % 4, modraw[:, (MOD1 + k) % 2, :], macc)

                def r(*ms):
                    for i in ms:
                        resid(l, 5, i, i % 2, lin0 + 4 + c * 12 + 4 + i + 1)

                for k in range(4):
                    m(k)
                    hidden(32 * l + 4 + c * 4 + k, 1 - par, k)
                r(0, 1)
                if mod:
                    mod_reduce(1, c * 2, c * 2 + 12)
                m(4)
                r(2, 3)
                m(5, 6)
                r(4, 5)
                m(7)
                r(6, 7)
                if mod:
                    mod_reduce(1, c * 2 + 1, c * 2 + 13)

            with dve.Fori(0, 3) as cc:
                half(cc * 2, 0, l == 0)
                half(cc * 2 + 1, 1, l == 0)
            half(6, 0, False)
            for m in range(KT):
                resid(l, 5, m, m % 2, lin0 + 88 + m + 1)
            if l == 0:
                dve.wait_ge(S["mod_evac"], 24)
                gain(1, 0)
                gain(1, 1)
        for t in (1, 3):
            dve.wait_ge(S["out_T"], t + 1)
            V.tensor_copy(outs[:, t, :], pair[1][:, :]).then_inc(S["out_d"], 1)

    @blk.tensor
    def _(pe):
        mm = nc.tensor.matmul

        def tr(out, in_, n=P):
            return nc.tensor.transpose(out, in_, ident[0:n, 0:n])

        def mod_sums(w, wd, acc):
            pe.wait_ge(S["mod_used"], w + 1)
            pe.wait_ge(S["mod_step"], wd * 3 + 3)
            for s, ps in ((0, ps6), (1, ps7)):
                for t in range(4):
                    last = tr(ps[:, t * P:(t + 1) * P], acc[:, s, t * P:(t + 1) * P])
            last.then_inc(S["modp_ready"], 1)

        def stats(n, m, splits):
            pe.wait_ge(S["stat_sq"], 8 * n + m + 1)
            for c0, w in splits:
                last = mm(psS[:, c0:c0 + w], ones[:, :], sqb[:, m % 2, c0:c0 + w], start=(m == 0), stop=(m == KT - 1))
            last.then_inc(S["stat_used"], 1)

        def fourier_weights(l):
            pe.wait_ge(S["tmp_in"], 48 * (l + 1))
            for s in range(2):
                for q in range(2):
                    last = mm(ps7[:, (2 * s + q) * HD:(2 * s + q + 1) * HD], tmpt[:, TMP_C + s * P:TMP_C + (s + 1) * P], fw[:, q, :], start=True, stop=True)
            last.then_inc(S["prep_w"], 1)

        pe.wait_ge(S["consts_in"], 14 * 16)
        tr(ps7[:, 0:96], rows[0:96, 0, :], 96).then_inc(S["rows_T"], 1)
        tr(ps7[:, 96:144], rows[0:48, 1, :], 48).then_inc(S["rows_T"], 1)
        pe.wait_ge(S["par_ready"], 2)
        maccs = [macc[:, :, :], Tb[:, :, 0:MCH]]
        mod_sums(3, 3, maccs[0])
        pe.wait_ge(S["x_in"], 16 * NT)
        for m in range(KT):
            if m >= 2:
                pe.wait_ge(S["x_ready"], m - 1)
            for t in range(NT):
                last = tr(pair[m % 2][:, t * P:(t + 1) * P], Xin[:, t, m * P:(m + 1) * P])
            last.then_inc(S["xT_ready"], 1)
            if m >= 2:
                stats(0, m - 2, SPLITS[0])
        stats(0, KT - 2, SPLITS[0])
        stats(0, KT - 1, SPLITS[0])
        for c in (1, 2, 3):
            pe.wait_ge(S["mod_evac"], c)
            mod_sums(4 * c + 3, 4 * c + 3, maccs[c % 2])
        pe.wait_ge(S["mod_evac"], 4)

        for l in range(DEPTH):
            u0, uf = l * UL, l * UL + UP + UO
            tiles = proj_tiles(l)
            fourier_weights(l)
            for u in range(UP):
                g = u // 4
                n = GROUPS[g][1]
                nk = 2 if n == 512 else 4
                part = u % 4
                parts = 4 if n == 512 else 2
                uu = u0 + u
                pe.wait_ge(S["lo_done"], uu + 1)
                here = [(t, w) for gg, t, w in tiles if gg == g]
                for t, w in here:
                    if part == 0 and g > 0:
                        prev = max(gg for gg, tt, _ in tiles if tt == t and gg < g) if any(tt == t and gg < g for gg, tt, _ in tiles) else None
                        if prev is not None:
                            pe.wait_ge(S["p_ready"], evac_index[l, prev, t])
                    for kk in range(nk):
                        k = part * nk + kk
                        if t == 0 and g == 0:
                            pe.wait_ge(S["a_ready"], 16 * l + k + 1)
                        if w < n:
                            cs = slice(kk * n, kk * n + w)
                        else:
                            cs = slice(kk * n, (kk + 1) * n)
                        ah, al = Ahi[:, k, t * P:(t + 1) * P], Alo[:, k, t * P:(t + 1) * P]
                        wh, wl = Whi[:, uu % 2, cs], Wlo[:, uu % 2, cs]
                        first, fin = part == 0 and kk == 0, part == parts - 1 and kk == nk - 1
                        out = tokbank[t][:, 0:w]
                        mm(out, ah, wh, start=first, stop=False)
                        mm(out, ah, wl, start=False, stop=False)
                        last = mm(out, al, wh, start=False, stop=fin)
                    if t == here[-1][0]:
                        last.then_inc(S["unit_done"], 1)
                    elif part == parts - 1:
                        last.then_inc(S["proj_ready"], 1)
                if l == 0 and u % 2 == 0 and u >= 4 or l == 0 and u == UP - 1:
                    c = u // 2 + 2 if u < UP - 1 else 11
                    if c == 4:
                        pe.wait_ge(S["prep_wd"], 2)
                    pe.wait_ge(S["mod_evac"], c)
                    mod_sums(4 * c + 3, 4 * c + 3, maccs[c % 2])
            pe.wait_ge(S["p_ready"], max(v for (ll, _, _), v in evac_index.items() if ll == l))
            tb = [[0, 0, 0, 0], [NT, NT, NL, NL]][l]
            for j, (kind, i) in enumerate(trs[l]):
                if TR_FIRST[l] + j >= 2:
                    pe.wait_ge(S["tr_evac"], TR_FIRST[l] + j - 1)
                dst = pair[(TR_FIRST[l] + j) % 2]
                if kind == "q":
                    pe.wait_ge(S["q_ready"], tb[0] + i + 1)
                    for q in range(4):
                        last = tr(dst[:, q * P:(q + 1) * P], Pq[:, i, q * P:(q + 1) * P])
                elif kind == "k":
                    pe.wait_ge(S["k_ready"], tb[1] + NT)
                    for t in range(NT):
                        last = tr(dst[:, t * P:(t + 1) * P], Pk[:, t, 0:P])
                else:
                    pe.wait_ge(S["rq_ready"], tb[2] + NL)
                    pe.wait_ge(S["rk_ready"], tb[3] + NL)
                    for t in range(TT[l]):
                        src = Pk[:, t, 256 + i * P:256 + (i + 1) * P] if kind == "rq" else Pr[:, t, i * P:(i + 1) * P]
                        last = tr(dst[:, t * P:(t + 1) * P], src)
                last.then_inc(S["tr_ready"], 1)
            pe.wait_ge(S["tr_evac"], TR_FIRST[l] + len(trs[l]))
            for k in range(NL):
                w = DFT_FIRST[l] + k
                pe.wait_ge(mod_in[w % 2], 16 * ((w - 16) // 2 + 1))
                for s in range(2):
                    for c in range(2):
                        last = mm(pair[s][:, c * 512:(c + 1) * 512], Pu[:, k, c * P:(c + 1) * P], modraw[:, w % 2, s * 512:(s + 1) * 512],
                                  start=(k == 0), stop=(k == NL - 1))
                last.then_inc(S["mod_used"], 1)
            if l == 0:
                w = DFT_FIRST[0] + NL
                pe.wait_ge(mod_in[w % 2], 16 * ((w - 16) // 2 + 1))
                tab = modraw[:, w % 2, :].rearrange("p (s k n) -> p s k n", s=2, k=2)
                for s in range(2):
                    for c in range(2):
                        for k in range(2):
                            last = mm(psS[:, s * 512 + c * 256:s * 512 + (c + 1) * 256], Pu[:, NL + k, c * P:(c + 1) * P], tab[:, s, k, :],
                                      start=(k == 0), stop=(k == 1))
                last.then_inc(S["mod_used"], 1)
            pe.wait_ge(S["za_evac"], l + 1)
            pe.wait_ge(S["zb_evac"], l + 1)
            pe.wait_ge(S["prep_wd"], 2 * l + 2)
            for c in range(2):
                for s in range(2):
                    last = mm(psA[:, c * 512:(c + 1) * 512], WCS[:, s, c, :], Zs[:, s, c, :], start=(s == 0), stop=(s == 1))
            last.then_inc(S["y_ready"], 1)
            if l == 0:
                pe.wait_ge(S["zc_evac"], 1)
                for c in range(2):
                    for s in range(2):
                        last = mm(psB[:, c * 256:(c + 1) * 256], WCS[:, s, c, :], Zc[:, s, c, :], start=(s == 0), stop=(s == 1))
                last.then_inc(S["y_ready"], 1)
            for j in range(NT - 1):
                for d in range(2):
                    t = WALK[d][j]
                    e = (l * (NT - 1) + j) * 2 + d
                    pe.wait_ge(S["kz_ready"], e + 1)
                    for q in range(2):
                        last = mm(ps7[:, q * P:(q + 1) * P], rs[:, 0, q * P:(q + 1) * P], Pr[:, t, 256 + q * P:256 + (q + 1) * P], start=True, stop=True)
                    last.then_inc(S["kv_ready"], 1)
            pe.wait_ge(S["st_ready"], (l + 1) * (2 + 4 * (NT - 1)))
            for t in range(TT[l]):
                r = l * NT + t
                if r >= 1:
                    pe.wait_ge(S["md_ready"], 2 * r)
                tc = slice(t * P, (t + 1) * P)
                for h in range(4):
                    q = slice(64 * (h % 2), 64 * (h % 2) + 64)
                    c0 = 512 * (h % 2) + P * (h // 2)
                    last = mm(psA[:, c0:c0 + P], rkT[q, h // 2, tc], rqT[q, h // 2, tc], start=True, stop=True)
                last.then_inc(S["sc_ready"], 1)
                if r >= 1:
                    pe.wait_ge(S["ro_ready"], 2 * r)
                for d in range(2):
                    for q in range(2):
                        last = mm(psS[:, d * 256 + q * P:d * 256 + (q + 1) * P], rqT[:, q, tc], SD[:, d, WALK[d].index(t), q, :], start=True, stop=True)
                last.then_inc(S["ret_ready"], 1)
                for d in range(2):
                    pe.wait_ge(S["md_ready"], 2 * r + d + 1)
                    for h in range(4):
                        c0 = 512 + d * 256 + h * HD
                        last = mm(psS[:, c0:c0 + HD], rs[:, 1 + d, HPOS[h] * P:(HPOS[h] + 1) * P], Pr[:, t, 256 + h * HD:256 + (h + 1) * HD], start=True, stop=True)
                last.then_inc(S["ret_ready"], 1)
                pe.wait_ge(S["ro_ready"], 2 * r + 2)
                for q in range(2):
                    last = tr(ps7[:, q * P:(q + 1) * P], rs[:, 5, q * P:(q + 1) * P])
                last.then_inc(S["rT_ready"], 1)
            pe.wait_ge(S["rT_lo"], l * NT + TT[l])
            pe.wait_ge(S["y_lo"], 2 * l + (2 if l == 0 else 1))
            pe.wait_ge(S["kq_lo"], 4 * l + 4)
            n_items = 8 * TT[l]
            for s in range(n_items + 5):
                if s < n_items:
                    it = ITEM_FIRST[l] + s
                    _, b, h, k = ITEMS[it]
                    ks, mprev, mnext = band(b)
                    nb = len(ks)
                    g = h // 4
                    q = qs[:, b % 2, g, h % 4, :]
                    if k == 0:
                        pe.wait_ge(S["qb_lo"], 2 * (l * NT + b) + 2)
                    dst = pair[it % 2]
                    if s >= 2:
                        pe.wait_ge(S["s_exp"], it - 1)
                    pieces = [(0, LAT, 2 * P)]
                    if nb:
                        pieces.append((2 * P, ks[0] * P, 2 * P))
                    if nb == 3:
                        pieces.append((4 * P, ks[2] * P, P))
                    for c0, k0, n in pieces:
                        mm(dst[:, c0:c0 + n], q, kh[:, g, k0:k0 + n], start=True, stop=False)
                        for i, mt in ((0, mprev), (1, mnext)):
                            if mt is not None and c0 <= (2 + mt) * P < c0 + n:
                                mm(dst[:, (2 + mt) * P:(3 + mt) * P], identb[:, :], maskb[:, i, :], start=False, stop=False)
                        last = mm(dst[:, c0:c0 + n], q, kl[:, g, k0:k0 + n], start=False, stop=True)
                    last.then_inc(S["s_ready"], 1)
                if 2 <= s < n_items + 2:
                    it = ITEM_FIRST[l] + s - 2
                    nk = len(band(ITEMS[it][1])[0]) + 2
                    pe.wait_ge(S["s_exp"], it + 1)
                    if s >= 3:
                        pe.wait_ge(S["pt_evac"], it)
                    for i in range(nk):
                        last = tr(psS[:, i * P:(i + 1) * P], Pb[:, it % 2, i * P:(i + 1) * P])
                    last.then_inc(S["pt_ready"], 1)
                if 3 <= s < n_items + 3:
                    it = ITEM_FIRST[l] + s - 3
                    _, b, h, k = ITEMS[it]
                    keys = [NL, NL + 1] + band(b)[0]
                    pe.wait_ge(S["pt_evac"], it + 1)
                    if k == 0 and b > 0:
                        pe.wait_ge(S["ao_ready"], l * NT + b)
                    for i, kt in enumerate(keys):
                        last = mm(ps6[:, h * HD:(h + 1) * HD], PTs[:, it % 2, i * P:(i + 1) * P],
                                  Pk[:, kt, P + (h // 4) * HD:P + (h // 4 + 1) * HD], start=(i == 0), stop=(i == len(keys) - 1))
                    last.then_inc(S["pv_ready"], 1)
                if s >= 12 and (s - 12) % 8 == 0 and (s - 12) // 8 < TT[l]:
                    b = (s - 12) // 8
                    pe.wait_ge(S["ao_ready"], l * NT + b + 1)
                    if b >= 1:
                        pe.wait_ge(S["aoT_lo"], l * NT + b)
                    for q in range(4):
                        last = tr(ps7[:, q * P:(q + 1) * P], AO[:, q * P:(q + 1) * P])
                    last.then_inc(S["aoT_ready"], 1)
            pe.wait_ge(S["aoT_lo"], l * NT + TT[l])

            def tile(dst, slot, offs, hi_, lo_, w, waits=None):
                for i, off in enumerate(offs):
                    if waits is not None:
                        waits(i)
                    wh, wl = Whi[:, slot, off:off + P], Wlo[:, slot, off:off + P]
                    first, fin = i == 0, i == len(offs) - 1
                    for wt, x, f, e in ((wh, hi_, first, False), (wh, lo_, False, False), (wl, hi_, False, fin)):
                        for c0, cn in SPLITS[l]:
                            last = mm(dst[:, c0:c0 + cn], wt, x[:, i, c0:c0 + cn], start=f, stop=e)
                return last

            k8 = [k * P for k in range(KT)]
            for u in range(UO):
                uu = u0 + UP + u
                pe.wait_ge(S["lo_done"], uu + 1)
                if u >= 2:
                    pe.wait_ge(S["resid_done"], 72 * l + u - 1)
                tile(pair[u % 2], uu % 2, k8, Ahi, Alo, CW[l]).then_inc(S["lin_ready"], 1)
                if u >= 2:
                    stats(2 * l + 1, u - 2, SPLITS[l])
            stats(2 * l + 1, 6, SPLITS[l])
            stats(2 * l + 1, 7, SPLITS[l])

            def a_wait(n):
                return lambda k: pe.wait_ge(S["a_ready"], 8 * n + k + 1)

            for k in range(4):
                uu = uf + k
                pe.wait_ge(S["lo_done"], uu + 1)
                if k >= 2:
                    pe.wait_ge(S["relu_done"], 32 * l + k - 1)
                tile(pair[k % 2], uu % 2, k8, Ahi, Alo, CW[l], a_wait(2 * l + 1) if k == 0 else None).then_inc(S["lin_ready"], 1)
            def ff2(c, par, k, uu, slot):
                pe.wait_ge(S["lo_done"], uu + 1)
                for o in range(2):
                    m = 2 * k + o
                    g = c * 8 + m
                    if m < 2:
                        pe.wait_ge(S["relu_done"], 32 * l + c * 4 + 7 + m)
                    else:
                        pe.wait_ge(S["resid_done"], 72 * l + 8 + g - 1)
                    if m == 0:
                        pe.wait_ge(S["h_lo"], 32 * l + c * 4 + 4)
                    offs = [i * 256 + o * P for i in range(CHUNK)]
                    last = tile(pair[m % 2], slot, offs, Hhi[:, par], Hlo[:, par], CW[l])
                    last.then_inc(S["lin_ready"], 1)

            def half(c, par, mod):
                for k in range(8):
                    uu = uf + 4 + c * 8 + k
                    slot = (uf + k) % 2
                    if k < 4:
                        f = 32 * l + 4 + c * 4 + k
                        pe.wait_ge(S["lo_done"], uu + 1)
                        pe.wait_ge(S["relu_done"], f - 1)
                        if k < 2:
                            pe.wait_ge(S["resid_done"], 72 * l + 7 + c * 8 + k)
                        tile(pair[k % 2], slot, k8, Ahi, Alo, CW[l]).then_inc(S["lin_ready"], 1)
                    else:
                        ff2(c, par, k - 4, uu, slot)
                    if mod and k in (4, 7):
                        pe.wait_ge(S["mod_evac"], c * 2 + 12 + (k == 7))
                        j = 3 if k == 4 else 7
                        mod_sums(c * 8 + MOD1 + j, c * 8 + NMOD + j, macc)

            with pe.Fori(0, 3) as cc:
                half(cc * 2, 0, l == 0)
                half(cc * 2 + 1, 1, l == 0)
            half(6, 0, False)
            for k in range(4):
                uu = uf + 60 + k
                pe.wait_ge(S["lo_done"], uu + 1)
                for o in range(2):
                    m = 2 * k + o
                    pe.wait_ge(S["resid_done"], 72 * l + 8 + 56 + m - 1)
                    if m == 0:
                        pe.wait_ge(S["h_lo"], 32 * l + 32)
                    offs = [i * 256 + o * P for i in range(CHUNK)]
                    tile(pair[m % 2], uu % 2, offs, Hhi[:, 1], Hlo[:, 1], CW[l]).then_inc(S["lin_ready"], 1)
                    if l == 0 and m >= 2:
                        stats(2, m - 2, SPLITS[0])
            if l == 0:
                stats(2, 6, SPLITS[0])
                stats(2, 7, SPLITS[0])
        pe.wait_ge(S["resid_done"], 144)
        for t in range(NL):
            if t >= 2:
                pe.wait_ge(S["out_a"] if t % 2 == 0 else S["out_d"], t // 2)
            for m in range(KT):
                last = tr(pair[t % 2][:, m * P:(m + 1) * P], X[:, m, t * P:(t + 1) * P])
            last.then_inc(S["out_T"], 1)

    stack.close()


def tables():
    import numpy as np
    f = np.float32
    i = np.arange(P)
    tab = np.zeros((P, TABLE), f)
    tab[:, T_ID:T_ID + P] = np.eye(P)
    q, k = i[:, None], i[None, :]
    tab[:, T_MPREV:T_MPREV + P] = np.where(k >= q, 0.0, -1e30)
    tab[:, T_MNEXT:T_MNEXT + P] = np.where(k <= q, 0.0, -1e30)
    tab[:, T_BLOCK:T_BLOCK + P] = (i[:, None] // HD == i[None, :] // HD)
    tok = np.arange(LAT)

    def cs(pos, half):
        fr = (f(10000.0) ** (-np.arange(half, dtype=f) / f(half))).astype(f)
        ang = (pos.astype(f)[:, None] * fr[None, :]).astype(f).astype(np.float64)
        return np.cos(ang), np.sin(ang)

    rc, rsn = cs(tok // 64, 16)
    cc, csn = cs(tok % 64, 16)
    tc, tsn = cs(tok, 32)
    rope = np.stack([np.concatenate([rc, rc, cc, cc], 1), np.concatenate([-rsn, rsn, -csn, csn], 1),
                     np.concatenate([tc, tc], 1), np.concatenate([-tsn, tsn], 1)], 1)
    tab[:, T_ROPE:T_TMP] = rope.reshape(NL, P, 4 * HD).transpose(1, 0, 2).reshape(P, -1)
    t0 = tab[:, T_TMP:]
    kq = i[None, :] - i[:, None]
    t0[:, TMP_DPOS:TMP_DPOS + P] = np.maximum(kq, 0)
    t0[:, TMP_DNEG:TMP_DNEG + P] = np.maximum(-kq, 0)
    t0[:, TMP_MPOS:TMP_MPOS + P] = kq >= 0
    t0[:, TMP_MNEG:TMP_MNEG + P] = kq <= 0
    j = np.arange(HD)
    ang = 2 * np.pi * (np.outer(j, j) % HD) / HD
    for s, m in enumerate((np.cos(ang), -np.sin(ang))):
        for b in range(2):
            t0[b * HD:(b + 1) * HD, TMP_C + s * P + b * HD:TMP_C + s * P + (b + 1) * HD] = m
    t0[:, TMP_IDX:TMP_IDX + 4] = np.stack([i + 1, P - 1 - i, P - i, i], 1)

    def dft(n):
        w = 2 * np.pi * (np.outer(np.arange(n), np.arange(n)) % n) / n
        return (np.stack([np.cos(w), np.sin(w)]) / np.sqrt(n * HD)).astype(f)

    lat = dft(LAT).reshape(2, NL, P, LAT).transpose(1, 2, 0, 3).reshape(NL, P, 2 * LAT)
    ctx = dft(CTX).reshape(2, 2, P, CTX).transpose(2, 0, 1, 3).reshape(P, 4 * CTX)
    return {"table": tab, "dft_lat": np.ascontiguousarray(lat), "dft_ctx": np.ascontiguousarray(ctx)}


_INS = ["x", "c", "ctx", "c_ctx", "w_mod", "b_mod", "norm1_g", "norm2_g", "w_in", "w_out", "q_norm_g", "k_norm_g",
        "attn_sink", "ret_decay_logit", "ret_gn_g", "fourier_w", "w_ff1", "w_ff2"]


def kernel(**inputs):
    import numpy as _np
    import concourse.bacc as _bacc
    from concourse import mybir as _mybir
    from concourse.bass_utils import run_bass_kernel_spmd as _run

    nc = _bacc.Bacc("TRN2", target_bir_lowering=False, num_devices=1)
    arrays, args = {}, {}
    consts = tables()
    for name in _INS + list(consts):
        v = _np.ascontiguousarray(consts[name] if name in consts else inputs[name])
        arrays[f"in_{name}_dram"] = v
        args[name] = nc.dram_tensor(f"in_{name}_dram", v.shape, _mybir.dt.from_np(v.dtype), kind="ExternalInput").ap()
    args["out"] = nc.dram_tensor("out_0_dram", (1, LAT, D), _mybir.dt.float32, kind="ExternalOutput").ap()
    build(nc, args)
    r = _run(nc, [arrays], core_ids=[0])
    return r.results[0]["out_0_dram"]
```

```python
import concourse.bass as bass
from concourse import mybir
from contextlib import ExitStack

P = 128
D, DEPTH, LAT, CTX = 1024, 2, 512, 256
KT = D // P
NT, NL = (LAT + CTX) // P, LAT // P
COLS = LAT + CTX
HD = 64
FL, FC = LAT // 2 + 1, CTX // 2 + 1
GROUPS = [(0, 512), (512, 512), (1024, 512), (1536, 512), (2048, 256)]
DFF = 4096
CHUNK = 4
NCHUNK = DFF // P // CHUNK
UE = 1024
UP, UO, UF = 18, 8, 64
UL = UP + UO + UF
NMOD = 48
MCH = 512
NST = 5
EPS = 1e-6
WARM = 8
T_ID, T_MPREV, T_MNEXT, T_ROPE = 0, 128, 256, 384
T_TMP = T_ROPE + NL * 256
TMP_DPOS, TMP_DNEG, TMP_MPOS, TMP_MNEG, TMP_C, TMP_S, TMP_IDX, TMP_XI = 0, 128, 256, 384, 512, 640, 768, 772
TMP_W = TMP_XI + 2 * P
TABLE = T_TMP + TMP_W


def proj_tiles(layer):
    out = []
    for g, (_, n) in enumerate(GROUPS):
        for t in range(NT):
            if layer == DEPTH - 1 and t >= NL and g in (0, 3, 4):
                continue
            out.append((g, t, 256 if (layer == DEPTH - 1 and t >= NL and g == 1) else n))
    return out


def build(nc, a):
    fp32, f32r, bf16 = mybir.dt.float32, mybir.dt.float32r, mybir.dt.bfloat16
    ALU, ACT, AX = mybir.AluOpType, mybir.ActivationFunctionType, mybir.AxisListType.X
    stack = ExitStack()

    def sb(name, shape, dt=fp32):
        return stack.enter_context(nc.sbuf_tensor(name, shape, dt))

    def overlay(*plans):
        got = []
        for n, plan in enumerate(plans):
            inner = ExitStack()
            target = stack if n == len(plans) - 1 else inner
            got.append([target.enter_context(nc.sbuf_tensor(*p)) for p in plan])
            inner.close()
        return got

    X = sb("X", [P, KT, COLS])
    (rs,), (Ahi, Alo) = overlay(
        [("ret_scratch", [P, 18, 512], fp32)],
        [("Ahi", [P, KT, COLS], f32r), ("Alo", [P, KT, COLS], f32r)])
    (Xin, rows, maskf, modst), (Zs, Zc), (SD,), (Pb, PTs, AO, _, _, _, kh), (Hhi, Hlo, tmpt), (Pq, Pk, Pr, Pg, Pu) = overlay(
        [("Xin", [P, NT, D], fp32), ("rows", [P, 2, P], fp32), ("maskf", [P, 2, P], fp32),
         ("modst", [P, NST, UE], fp32)],
        [("Zs", [P, 2, 2, LAT], fp32), ("Zc", [P, 2, 2, CTX], fp32)],
        [("SD", [P, 2, NT, 2, P], fp32)],
        [("Pb", [P, 2, 640], fp32), ("PTs", [P, 2, 640], fp32), ("AO", [P, 512], fp32), ("skip_Pk", [P, NT, 512], fp32),
         ("skip_Pr", [P, NT, 512], fp32), ("skip_Pg", [P, NT, 512], fp32), ("kh", [P, 2, COLS], f32r)],
        [("Hhi", [P, 2, CHUNK, COLS], f32r), ("Hlo", [P, 2, CHUNK, COLS], f32r), ("tmpt", [P, 1536], fp32)],
        [("Pq", [P, NT, 512], fp32), ("Pk", [P, NT, 512], fp32), ("Pr", [P, NT, 512], fp32),
         ("Pg", [P, NT, 512], fp32), ("Pu", [P, NT, 256], fp32)])
    PG = [Pq, Pk, Pr, Pg, Pu]
    (Tb, Ab, sqb, _, macc), (outs,), (_, _, scr), (_, kl), (qT, kT, rqT, rkT) = overlay(
        [("Tb", [P, 2, COLS], fp32), ("Ab", [P, 2, COLS], fp32), ("sqb", [P, 2, COLS], fp32), ("skip_scr", [P, COLS], fp32),
         ("macc", [P, 2, 512], fp32)],
        [("outs", [P, NL, D], fp32)],
        [("skip_q", [P, 4, COLS], fp32), ("skip_k", [P, COLS], fp32), ("scr", [P, 3, 512], fp32)],
        [("skip_q2", [P, 4, COLS], fp32), ("kl", [P, COLS], f32r)],
        [("qT", [P, 4, COLS], fp32), ("kT", [P, COLS], fp32), ("rqT", [P, 2, COLS], fp32), ("rkT", [P, 2, COLS], fp32)])
    raw = sb("raw", [P, 2, UE])
    (qs,), (modraw,) = overlay([("qs", [P, 2, 2, 4, P], f32r)], [("modraw", [P, 2, UE], fp32)])
    Whi = sb("Whi", [P, 2, UE], f32r)
    Wlo = sb("Wlo", [P, 2, UE], f32r)
    ident = sb("ident", [P, P])
    ones = sb("ones", [P, 1])
    rstd = sb("rstd", [P, 2, NT])
    warm = sb("warm", [P, 1])
    identb = sb("identb", [P, P], bf16)
    maskb = sb("maskb", [P, 2, P], bf16)
    rope = sb("rope", [P, NL, 4, HD])
    ropeg = sb("ropeg", [P, NL, 4, HD])
    decay = sb("decay", [P, 2, 4, P])
    WCS = sb("WCS", [P, 2, 2, P])
    bmodT = sb("bmodT", [P, DEPTH, NMOD])
    parT = sb("parT", [P, 48])
    csil = sb("csil", [P, KT, 2])
    modT = sb("modT", [P, DEPTH, NMOD, 2])
    gs = sb("gs", [P, DEPTH, 2, KT, 2])
    qkg = sb("qkg", [P, 2, HD])
    gng = sb("gng", [P, 256])
    sinkb = sb("sinkb", [P, DEPTH, 8])
    nsink = sb("nsink", [P, DEPTH, 8])
    dlog = sb("dlog", [P, DEPTH, 8])
    lgt = sb("lgt", [P, 4, 16])
    XQ = sb("XQ", [P, 2, 2, P])
    lgp = sb("lgp", [P, 2, 2])
    ZE = sb("ZE", [P, 2, 4])
    CD = sb("CD", [P, 2, 2])
    fw = tmpt[:, TMP_W:TMP_W + 2 * HD].rearrange("p (q d) -> p q d", q=2)
    ssq = sb("ssq", [P, NT, 10])
    srt = sb("srt", [P, NT, 10])
    mx = sb("mx", [P, 2])
    nm = sb("nm", [P, 2, 8])
    den = sb("den", [P, 2, 8])
    esi = sb("esi", [P, 8])
    es = sb("es", [P, 8])
    gst = sb("gst", [P, 3, 4, 8])
    epst = sb("epst", [P, 1])

    def pb(name, n):
        return stack.enter_context(nc.psum_tensor(name, [P, n], fp32))

    psA, psB, psS = pb("psA", 1024), pb("psB", 1024), pb("psS", 1024)
    pair = [psA, psB]
    ps6, ps7 = pb("ps6", 512), pb("ps7", 512)
    tokbank = [psA[:, 0:512], psA[:, 512:1024], psB[:, 0:512], psB[:, 512:1024], psS[:, 0:512], psS[:, 512:1024]]

    names = """consts_in x_in tmp_in stored rows_T par_ready csil_ready mod_pe mod_first mod_used mod_step modp_ready mod_red mod_evac xT_ready x_ready
        stat_sq stat_done sq_sum rt_sqrt rstd_ready rb_ready dve a_full a_hi a_lo_even a_lo_odd hi_done lo_done unit_done proj_ready p_ready qk_var qk_sqrt
        q_ready k_ready rq_ready rk_ready tr_ready tr_evac za_evac zb_evac zc_evac y_ready y_hi y_lo
        kz_ready kv_ready st_ready sc_ready md_ready sd_zero xq_ready gg_ready rot_step ret_ready g_cent g_sq g_gate g_var g_sqrt ro_ready rT_ready rT_hi rT_lo
        kq_hi kl_ready qb_hi qb_lo s_ready s_max s_exp pt_ready pt_evac pv_ready es_in es_out ao_ready aoT_ready aoT_hi aoT_lo
        lin_ready relu_done h_full h_hi h_lo resid_done prep_lg prep_e prep_act prep_w prep_wd prep_dm out_T out_a out_d
        act pool_init mask_ready""".split()
    S = {n: stack.enter_context(nc.semaphore(n)) for n in names}
    raw_in = [stack.enter_context(nc.semaphore(f"raw_in{i}")) for i in range(2)]
    mod_in = [stack.enter_context(nc.semaphore(f"mod_in{i}")) for i in range(2)]
    modst_in = [stack.enter_context(nc.semaphore(f"modst_in{i}")) for i in range(NST)]

    evac_index, n = {}, 0
    for l in range(DEPTH):
        for g, t, _ in proj_tiles(l):
            n += 2 if g == 2 else 1
            evac_index[l, g, t] = n
    TT = [NT, NL]
    CW = [COLS, LAT]
    SPLITS = [[(0, 512), (512, 256)], [(0, 512)]]
    MOD0 = 16
    MOD1 = 53
    DFT_FIRST = [40, 101]
    LATE = 45
    WALK = [[4, 5, 0, 1, 2, 3], [5, 4, 3, 2, 1, 0]]
    HPOS = [0, 2, 1, 3]
    LT = UO + 32 + 64
    trs = []
    for l in range(DEPTH):
        trs.append([("q", t) for t in range(TT[l])] + [("k", 0)] + [(k, p) for k in ("rq", "rk") for p in range(2)])
    TR_FIRST = [0, len(trs[0])]
    ITEMS = []
    for l in range(DEPTH):
        for b in range(TT[l]):
            for k in range(8):
                ITEMS.append((l, b, k // 2 + 4 * (k % 2), k))
    ITEM_FIRST = [0, 8 * TT[0]]

    def band(b):
        if b >= NL:
            return [], None, None
        ks = list(range(max(0, b - 1), min(NL, b + 2)))
        return ks, (0 if b > 0 else None), (len(ks) - 1 if b < NL - 1 else None)

    def kz_at(e):
        return rs[:, e // 2, (e % 2) * 256:(e % 2) * 256 + 256]

    def cent_at(t):
        return rs[:, t % 3, :]

    def sq_at(t):
        return rs[:, 3 + t % 2, :]

    def sum_at(t):
        return rs[:, 5, (t % 2) * 256:(t % 2) * 256 + 256]

    def xq_at(t):
        return rs[:, 12 + t % 2, :]

    def md_at(t, d):
        return rs[:, 14 + 2 * (t % 2) + d, :]

    def kv_at(e):
        bank = (ps6[:, :], ps7[:, :], psS[:, 0:512], psS[:, 512:1024])[e // 2 % 4]
        return bank[:, (e % 2) * 256:(e % 2) * 256 + 256]

    NST_E = 2 * (NT - 1)
    Q_TR = [TR_FIRST[l] + TT[l] + 3 for l in range(DEPTH)]

    def norm_at(j):
        return (Tb, Ab)[j // 2 % 2][:, j % 2, :]

    sq_sums = Ab[:, 0, :]

    def a_lo(n, j):
        return S[("a_lo_even", "a_lo_odd")[j % 2]], 4 * n + j // 2 + 1

    def unit_through(u):
        l, j = u // UL, u % UL
        if j < UP:
            return "unit_done", UP * l + j + 1
        j -= UP
        if j < UO:
            return "lin_ready", LT * l + j + 1
        j -= UO
        if j < 4:
            return "lin_ready", LT * l + UO + j + 1
        c, k = (j - 4) // 8, (j - 4) % 8
        if c == NCHUNK - 1:
            k += 4
        return "lin_ready", LT * l + UO + 4 + 12 * c + (k + 1 if k < 4 else 4 * (c < NCHUNK - 1) + 2 * (k - 3))

    def proj_signal(l, g, t):
        here = [tt for gg, tt, _ in proj_tiles(l) if gg == g]
        if t == here[-1]:
            return "unit_done", UP * l + (4 * g + 4 if g < 4 else UP)
        n = sum(len(proj_tiles(x)) - len(GROUPS) for x in range(l))
        for gg in range(g):
            n += sum(1 for x, _, _ in proj_tiles(l) if x == gg) - 1
        return "proj_ready", n + here.index(t) + 1

    blk = stack.enter_context(nc.Block())

    @blk.sync
    def _(sp):
        def w_load(u, slot, dst, src, first):
            if not first:
                sp.wait_ge(S["lo_done"], u - 1)
            sp.dma_start(dst, src).then_inc(raw_in[slot], 16)

        def m_load(w, slot, dst, src):
            if not isinstance(w, int) or w > MOD0 + 1:
                sp.wait_ge(S["mod_used"], w - 1 - MOD0)
            sp.dma_start(dst, src).then_inc(mod_in[slot], 16)

        r8 = lambda slot: raw[:, slot, :].rearrange("p (k n) -> p k n", k=8)
        r2 = lambda slot: raw[:, slot, :].rearrange("p (k n) -> p k n", k=2)
        r4 = lambda slot: raw[:, slot, :].rearrange("p (k n) -> p k n", k=4)
        m2 = lambda slot: modraw[:, slot, :].rearrange("p (k n) -> p k n", k=2)

        def mod_src(l, chunk, part):
            return a["w_mod"][l].rearrange("(k p) n -> p k n", p=P)[:, 2 * part:2 * part + 2, bass.ds(chunk * MCH, MCH)]

        def proj_src(l, u):
            g, part = u // 4, u % 4
            c0, n = GROUPS[g]
            k = 2 if n == 512 else 4
            v = a["w_in"][l].rearrange("(k p) n -> p k n", p=P)
            return v[:, part * k:(part + 1) * k, c0:c0 + n]

        def ff1_src(l, f):
            return a["w_ff1"][l].rearrange("(k p) n -> p k n", p=P)[:, :, bass.ds(f * P, P)]

        def ff2_src(l, c, o):
            return a["w_ff2"][l].rearrange("(k p) n -> p k n", p=P)[:, bass.ds(c * CHUNK, CHUNK), o * 256:(o + 1) * 256]

        def tmp_load(l):
            for i, nme in enumerate(("q_norm_g", "k_norm_g")):
                sp.dma_start(qkg[:, i, :], a[nme][l].partition_broadcast(P)).then_inc(S["tmp_in"], 16)
            sp.dma_start(gng[:, :], a["ret_gn_g"][l].partition_broadcast(P)).then_inc(S["tmp_in"], 16)
            sp.dma_start(tmpt[:, 0:TMP_W], a["table"][:, T_TMP:TABLE]).then_inc(S["tmp_in"], 16)
            for pp in range(2):
                sp.dma_start(fw[:, pp, :], a["fourier_w"][l, 2 * pp:2 * pp + 2].rearrange("g c d -> (g c) d"))\
                    .then_inc(S["tmp_in"], 16)

        con = S["consts_in"]
        sp.dma_start(ident[:, :], a["table"][:, T_ID:T_ID + P]).then_inc(con, 16)
        sp.dma_start(rows[0:96, 0, :], a["b_mod"].rearrange("l (t p) -> (l t) p", p=P)).then_inc(con, 16)
        for i, nme in enumerate(("norm1_g", "norm2_g")):
            sp.dma_start(rows[16 * i:16 * i + 16, 1, :], a[nme].rearrange("l (t p) -> (l t) p", p=P)).then_inc(con, 16)
        sp.dma_start(rows[32:40, 1, :], a["c"].rearrange("o (t p) -> (o t) p", p=P)).then_inc(con, 16)
        sp.dma_start(rows[40:48, 1, :], a["c_ctx"].rearrange("(t p) -> t p", p=P)).then_inc(con, 16)

        def first_mod(i):
            if i >= NST:
                before = i - NST
                sp.wait_ge(S[("mod_pe", "mod_first")[before % 2]], before // 2 + 1)
            w = 8 * (i % 2) + i // 2
            sp.dma_start(modst[:, i % NST, :].rearrange("p (k n) -> p k n", k=2), mod_src(0, w // 4, w % 4)).then_inc(modst_in[i % NST], 16)

        for w in range(NST):
            first_mod(w)
        sp.dma_start(maskf[:, :, :], a["table"][:, T_MPREV:T_MPREV + 2 * P].rearrange("p (a b) -> p a b", a=2)).then_inc(con, 16)
        sp.dma_start(rope[:, :, :, :].rearrange("p a b c -> p (a b c)"), a["table"][:, T_ROPE:T_TMP]).then_inc(con, 16)
        sp.dma_start(sinkb[:, :, :], a["attn_sink"].partition_broadcast(P)).then_inc(con, 16)
        sp.dma_start(dlog[:, :, :], a["ret_decay_logit"].rearrange("l a h -> l (a h)").partition_broadcast(P)).then_inc(con, 16)
        tmp_load(0)
        for t in range(NT):
            src = a["x"][0, t * P:(t + 1) * P, :] if t < NL else a["ctx"][0, (t - NL) * P:(t - NL + 1) * P, :]
            sp.dma_start(Xin[:, t, :], src).then_inc(S["x_in"], 16)
        for w in range(NST, 16):
            first_mod(w)

        def beside(u):
            for w in (12 + 2 * u, 13 + 2 * u):
                m_load(w, w % 2, m2(w % 2), mod_src(0, w // 4, w % 4))

        def late(i):
            w = LATE + i
            m_load(w, w % 2, m2(w % 2), mod_src(0, (40 + i) // 4, i % 4))

        for l in range(DEPTH):
            u0 = l * UL
            for u in range(UP):
                dst = (r2 if u < 16 else r4)((u0 + u) % 2)
                w_load(u0 + u, (u0 + u) % 2, dst, proj_src(l, u), u0 + u < 2)
                if l == 0 and 4 <= u < 16:
                    beside(u - 2)
            wo = a["w_out"][l].rearrange("(k p) n -> p k n", p=P)
            for u in range(2):
                w_load(u0 + UP + u, (u0 + UP + u) % 2, r8((u0 + UP + u) % 2), wo[:, :, u * P:(u + 1) * P], False)
            for k in range(NL):
                w = DFT_FIRST[l] + k
                m_load(w, w % 2, modraw[:, w % 2, 0:2 * FL], a["dft_lat"][k])
            if l == 0:
                w = DFT_FIRST[l] + NL
                m_load(w, w % 2, modraw[:, w % 2, 0:4 * FC], a["dft_ctx"])
            for u in range(2, UO):
                w_load(u0 + UP + u, (u0 + UP + u) % 2, r8((u0 + UP + u) % 2), wo[:, :, u * P:(u + 1) * P], False)
                if l == 0 and u == 3:
                    sp.wait_ge(S["lin_ready"], 1)
                if l == 0 and u >= 3:
                    late(u - 3)
            if l == 0:
                for i in range(UO - 3, 8):
                    late(i)
            uf = u0 + UP + UO
            def half(c, mod):
                for k in range(8):
                    u = uf + 4 + c * 8 + k
                    slot = (uf + k) % 2
                    if k < 4:
                        w_load(u, slot, r8(slot), ff1_src(l, (c + 1) * 4 + k), False)
                    else:
                        w_load(u, slot, r4(slot), ff2_src(l, c, k - 4), False)
                    if mod:
                        slot = (MOD1 + k) % 2
                        m_load(MOD1 + c * 8 + k, slot, m2(slot), mod_src(1, c * 2 + k // 4, k % 4))

            for k in range(4):
                w_load(uf + k, (uf + k) % 2, r8((uf + k) % 2), ff1_src(l, k), False)
            if l == 0:
                sp.wait_ge(S["lin_ready"], UO)
                tmp_load(1)
            with sp.Fori(0, 6) as c:
                half(c, l == 0)
            half(6, False)
            for k in range(4):
                u = uf + 60 + k
                w_load(u, u % 2, r4(u % 2), ff2_src(l, NCHUNK - 1, k), False)
        for t in range(NL):
            sp.wait_ge(S["out_a"] if t % 2 == 0 else S["out_d"], t // 2 + 1)
            sp.dma_start(a["out"][0, t * P:(t + 1) * P, :], outs[:, t, :]).then_inc(S["stored"], 16)
        sp.wait_ge(S["stored"], 16 * NL)

    @blk.gpsimd
    def _(pool):
        nc.gpsimd.memset(WCS[:, :, :, :], 0.0).then_inc(S["pool_init"], 1)
        nc.gpsimd.memset(ones[:, :], 1.0).then_inc(S["pool_init"], 1)
        nc.gpsimd.memset(epst[:, :], EPS).then_inc(S["pool_init"], 1)

        def low_parts(u0, u1):
            with pool.Fori(u0 // 2, u1 // 2) as i:
                for s in range(2):
                    pool.wait_ge(S["hi_done"], i * 2 + s + 1)
                    nc.gpsimd.tensor_tensor(Wlo[:, s, :], raw[:, s, :], Whi[:, s, :], ALU.subtract).then_inc(S["lo_done"], 1)

        def low_part(u):
            pool.wait_ge(S["hi_done"], u + 1)
            nc.gpsimd.tensor_tensor(Wlo[:, u % 2, :], raw[:, u % 2, :], Whi[:, u % 2, :], ALU.subtract).then_inc(S["lo_done"], 1)

        steps = [0]

        def rotate(v, t, ready, out_sem):
            pool.wait_ge(S["p_ready"], ready)
            tmp = Ab[:, 0, 0:512]
            h4 = lambda x: x.rearrange("p (h d) -> p h d", h=4)
            halves = lambda x: x.rearrange("p (h f i) -> p h f i", h=4, f=2)
            c, sn = rope[:, t, 2, :], rope[:, t, 3, :].rearrange("p (f i) -> p f i", f=2)
            nc.gpsimd.tensor_tensor(h4(tmp[:, 0:256]), h4(v), c.unsqueeze(1).to_broadcast([P, 4, HD]), ALU.mult).then_inc(S["rot_step"], 1)
            for f in range(2):
                nc.gpsimd.tensor_tensor(halves(tmp[:, 256:512])[:, :, f, :], halves(v)[:, :, 1 - f, :],
                                        sn[:, f, :].unsqueeze(1).to_broadcast([P, 4, HD // 2]), ALU.mult).then_inc(S["rot_step"], 1)
            steps[0] += 3
            pool.wait_ge(S["rot_step"], steps[0])
            nc.gpsimd.tensor_tensor(v, tmp[:, 0:256], tmp[:, 256:512], ALU.add).then_inc(out_sem, 1)

        def norm(n, cols):
            for j in range(1, KT, 2):
                pool.wait_ge(S["a_hi"], 8 * n + j + 1)
                nc.gpsimd.tensor_tensor(Alo[:, j, 0:cols], norm_at(j)[:, 0:cols], Ahi[:, j, 0:cols], ALU.subtract).then_inc(S["a_lo_odd"], 1)

        low_parts(0, 2)
        for l in range(DEPTH):
            norm(2 * l, COLS)
            if l == 0:
                low_parts(2, 10)
                for i in range(8):
                    low_part(10 + i)
                    if i:
                        pool.wait_ge(S["rq_ready" if i <= 4 else "rk_ready"], i if i <= 4 else i - 4)
                    rotate(Pk[:, i % 4, 256:512] if i < 4 else Pr[:, i % 4, 0:256], i % 4, evac_index[0, 1 if i < 4 else 2, i % 4],
                           S["rq_ready" if i < 4 else "rk_ready"])
                low_parts(18, UP + 2)
            else:
                low_parts(l * UL + 2, l * UL + UP + 2)
            pool.wait_ge(S["prep_act"], 15 * (l + 1))
            pool.wait_ge(S["unit_done"], UP * (l + 1))
            for j in range(NT - 1):
                for d in range(2):
                    t = WALK[d][j]
                    e = 2 * j + d
                    if t < NL:
                        pool.wait_ge(S["rk_ready"], l * NL + t + 1)
                    else:
                        pool.wait_ge(S["p_ready"], evac_index[l, 2, t])
                    nc.gpsimd.tensor_tensor(kz_at(e).rearrange("p (h d) -> p h d", h=4), Pr[:, t, 0:256].rearrange("p (h d) -> p h d", h=4),
                                            ZE[:, d, :].unsqueeze(2).to_broadcast([P, 4, HD]), ALU.mult).then_inc(S["kz_ready"], 1)

            def decayed_queries(t):
                if t >= 2:
                    pool.wait_ge(S["ret_ready"], l * NT + t - 1)
                for d in range(2):
                    nc.gpsimd.tensor_tensor(xq_at(t).rearrange("p (d q n) -> p d q n", d=2, q=2)[:, d], rqT[:, :, t * P:(t + 1) * P],
                                            XQ[:, d, :, :], ALU.mult).then_inc(S["xq_ready"], 1)

            pool.wait_ge(S["y_ready"], 2 * l + (2 if l == 0 else 1))
            nc.gpsimd.memset(SD[:, :, :, :, :], 0.0).then_inc(S["sd_zero"], 1)
            pool.wait_ge(S["tr_evac"], Q_TR[l])
            decayed_queries(0)
            decayed_queries(1)
            for t in range(TT[l]):
                pool.wait_ge(S["p_ready"], evac_index[l, 3, t])
                nc.gpsimd.tensor_tensor(Pg[:, t, :].rearrange("p (d n) -> p d n", d=2), Pg[:, t, :].rearrange("p (d n) -> p d n", d=2),
                                        gng[:, :].unsqueeze(1).to_broadcast([P, 2, 256]), ALU.mult).then_inc(S["gg_ready"], 1)
            pool.wait_ge(S["gg_ready"], l * NT + TT[l])
            pool.wait_ge(S["kq_hi"], 4 * l + 4)
            for g in range(2):
                if g:
                    pool.wait_ge(S["kl_ready"], 2 * l + 1)
                q = slice(64 * g, 64 * g + 64)
                nc.gpsimd.tensor_tensor(kl[q, :], kT[q, :], kh[q, g, :], ALU.subtract).then_inc(S["kl_ready"], 1)
            pool.wait_ge(S["kl_ready"], 2 * l + 2)
            for t in range(TT[l]):
                if t + 2 < TT[l]:
                    decayed_queries(t + 2)
                pool.wait_ge(S["g_sq"], l * NT + t + 1)
                pool.wait_ge(S["gg_ready"], l * NT + t + 1)
                nc.gpsimd.tensor_tensor(cent_at(t), cent_at(t), Pg[:, t, :], ALU.mult).then_inc(S["g_gate"], 1)
            low_parts(l * UL + UP + 2, l * UL + UP + UO + 2)
            norm(2 * l + 1, CW[l])
            low_parts(l * UL + UP + UO + 2, min((l + 1) * UL + 2, DEPTH * UL))

    @blk.scalar
    def _(act):
        def hi(slot, round_, sem, value):
            act.wait_ge(raw_in[slot], round_ * 16 + 16)
            if sem is not None:
                act.wait_ge(S[sem], value)
            nc.scalar.activation(Whi[:, slot, :], raw[:, slot, :], ACT.Copy).then_inc(S["hi_done"], 1)

        def hi_static(u):
            if u < DEPTH * UL:
                sem, value = unit_through(u - 2) if u >= 2 else (None, 0)
                hi(u % 2, u // 2, sem, value)

        act_count = [0]

        def link(ins):
            ins.then_inc(S["act"], 1)
            act_count[0] += 1
            act.wait_ge(S["act"], act_count[0])

        def stat_squares(n, m, cols, ready, value):
            act.wait_ge(ready, value)
            if m >= 2:
                act.wait_ge(S["sq_sum"], 6 * n + (1 if m == 2 else m - 2))
            if m == KT - 1:
                link(nc.scalar.activation(warm[:, :], epst[:, :], ACT.Sqrt))
            nc.scalar.activation(sqb[:, m % 2, 0:cols], X[:, m, 0:cols], ACT.Square).then_inc(S["stat_sq"], 1)

        def norm(n, cols):
            l, g = n // 2, n % 2
            act.wait_ge(S["stat_done"], n + 1)
            nc.scalar.activation(rstd[:, 0, 0:cols // P], psS[:, 0:cols // P], ACT.Sqrt, scale=1.0 / D, bias=epst[:, 0:1]).then_inc(S["rt_sqrt"], 1)
            for k in range(KT):
                act.wait_ge(S["a_full"], 8 * n + k + 1)
                sh = modT[:, l, 24 * g + k, :]
                for dst in (Ahi[:, k, :], norm_at(k)) if k % 2 else (Ahi[:, k, :],):
                    if cols > LAT:
                        nc.scalar.activation(dst[:, LAT:cols], norm_at(k)[:, LAT:cols], ACT.Identity, bias=sh[:, 1:2])
                    last = nc.scalar.activation(dst[:, 0:LAT], norm_at(k)[:, 0:LAT], ACT.Identity, bias=sh[:, 0:1])
                last.then_inc(S["a_hi"], 1)

        def prep(l):
            act.wait_ge(S["prep_lg"], 4 * l + 1)
            link(nc.scalar.activation(lgt[:, 1, 0:8], lgt[:, 0, 0:8], ACT.Exp, scale=-1.0))
            nc.scalar.activation(lgt[:, 2, 0:8], lgt[:, 1, 0:8], ACT.Ln, bias=1.0).then_inc(S["prep_e"], 1)

        def prep_tables(l):
            act.wait_ge(S["prep_lg"], 4 * l + 4)
            act.wait_ge(S["tmp_in"], 96 * (l + 1))
            lg = lgt[:, 3, 0:8]
            for d in range(2):
                dist = tmpt[:, (TMP_DPOS, TMP_DNEG)[d]:(TMP_DPOS, TMP_DNEG)[d] + P]
                for h in range(4):
                    nc.scalar.activation(decay[:, d, HPOS[h], :], dist, ACT.Exp, scale=lgt[:, 3, 4 * d + h:4 * d + h + 1]).then_inc(S["prep_act"], 1)
                nc.scalar.activation(ZE[:, d, :], lg[:, 4 * d:4 * d + 4], ACT.Exp, scale=tmpt[:, TMP_IDX + d:TMP_IDX + d + 1]).then_inc(S["prep_act"], 1)
                for q in range(2):
                    nc.scalar.activation(XQ[:, d, q, :], tmpt[:, TMP_XI + d * P:TMP_XI + (d + 1) * P], ACT.Exp, scale=lgp[:, d, q:q + 1]).then_inc(S["prep_act"], 1)
            nc.scalar.activation(CD[:, :, :], lgp[:, :, :], ACT.Exp, scale=float(P)).then_inc(S["prep_act"], 1)

        act.wait_ge(S["pool_init"], 3)
        act.wait_ge(S["par_ready"], 2)
        nc.scalar.activation(csil[:, :, :], parT[:, 32:48].rearrange("p (s k) -> p k s", s=2), ACT.Silu).then_inc(S["csil_ready"], 1)
        for m in range(KT):
            act.wait_ge(S["xT_ready"], m + 1)
            nc.scalar.activation(X[:, m, :], pair[m % 2][:, 0:COLS], ACT.Copy).then_inc(S["x_ready"], 1)
            if m:
                stat_squares(0, m - 1, COLS, S["x_ready"], m)
        stat_squares(0, KT - 1, COLS, S["x_ready"], KT)
        hi_static(0)
        hi_static(1)

        for l in range(DEPTH):
            u0, uf = l * UL, l * UL + UP + UO
            norm(2 * l, COLS)
            tiles = proj_tiles(l)
            for u in range(UP):
                last_of_group = (u % 4 == 3) if u < 16 else (u == 17)
                if last_of_group:
                    g = u // 4
                    if g == 4:
                        act.wait_ge(S["prep_dm"], 2 * l + 2)
                    for j, (gg, t, w) in enumerate(tiles):
                        if gg != g:
                            continue
                        sem, value = proj_signal(l, g, t)
                        act.wait_ge(S[sem], value)
                        dst, src = PG[g][:, t, 0:w], tokbank[t][:, 0:w]
                        if g == 0:
                            dst = dst.rearrange("p (j a d) -> p a j d", j=4, a=2)
                            src = src.rearrange("p (a j d) -> p a j d", a=2, j=4)
                        if g == 2:
                            nc.scalar.activation(dst[:, 0:256], src[:, 0:256], ACT.Copy, scale=HD ** -0.5).then_inc(S["p_ready"], 1)
                            nc.scalar.activation(dst[:, 256:512], src[:, 256:512], ACT.Copy).then_inc(S["p_ready"], 1)
                        else:
                            nc.scalar.activation(dst, src, ACT.Silu if g == 3 else ACT.Copy).then_inc(S["p_ready"], 1)
                hi_static(u0 + u + 2)
                if u == 0:
                    prep(l)
                if u == 2:
                    prep_tables(l)
                if u == 9:
                    act.wait_ge(S["qk_var"], l + 1)
                    nc.scalar.activation(srt[:, :, :], ssq[:, :, :], ACT.Sqrt).then_inc(S["qk_sqrt"], 1)
            if l == 0:
                act.wait_ge(S["rk_ready"], NL)
            for j, (kind, i) in enumerate(trs[l]):
                act.wait_ge(S["tr_ready"], TR_FIRST[l] + j + 1)
                src = pair[(TR_FIRST[l] + j) % 2]
                if kind == "q":
                    dst, src = qT[:, :, i * P:(i + 1) * P], src[:, 0:512].rearrange("p (a b) -> p a b", a=4)
                elif kind == "k":
                    dst, src = kT[:, :], src[:, 0:COLS]
                else:
                    dst, src = (rqT if kind == "rq" else rkT)[:, i, 0:CW[l]], src[:, 0:CW[l]]
                nc.scalar.activation(dst, src, ACT.Copy).then_inc(S["tr_evac"], 1)
            act.wait_ge(S["mod_used"], DFT_FIRST[l] + NL - MOD0)
            za = psA[:, :].rearrange("p (a b) -> p a b", a=2)
            nc.scalar.activation(Zs[:, 0, :, 0:FL], za[:, :, 0:FL], ACT.Copy)
            nc.scalar.activation(Zs[:, 0, :, FL:LAT], za[:, :, LAT - FL:0:-1], ACT.Copy).then_inc(S["za_evac"], 1)
            if l == 0:
                act.wait_ge(S["mod_used"], DFT_FIRST[0] + NL + 1 - MOD0)
                for s in range(2):
                    zc = psS[:, s * 512:(s + 1) * 512].rearrange("p (a b) -> p a b", a=2)
                    nc.scalar.activation(Zc[:, s, :, 0:FC], zc[:, :, 0:FC], ACT.Copy)
                    nc.scalar.activation(Zc[:, s, :, FC:CTX], zc[:, :, CTX - FC:0:-1], ACT.Copy, scale=1.0 - 2 * s).then_inc(S["zc_evac"], 1)
            for g in range(2):
                for half_ in range(2):
                    nc.scalar.activation(kh[64 * half_:64 * half_ + 64, g, :], kT[64 * g:64 * g + 64, :], ACT.Copy).then_inc(S["kq_hi"], 1)

            def query_hi(b):
                if b >= 2:
                    act.wait_ge(S["s_ready"], ITEM_FIRST[l] + 8 * (b - 1))
                for g in range(2):
                    q = slice(64 * g, 64 * g + 64)
                    nc.scalar.activation(qs[q, b % 2, g, :, :], qT[q, :, b * P:(b + 1) * P], ACT.Copy).then_inc(S["qb_hi"], 1)

            query_hi(0)
            n_items = 8 * TT[l]
            act.wait_ge(S["y_ready"], 2 * l + 1)
            nc.scalar.activation(Ahi[:, 6:8, 0:LAT], psA[:, :].rearrange("p (a b) -> p a b", a=2), ACT.Copy).then_inc(S["y_hi"], 1)
            if l == 0:
                act.wait_ge(S["y_ready"], 2)
                nc.scalar.activation(Ahi[:, 6:8, LAT:COLS], psB[:, 0:512].rearrange("p (a b) -> p a b", a=2), ACT.Copy).then_inc(S["y_hi"], 1)
            def retention(s):
                if 1 <= s < TT[l] + 1:
                    t, r = s - 1, l * NT + s - 1
                    act.wait_ge(S["g_cent"], r + 1)
                    if t >= 2:
                        act.wait_ge(S["g_var"], r - 1)
                    nc.scalar.activation(sq_at(t), cent_at(t), ACT.Square).then_inc(S["g_sq"], 1)
                if 2 <= s < TT[l] + 2:
                    t, r = s - 2, l * NT + s - 2
                    act.wait_ge(S["g_var"], r + 1)
                    nc.scalar.activation(gst[:, t % 3, 2, :], gst[:, t % 3, 1, :], ACT.Sqrt).then_inc(S["g_sqrt"], 1)
                if s >= 4:
                    t, r = s - 4, l * NT + s - 4
                    act.wait_ge(S["rT_ready"], r + 1)
                    nc.scalar.activation(Ahi[:, 4:6, t * P:(t + 1) * P], (ps6, ps7)[t % 2][:, 0:256].rearrange("p (a b) -> p a b", a=2), ACT.Copy).then_inc(S["rT_hi"], 1)
            def attention(s):
                if 2 <= s < n_items + 2:
                    it = ITEM_FIRST[l] + s - 2
                    w = (len(band(ITEMS[it][1])[0]) + 2) * P
                    act.wait_ge(S["pt_ready"], it + 1)
                    if it >= 2:
                        act.wait_ge(S["pv_ready"], it - 1)
                    nc.scalar.activation(PTs[:, it % 2, 0:w], psS[:, 0:w], ACT.Copy).then_inc(S["pt_evac"], 1)
                if s < n_items:
                    it = ITEM_FIRST[l] + s
                    _, b, h, k = ITEMS[it]
                    if k == 5 and b + 1 < TT[l]:
                        query_hi(b + 1)
                    ks, _, _ = band(b)
                    w = (len(ks) + 2) * P
                    q = b % 2
                    act.wait_ge(S["s_max"], it + 1)
                    if it >= 2:
                        act.wait_ge(S["pt_ready"], it - 1)
                    nc.scalar.activation(Pb[:, it % 2, 0:w], pair[it % 2][:, 0:w], ACT.Exp, bias=nm[:, q, h:h + 1],
                                         scale=HD ** -0.5, accum_out=den[:, q, h:h + 1]).then_inc(S["s_exp"], 1)
                    if k == 7:
                        act.wait_ge(S["es_in"], l * NT + b + 1)
                        nc.scalar.activation(es[:, :], esi[:, :], ACT.Exp).then_inc(S["es_out"], 1)
                if s >= 12 and (s - 12) % 8 == 0 and (s - 12) // 8 < TT[l]:
                    b = (s - 12) // 8
                    act.wait_ge(S["aoT_ready"], l * NT + b + 1)
                    nc.scalar.activation(Ahi[:, 0:4, b * P:(b + 1) * P], (ps6, ps7)[b % 2][:, :].rearrange("p (a b) -> p a b", a=4), ACT.Copy).then_inc(S["aoT_hi"], 1)
            for s in range(TT[l]):
                retention(s)
            retention(TT[l])
            for i in range(3):
                retention(TT[l] + 1 + i)
                attention(i)
            for s in range(3, n_items + 5):
                attention(s)
            for u in range(UO):
                hi_static(u0 + UP + u + 2)
                if u >= 1:
                    stat_squares(2 * l + 1, u - 1, CW[l], S["resid_done"], 72 * l + u)
            stat_squares(2 * l + 1, 7, CW[l], S["resid_done"], 72 * l + 8)
            norm(2 * l + 1, CW[l])

            def relu(f, hpar, p, k, before):
                act.wait_ge(S["lin_ready"], before + 1)
                nc.scalar.activation(Tb[:, k % 2, 0:CW[l]], pair[p][:, 0:CW[l]], ACT.Relu).then_inc(S["relu_done"], 1)
                act.wait_ge(S["h_full"], f + 1)
                nc.scalar.activation(Hhi[:, hpar, k, 0:CW[l]], Ab[:, k % 2, 0:CW[l]], ACT.Copy).then_inc(S["h_hi"], 1)

            lin0 = 104 * l + 8
            for k in range(4):
                hi_static(uf + k + 2)
                relu(32 * l + k, 0, k % 2, k, lin0 + k)

            def half(c, par):
                for k in range(8):
                    hi((uf + k) % 2, (uf + 6 + k) // 2 + c * 4, "lin_ready",
                       lin0 + 4 + c * 12 + (k + 1 if k < 4 else 4 + 2 * (k - 3)))
                    if k < 4:
                        relu(32 * l + 4 + c * 4 + k, 1 - par, k % 2, k, lin0 + 4 + c * 12 + k)

            with act.Fori(0, 3) as cc:
                half(cc * 2, 0)
                half(cc * 2 + 1, 1)
            half(6, 0)
            for k in range(4):
                hi_static(uf + 62 + k)
                if l == 0:
                    for m in (2 * k, 2 * k + 1):
                        stat_squares(2, m, COLS, S["resid_done"], 64 + m + 1)
        for t in (0, 2):
            act.wait_ge(S["out_T"], t + 1)
            nc.scalar.activation(outs[:, t, :], pair[0][:, :], ACT.Copy).then_inc(S["out_a"], 1)

    @blk.vector
    def _(dve):
        V = nc.vector
        counts = {"rq_ready": NL, "rk_ready": NL}

        def link(ins, sem="dve"):
            counts[sem] = counts.get(sem, 0) + 1
            ins.then_inc(S[sem], 1)
            dve.wait_ge(S[sem], counts[sem])

        def bc(ap, axis, shape):
            return ap.unsqueeze(axis).to_broadcast(shape)

        def mod_unit(used, w, wd, part, src, acc):
            step = 0
            for kk in range(2):
                for s in range(2):
                    new = part == 0 and kk == 0
                    if not new:
                        if kk == 0 and s == 1:
                            if not isinstance(w, int) or w > 0:
                                dve.wait_ge(used, w)
                        else:
                            dve.wait_ge(S["mod_step"], wd * 3 + (kk and s + 1))
                    col = csil[:, 2 * part + kk, s:s + 1]
                    if new:
                        ins = V.tensor_scalar(acc[:, s, :], src[:, kk * MCH:(kk + 1) * MCH], col, None, ALU.mult)
                    else:
                        ins = V.scalar_tensor_tensor(out=acc[:, s, :], in0=src[:, kk * MCH:(kk + 1) * MCH], scalar=col,
                                                     in1=acc[:, s, :], op0=ALU.mult, op1=ALU.add)
                    step += 1
                    ins.then_inc(S["mod_step"] if step < 4 else used, 1)

        def mod_reduce(l, chunk, g):
            dve.wait_ge(S["modp_ready"], g + 1)
            for s, ps in ((0, ps6), (1, ps7)):
                V.tensor_reduce(modT[:, l, bass.ds(chunk * 4, 4), s], ps[:, :].rearrange("p (t k) -> p t k", t=4),
                                axis=AX, op=ALU.add).then_inc(S["mod_red"], 1)
            dve.wait_ge(S["mod_red"], g * 2 + 2)
            V.tensor_tensor(modT[:, l, bass.ds(chunk * 4, 4), :], modT[:, l, bass.ds(chunk * 4, 4), :],
                            bc(bmodT[:, l, bass.ds(chunk * 4, 4)], 2, [P, 4, 2]), ALU.add).then_inc(S["mod_evac"], 1)

        def gain(l, k):
            g = parT[:, 16 * k + 8 * l:16 * k + 8 * l + 8]
            link(V.scalar_tensor_tensor(out=gs[:, l, k, :, :], in0=modT[:, l, 24 * k + 8:24 * k + 16, :], scalar=1.0,
                                        in1=bc(g, 2, [P, 8, 2]), op0=ALU.add, op1=ALU.mult))

        def norm(l, k, cols):
            n = 2 * l + k
            dve.wait_ge(S["rt_sqrt"], n + 1)
            V.reciprocal(rstd[:, 1, 0:cols // P], rstd[:, 0, 0:cols // P]).then_inc(S["rstd_ready"], 1)

            def low(j):
                dve.wait_ge(S["a_hi"], 8 * n + j + 1)
                x, sh = norm_at(j), modT[:, l, 24 * k + j, :]
                if cols > LAT:
                    V.scalar_tensor_tensor(out=Alo[:, j, LAT:cols], in0=x[:, LAT:cols], scalar=sh[:, 1:2], in1=Ahi[:, j, LAT:cols],
                                           op0=ALU.add, op1=ALU.subtract)
                V.scalar_tensor_tensor(out=Alo[:, j, 0:LAT], in0=x[:, 0:LAT], scalar=sh[:, 0:1], in1=Ahi[:, j, 0:LAT],
                                       op0=ALU.add, op1=ALU.subtract).then_inc(S["a_lo_even"], 1)

            dve.wait_ge(S["rb_ready"], n + 1)
            for j in range(KT):
                if j >= 4 and j % 2:
                    dve.wait_ge(*a_lo(n, j - 4))
                x = norm_at(j)
                if cols > LAT:
                    V.scalar_tensor_tensor(out=x[:, LAT:cols], in0=X[:, j, LAT:cols], scalar=gs[:, l, k, j, 1:2], in1=ps7[:, 0:cols - LAT],
                                           op0=ALU.mult, op1=ALU.mult)
                V.scalar_tensor_tensor(out=x[:, 0:LAT], in0=X[:, j, 0:LAT], scalar=gs[:, l, k, j, 0:1], in1=ps6[:, 0:LAT],
                                       op0=ALU.mult, op1=ALU.mult).then_inc(S["a_full"], 1)
                if j % 2:
                    low(j - 1)

        def sq_add(n, m):
            w = CW[n // 2] if n % 2 else COLS
            dve.wait_ge(S["stat_sq"], 8 * n + m + 1)
            if m > 1:
                dve.wait_ge(S["sq_sum"], 6 * n + m - 1)
            V.tensor_tensor(sq_sums[:, 0:w], sqb[:, 0, 0:w] if m == 1 else sq_sums[:, 0:w], sqb[:, m % 2, 0:w], ALU.add).then_inc(S["sq_sum"], 1)

        def prep_logit(l):
            x = dlog[:, l, :]
            link(V.tensor_scalar(lgt[:, 0, 8:16], x, -1.0, None, ALU.mult))
            link(V.tensor_tensor(lgt[:, 0, 0:8], x, lgt[:, 0, 8:16], ALU.max), "prep_lg")
            link(V.tensor_scalar(lgt[:, 3, 8:16], x, 0.0, None, ALU.min))

        def prep_gains(l):
            dve.wait_ge(S["tmp_in"], 96 * (l + 1))
            for i in range(2):
                g = qkg[:, i, :]
                link(V.tensor_tensor(ropeg[:, :, 2 * i, :], rope[:, :, 0, :], bc(g, 1, [P, NL, HD]), ALU.mult))
                for f in range(2):
                    gsw = g.rearrange("p (r f i) -> p r f i", r=2, f=2)[:, :, 1 - f, :]
                    o = ropeg[:, :, 2 * i + 1, :].rearrange("p t (r f i) -> p t r f i", r=2, f=2)
                    s = rope[:, :, 1, :].rearrange("p t (r f i) -> p t r f i", r=2, f=2)
                    for r in range(2):
                        link(V.tensor_tensor(o[:, :, r, f, :], s[:, :, r, f, :], bc(gsw[:, r, :], 1, [P, NL, 16]), ALU.mult))
            dve.wait_ge(S["prep_e"], l + 1)
            link(V.tensor_tensor(lgt[:, 3, 0:8], lgt[:, 3, 8:16], lgt[:, 2, 0:8], ALU.subtract), "prep_lg")
            for s in range(2):
                src = lgt[64 * s:64 * s + 64, 3, 0:8].rearrange("p (d q s) -> p d q s", d=2, s=2)
                link(V.tensor_copy(lgp[64 * s:64 * s + 64, :, :], src[:, :, :, s]), "prep_lg")

        def prep_masks(l):
            dve.wait_ge(S["prep_act"], 15 * (l + 1))
            for d in range(2):
                m = tmpt[:, (TMP_MPOS, TMP_MNEG)[d]:(TMP_MPOS, TMP_MNEG)[d] + P]
                link(V.tensor_tensor(decay[:, d, :, :], decay[:, d, :, :], bc(m, 1, [P, 4, P]), ALU.mult), "prep_dm")

        def fourier_copy(l):
            dve.wait_ge(S["prep_w"], l + 1)
            for s in range(2):
                q = slice(64 * s, 64 * s + 64)
                link(V.tensor_copy(WCS[q, :, :, 64 * s:64 * s + 64],
                                   ps7[q, 0:256].rearrange("p (a b c) -> p a b c", a=2, b=2)), "prep_wd")

        dve.wait_ge(S["pool_init"], 3)
        dve.wait_ge(S["rows_T"], 2)
        link(V.tensor_copy(bmodT[:, :, :].rearrange("p a b -> p (a b)"), ps7[:, 0:96]), "par_ready")
        link(V.tensor_copy(parT[:, :], ps7[:, 96:144]), "par_ready")
        link(V.tensor_copy(identb[:, :], ident[:, :]), "mask_ready")
        link(V.tensor_copy(maskb[:, :, :], maskf[:, :, :]), "mask_ready")
        link(V.tensor_scalar(nsink[:, :, :], sinkb[:, :, :], -1.0, None, ALU.mult))
        dve.wait_ge(S["csil_ready"], 1)
        maccs = [macc[:, :, :], Tb[:, :, 0:MCH]]

        def start(i):
            dve.wait_ge(modst_in[(2 * i + 1) % NST], 16 * ((2 * i + 1) // NST + 1))
            mod_unit(S["mod_first"], i, i, i % 4, modst[:, (2 * i + 1) % NST, :], maccs[i // 4])

        start(0)
        fourier_copy(0)
        for i in range(1, 8):
            start(i)
            if i >= 3:
                sq_add(0, i - 2)
            if i == 5:
                mod_reduce(0, 2, 0)
        for c in range(2):
            dve.wait_ge(S["mod_pe"], 8)
            V.tensor_tensor(modT[:, 0, 4 * c:4 * c + 4, :], psS[:, 512 + 8 * c:520 + 8 * c].rearrange("p (t s) -> p t s", t=4),
                            bc(bmodT[:, 0, 4 * c:4 * c + 4], 2, [P, 4, 2]), ALU.add).then_inc(S["mod_evac"], 1)
        mod_reduce(0, 3, 1)
        sq_add(0, 6)
        dve.wait_ge(S["mod_evac"], 4)
        gain(0, 0)

        def resid(l, chunk, m, p, value):
            dve.wait_ge(S["lin_ready"], value)
            w = CW[l]
            if w > LAT:
                V.scalar_tensor_tensor(out=X[:, m, LAT:w], in0=pair[p][:, LAT:w], scalar=modT[:, l, 8 * chunk + m, 1:2],
                                       in1=X[:, m, LAT:w], op0=ALU.mult, op1=ALU.add)
            V.scalar_tensor_tensor(out=X[:, m, 0:LAT], in0=pair[p][:, 0:LAT], scalar=modT[:, l, 8 * chunk + m, 0:1],
                                   in1=X[:, m, 0:LAT], op0=ALU.mult, op1=ALU.add).then_inc(S["resid_done"], 1)

        y_n = 0
        for l in range(DEPTH):
            prep_logit(l)
            norm(l, 0, COLS)
            def rotate(v, nh, C, Sn, r, out_sem):
                n, i = nh * HD, HD // (2 * r)
                v3 = v.rearrange("p (h d) -> p h d", h=nh)
                link(V.tensor_tensor(scr[:, 1, 0:n].rearrange("p (h d) -> p h d", h=nh), v3, bc(C, 1, [P, nh, HD]), ALU.mult))
                vs = v.rearrange("p (h r f i) -> p h r f i", h=nh, r=r, f=2)
                os = scr[:, 2, 0:n].rearrange("p (h r f i) -> p h r f i", h=nh, r=r, f=2)
                ss = Sn.rearrange("p (r f i) -> p r f i", r=r, f=2)
                for f in range(2):
                    for q in range(r):
                        link(V.tensor_tensor(os[:, :, q, f, :], vs[:, :, q, 1 - f, :], bc(ss[:, q, f, :], 1, [P, nh, i]), ALU.mult))
                link(V.tensor_tensor(v, scr[:, 1, 0:n], scr[:, 2, 0:n], ALU.add), out_sem)

            def q_squares(t):
                if t < TT[l]:
                    dve.wait_ge(S["p_ready"], evac_index[l, 0, t])
                    link(V.tensor_tensor(scr[:, 0, :], Pq[:, t, :], Pq[:, t, :], ALU.mult))
                    link(V.reduce_sum(ssq[:, t, 0:8], scr[:, 0, :].rearrange("p (h d) -> p h d", h=8), axis=AX))
                else:
                    link(V.memset(ssq[:, t, 0:8], 1.0))

            def k_squares():
                for t in range(NT):
                    dve.wait_ge(S["p_ready"], evac_index[l, 1, t])
                    link(V.tensor_tensor(scr[:, 0, 0:P], Pk[:, t, 0:P], Pk[:, t, 0:P], ALU.mult))
                    link(V.reduce_sum(ssq[:, t, 8:10], scr[:, 0, 0:P].rearrange("p (h d) -> p h d", h=2), axis=AX))
                link(V.tensor_scalar(ssq[:, :, :], ssq[:, :, :], 1.0 / HD, EPS, ALU.mult, ALU.add), "qk_var")

            def qk_roots():
                dve.wait_ge(S["qk_sqrt"], l + 1)
                link(V.reciprocal(srt[:, :, :], srt[:, :, :]))

            def qk(t):
                for v, nh, c0, i, sem in ((Pq[:, t, :], 8, 0, 0, "q_ready"), (Pk[:, t, 0:P], 2, 8, 1, "k_ready")):
                    if i == 0 and t >= TT[l]:
                        continue
                    v3 = v.rearrange("p (h d) -> p h d", h=nh)
                    link(V.tensor_tensor(v3, v3, bc(srt[:, t, c0:c0 + nh], 2, [P, nh, HD]), ALU.mult))
                    if t < NL:
                        rotate(v, nh, ropeg[:, t, 2 * i, :], ropeg[:, t, 2 * i + 1, :], 2, sem)
                    else:
                        link(V.tensor_tensor(v3, v3, bc(qkg[:, i, :], 1, [P, nh, HD]), ALU.mult), sem)

            def rq(t):
                rotate(Pk[:, t, 256:512], 4, rope[:, t, 2, :], rope[:, t, 3, :], 1, "rq_ready")

            def rk(t):
                dve.wait_ge(S["p_ready"], evac_index[l, 2, t])
                rotate(Pr[:, t, 0:256], 4, rope[:, t, 2, :], rope[:, t, 3, :], 1, "rk_ready")

            work = {2: [(prep_gains, l)], 5: [(prep_masks, l)], 6: [(q_squares, t) for t in (0, 1, 2)], 7: [(q_squares, t) for t in (3, 4, 5)], 9: [(k_squares,)],
                    11: [(qk_roots,), (qk, 0)], 12: [(qk, 1)], 13: [(qk, 2)], 14: [(qk, 3)], 15: [(qk, 4)],
                    16: [(qk, 5), (rq, 0)], 17: [(rq, 1), (rq, 2), (rq, 3)]}
            if l == 0:
                work = {u: [w for w in ws if w[0] is not rq] for u, ws in work.items()}
            for u in range(2, UP):
                if l == 0:
                    if u % 2 == 0 and u >= 6:
                        mod_reduce(0, u // 2 + 1, u // 2 - 1)
                    if u == 4:
                        dve.wait_ge(*a_lo(0, KT - 1))
                    for w in ((12 + 2 * u, 13 + 2 * u) if u < 14 else ()):
                        dve.wait_ge(mod_in[w % 2], 16 * ((w - MOD0) // 2 + 1))
                        mod_unit(S["mod_used"], w - MOD0, w - 8, w % 4, modraw[:, w % 2, :], maccs[w // 4 % 2])
                for f, *args in work.get(u, []):
                    f(*args)
            if l == 0:
                dve.wait_ge(S["mod_evac"], 10)
                gain(0, 1)
            if l:
                for t in range(NL):
                    rk(t)
            dve.wait_ge(S["mod_used"], DFT_FIRST[l] + NL - MOD0)
            zb = psB[:, :].rearrange("p (a b) -> p a b", a=2)
            V.tensor_copy(Zs[:, 1, :, 0:FL], zb[:, :, 0:FL])
            V.tensor_scalar(Zs[:, 1, :, FL:LAT], zb[:, :, LAT - FL:0:-1], -1.0, None, ALU.mult).then_inc(S["zb_evac"], 1)
            dve.wait_ge(S["y_hi"], 2 * l + 1)
            V.tensor_tensor(Alo[:, 6:8, 0:LAT], psA[:, :].rearrange("p (a b) -> p a b", a=2), Ahi[:, 6:8, 0:LAT], ALU.subtract).then_inc(S["y_lo"], 1)
            if l == 0:
                dve.wait_ge(S["y_hi"], 2)
                V.tensor_tensor(Alo[:, 6:8, LAT:COLS], psB[:, 0:512].rearrange("p (a b) -> p a b", a=2), Ahi[:, 6:8, LAT:COLS], ALU.subtract).then_inc(S["y_lo"], 1)
            dve.wait_ge(S["sd_zero"], l + 1)
            for e in range(NST_E):
                j, d = e // 2, e % 2
                before = l * NST_E * 4 + 4 * (e - 1)
                if e >= 2:
                    dve.wait_ge(S["st_ready"], before)
                dve.wait_ge(S["kv_ready"], l * (NT - 1) + j + 1)
                kv = kv_at(e)
                for s in range(2):
                    for q in range(2):
                        rows_, cols_ = slice(64 * s, 64 * s + 64), slice(64 * s, 64 * s + 64)
                        V.scalar_tensor_tensor(out=SD[rows_, d, j + 1, q, cols_], in0=SD[rows_, d, j, q, cols_], scalar=CD[rows_, d, q:q + 1],
                                               in1=kv[rows_, q * P + 64 * s:q * P + 64 * s + 64], op0=ALU.mult, op1=ALU.add)\
                            .then_inc(S["st_ready"], 1)
            def query_lo(b, g):
                dve.wait_ge(S["qb_hi"], 2 * (l * NT + b) + g + 1)
                q, across = slice(64 * g, 64 * g + 64), slice(64 - 64 * g, 128 - 64 * g)
                V.tensor_tensor(qs[across, b % 2, g, :, :], qT[q, :, b * P:(b + 1) * P], qs[q, b % 2, g, :, :], ALU.subtract).then_inc(S["qb_lo"], 1)

            n_items = 8 * TT[l]

            def retention(s):
                if s == TT[l] - 1:
                    query_lo(0, 0)
                    query_lo(0, 1)
                if s < TT[l]:
                    t, r = s, l * NT + s
                    dve.wait_ge(S["sc_ready"], r + 1)
                    if t >= 2:
                        dve.wait_ge(S["ret_ready"], r - 1)
                    for d in range(2):
                        V.tensor_tensor(md_at(t, d).rearrange("p (s n) -> p s n", s=2), pair[t % 2][:, :].rearrange("p (s n) -> p s n", s=2)[:, :, 0:256],
                                        decay[:, d, :, :].rearrange("p (s q) n -> p s (q n)", s=2), ALU.mult).then_inc(S["md_ready"], 1)
                if 1 <= s < TT[l] + 1:
                    t, r = s - 1, l * NT + s - 1
                    g = gst[:, t % 3]
                    o3 = psS[:, (t % 2) * 512:(t % 2) * 512 + 512].rearrange("p (h d) -> p h d", h=8)
                    dve.wait_ge(S["ret_ready"], r + 1)
                    link(V.reduce_sum(g[:, 0, :], o3, axis=AX))
                    link(V.tensor_scalar(g[:, 0, :], g[:, 0, :], -1.0 / HD, None, ALU.mult))
                    V.tensor_tensor(cent_at(t).rearrange("p (h d) -> p h d", h=8), o3, bc(g[:, 0, :], 2, [P, 8, HD]), ALU.add).then_inc(S["g_cent"], 1)
                if 2 <= s < TT[l] + 2:
                    t, r = s - 2, l * NT + s - 2
                    g = gst[:, t % 3]
                    dve.wait_ge(S["g_sq"], r + 1)
                    link(V.reduce_sum(g[:, 1, :], sq_at(t).rearrange("p (h d) -> p h d", h=8), axis=AX))
                    V.tensor_scalar(g[:, 1, :], g[:, 1, :], 1.0 / HD, EPS, ALU.mult, ALU.add).then_inc(S["g_var"], 1)
                if 3 <= s < TT[l] + 3:
                    t, r = s - 3, l * NT + s - 3
                    g = gst[:, t % 3]
                    dve.wait_ge(S["g_sqrt"], r + 1)
                    link(V.reciprocal(g[:, 3, :], g[:, 2, :]))
                    dve.wait_ge(S["g_gate"], r + 1)
                    c3 = cent_at(t).rearrange("p (h d) -> p h d", h=8)
                    link(V.tensor_tensor(c3, c3, bc(g[:, 3, :], 2, [P, 8, HD]), ALU.mult))
                    if t >= 2:
                        dve.wait_ge(S["rT_ready"], r - 1)
                    V.tensor_tensor(sum_at(t), cent_at(t)[:, 0:256], cent_at(t)[:, 256:512], ALU.add).then_inc(S["ro_ready"], 1)
                if s >= 4:
                    t, r = s - 4, l * NT + s - 4
                    dve.wait_ge(S["rT_hi"], r + 1)
                    V.tensor_tensor(Alo[:, 4:6, t * P:(t + 1) * P], (ps6, ps7)[t % 2][:, 0:256].rearrange("p (a b) -> p a b", a=2),
                                    Ahi[:, 4:6, t * P:(t + 1) * P], ALU.subtract).then_inc(S["rT_lo"], 1)

            def attention(s):
                if s >= 10 and (s - 10) % 8 == 0 and (s - 10) // 8 < TT[l]:
                    b = (s - 10) // 8
                    dve.wait_ge(S["es_out"], l * NT + b + 1)
                    link(V.tensor_tensor(es[:, :], es[:, :], den[:, b % 2, :], ALU.add))
                    link(V.reciprocal(es[:, :], es[:, :]))
                if s >= 11 and (s - 11) % 8 == 0 and (s - 11) // 8 < TT[l]:
                    b = (s - 11) // 8
                    dve.wait_ge(S["pv_ready"], ITEM_FIRST[l] + 8 * b + 8)
                    V.tensor_tensor(AO[:, :].rearrange("p (h d) -> p h d", h=8), (ps6, ps7)[b % 2][:, :].rearrange("p (h d) -> p h d", h=8),
                                    bc(es[:, :], 2, [P, 8, HD]), ALU.mult).then_inc(S["ao_ready"], 1)
                if s < n_items:
                    it = ITEM_FIRST[l] + s
                    _, b, h, k = ITEMS[it]
                    w = (len(band(b)[0]) + 2) * P
                    dve.wait_ge(S["s_ready"], it + 1)
                    link(V.reduce_max(mx[:, it % 2:it % 2 + 1], pair[it % 2][:, 0:w], axis=AX))
                    link(V.tensor_scalar(nm[:, b % 2, h:h + 1], mx[:, it % 2:it % 2 + 1], -HD ** -0.5, nsink[:, l, h:h + 1],
                                         ALU.mult, ALU.min), "s_max")
                    if k == 7:
                        if l * NT + b >= 1:
                            dve.wait_ge(S["es_out"], l * NT + b)
                        link(V.tensor_tensor(esi[:, :], nm[:, b % 2, :], sinkb[:, l, :], ALU.add), "es_in")
                    if k in (5, 6) and b + 1 < TT[l]:
                        query_lo(b + 1, k - 5)
                if s >= 12 and (s - 12) % 8 == 0 and (s - 12) // 8 < TT[l]:
                    b = (s - 12) // 8
                    dve.wait_ge(S["aoT_hi"], l * NT + b + 1)
                    V.tensor_tensor(Alo[:, 0:4, b * P:(b + 1) * P], (ps6, ps7)[b % 2][:, :].rearrange("p (a b) -> p a b", a=4),
                                    Ahi[:, 0:4, b * P:(b + 1) * P], ALU.subtract).then_inc(S["aoT_lo"], 1)

            for s in range(TT[l]):
                retention(s)
            retention(TT[l])
            for i in range(3):
                retention(TT[l] + 1 + i)
                attention(i)
            for s in range(3, n_items + 5):
                attention(s)
            for m in range(KT):
                resid(l, 2, m, m % 2, 104 * l + m + 1)
                if m >= 2:
                    sq_add(2 * l + 1, m - 1)
                if l == 0:
                    for i in ([0, 1] if m == 0 else [m + 1] if m < KT - 1 else []):
                        w = LATE + i
                        dve.wait_ge(mod_in[w % 2], 16 * ((w - MOD0) // 2 + 1))
                        mod_unit(S["mod_used"], w - MOD0, 32 + i, i % 4, modraw[:, w % 2, :], maccs[i // 4])
                    if m == 5:
                        mod_reduce(0, 10, 8)
            if l == 0:
                mod_reduce(0, 11, 9)
            norm(l, 1, CW[l])
            w = CW[l]

            def hidden(f, hpar, k):
                dve.wait_ge(S["relu_done"], f + 1)
                V.tensor_tensor(Ab[:, k % 2, 0:w], Tb[:, k % 2, 0:w], Tb[:, k % 2, 0:w], ALU.mult).then_inc(S["h_full"], 1)
                dve.wait_ge(S["h_hi"], f + 1)
                V.tensor_tensor(Hlo[:, hpar, k, 0:w], Ab[:, k % 2, 0:w], Hhi[:, hpar, k, 0:w], ALU.subtract).then_inc(S["h_lo"], 1)

            lin0 = 104 * l + 8
            for k in range(4):
                hidden(32 * l + k, 0, k)

            def half(c, par, mod):
                def m(*ks):
                    for k in ks:
                        if mod:
                            w = c * 8 + MOD1 + k
                            dve.wait_ge(mod_in[(MOD1 + k) % 2], c * 64 + 16 * ((MOD1 + k - MOD0) // 2 + 1))
                            mod_unit(S["mod_used"], w - MOD0, c * 8 + NMOD - 8 + k, k % 4, modraw[:, (MOD1 + k) % 2, :], macc)

                def r(*ms):
                    for i in ms:
                        resid(l, 5, i, i % 2, lin0 + 4 + c * 12 + 4 + i + 1)

                for k in range(4):
                    m(k)
                    hidden(32 * l + 4 + c * 4 + k, 1 - par, k)
                r(0, 1)
                if mod:
                    mod_reduce(1, c * 2, c * 2 + 10)
                m(4)
                r(2, 3)
                m(5, 6)
                r(4, 5)
                m(7)
                r(6, 7)
                if mod:
                    mod_reduce(1, c * 2 + 1, c * 2 + 11)

            with dve.Fori(0, 3) as cc:
                half(cc * 2, 0, l == 0)
                half(cc * 2 + 1, 1, l == 0)
            half(6, 0, False)
            if l == 0:
                fourier_copy(1)
            for m in range(KT):
                resid(l, 5, m, m % 2, lin0 + 88 + m + 1)
                if l == 0 and m >= 2:
                    sq_add(2, m - 1)
            if l == 0:
                dve.wait_ge(S["mod_evac"], 24)
                gain(1, 0)
                gain(1, 1)
        for t in (1, 3):
            dve.wait_ge(S["out_T"], t + 1)
            V.tensor_copy(outs[:, t, :], pair[1][:, :]).then_inc(S["out_d"], 1)

    @blk.tensor
    def _(pe):
        mm = nc.tensor.matmul

        def tr(out, in_, n=P):
            return nc.tensor.transpose(out, in_, ident[0:n, 0:n])

        def mod_sums(used, w, wd, acc):
            pe.wait_ge(used, w + 1)
            pe.wait_ge(S["mod_step"], wd * 3 + 3)
            for s, ps in ((0, ps6), (1, ps7)):
                for t in range(4):
                    last = tr(ps[:, t * P:(t + 1) * P], acc[:, s, t * P:(t + 1) * P])
            last.then_inc(S["modp_ready"], 1)

        def token_sums(n, squares, tiles_, first, last_):
            for t in range(tiles_):
                ins = mm(psS[:, t:t + 1], squares[:, t * P:(t + 1) * P], ones[:, :], start=(first and t == 0), stop=(last_ and t == tiles_ - 1))
            return ins

        def stats(n, tiles_):
            pe.wait_ge(S["sq_sum"], 6 * n + 6)
            token_sums(n, sq_sums, tiles_, True, False)
            pe.wait_ge(S["stat_sq"], 8 * n + 8)
            token_sums(n, sqb[:, 1], tiles_, False, True).then_inc(S["stat_done"], 1)

        def spread(n, tiles_):
            pe.wait_ge(S["rstd_ready"], n + 1)
            for t in range(tiles_):
                last = tr(ps6[:, t * P:(t + 1) * P] if t < NL else ps7[:, (t - NL) * P:(t - NL + 1) * P], rstd[:, 1, t:t + 1].to_broadcast([P, P]))
            last.then_inc(S["rb_ready"], 1)

        def fourier_weights(l):
            pe.wait_ge(S["tmp_in"], 96 * (l + 1))
            for s in range(2):
                for q in range(2):
                    last = mm(ps7[:, (2 * s + q) * HD:(2 * s + q + 1) * HD], tmpt[:, TMP_C + s * P:TMP_C + (s + 1) * P], fw[:, q, :], start=True, stop=True)
            last.then_inc(S["prep_w"], 1)

        def keep_clock(bank, n):
            for i in range(n):
                mm(bank[:, 0:512], Whi[:, 0, 0:P], Whi[:, 0, 0:512], start=True, stop=True)

        pe.wait_ge(S["consts_in"], 10 * 16)
        tr(ps7[:, 0:96], rows[0:96, 0, :], 96).then_inc(S["rows_T"], 1)
        tr(ps7[:, 96:144], rows[0:48, 1, :], 48).then_inc(S["rows_T"], 1)
        pe.wait_ge(S["par_ready"], 2)
        maccs = [macc[:, :, :], Tb[:, :, 0:MCH]]

        def first_mod(i):
            c, part = i // 4, i % 4
            pe.wait_ge(modst_in[2 * i % NST], 16 * (2 * i // NST + 1))
            for kk in range(2):
                for t in range(4):
                    k0, c0 = kk * MCH + t * P, 512 + 8 * c + 2 * t
                    last = mm(psS[:, c0:c0 + 2], modst[:, 2 * i % NST, k0:k0 + P], csil[:, 2 * part + kk, :],
                              start=(i == 0 and kk == 0 and t == 0), stop=(i == 7 and kk == 1 and t == 3))
            last.then_inc(S["mod_pe"], 1)

        pe.wait_ge(S["csil_ready"], 1)
        for i in range(3):
            first_mod(i)
            if i == 0:
                fourier_weights(0)
        pe.wait_ge(S["x_in"], 16 * NT)
        for m in range(KT):
            if m >= 2:
                pe.wait_ge(S["x_ready"], m - 1)
            for t in range(NT):
                last = tr(pair[m % 2][:, t * P:(t + 1) * P], Xin[:, t, m * P:(m + 1) * P])
            last.then_inc(S["xT_ready"], 1)
            if m < 5:
                first_mod(3 + m)
            if m == 3:
                pe.wait_ge(S["prep_wd"], 2)
                mod_sums(S["mod_first"], 3, 3, maccs[0])
        pe.wait_ge(S["mod_evac"], 1)
        mod_sums(S["mod_first"], 7, 7, maccs[1])
        stats(0, NT)
        pe.wait_ge(S["mod_evac"], 4)

        for l in range(DEPTH):
            u0, uf = l * UL, l * UL + UP + UO
            tiles = proj_tiles(l)
            pe.wait_ge(S["prep_wd"], 2 * l + 2)
            spread(2 * l, NT)
            for u in range(UP):
                g = u // 4
                n = GROUPS[g][1]
                nk = 2 if n == 512 else 4
                part = u % 4
                parts = 4 if n == 512 else 2
                uu = u0 + u
                pe.wait_ge(S["lo_done"], uu + 1)
                here = [(t, w) for gg, t, w in tiles if gg == g]
                for t, w in here:
                    if part == 0 and g > 0:
                        prev = max(gg for gg, tt, _ in tiles if tt == t and gg < g) if any(tt == t and gg < g for gg, tt, _ in tiles) else None
                        if prev is not None:
                            pe.wait_ge(S["p_ready"], evac_index[l, prev, t])
                    for kk in range(nk):
                        k = part * nk + kk
                        if t == 0 and g == 0:
                            pe.wait_ge(*a_lo(2 * l, k))
                        if w < n:
                            cs = slice(kk * n, kk * n + w)
                        else:
                            cs = slice(kk * n, (kk + 1) * n)
                        ah, al = Ahi[:, k, t * P:(t + 1) * P], Alo[:, k, t * P:(t + 1) * P]
                        wh, wl = Whi[:, uu % 2, cs], Wlo[:, uu % 2, cs]
                        first, fin = part == 0 and kk == 0, part == parts - 1 and kk == nk - 1
                        out = tokbank[t][:, 0:w]
                        mm(out, ah, wh, start=first, stop=False)
                        mm(out, ah, wl, start=False, stop=False)
                        last = mm(out, al, wh, start=False, stop=fin)
                    if t == here[-1][0]:
                        last.then_inc(S["unit_done"], 1)
                    elif part == parts - 1:
                        last.then_inc(S["proj_ready"], 1)
                for c in ([u // 2 + 2] if l == 0 and u % 2 and 5 <= u < 16 else []):
                    pe.wait_ge(S["mod_evac"], c)
                    mod_sums(S["mod_used"], 4 * c + 3 - MOD0, 4 * c - 5, maccs[c % 2])
            pe.wait_ge(S["p_ready"], max(v for (ll, _, _), v in evac_index.items() if ll == l))
            tb = [[0, 0, 0, 0], [NT, NT, NL, NL]][l]
            for j, (kind, i) in enumerate(trs[l]):
                if TR_FIRST[l] + j >= 2:
                    pe.wait_ge(S["tr_evac"], TR_FIRST[l] + j - 1)
                dst = pair[(TR_FIRST[l] + j) % 2]
                if kind == "q":
                    pe.wait_ge(S["q_ready"], tb[0] + i + 1)
                    for q in range(4):
                        last = tr(dst[:, q * P:(q + 1) * P], Pq[:, i, q * P:(q + 1) * P])
                elif kind == "k":
                    pe.wait_ge(S["k_ready"], tb[1] + NT)
                    for t in range(NT):
                        last = tr(dst[:, t * P:(t + 1) * P], Pk[:, t, 0:P])
                else:
                    pe.wait_ge(S["rq_ready"], tb[2] + NL)
                    pe.wait_ge(S["rk_ready"], tb[3] + NL)
                    for t in range(TT[l]):
                        src = Pk[:, t, 256 + i * P:256 + (i + 1) * P] if kind == "rq" else Pr[:, t, i * P:(i + 1) * P]
                        last = tr(dst[:, t * P:(t + 1) * P], src)
                last.then_inc(S["tr_ready"], 1)
            pe.wait_ge(S["tr_evac"], TR_FIRST[l] + len(trs[l]))
            for k in range(NL):
                w = DFT_FIRST[l] + k
                pe.wait_ge(mod_in[w % 2], 16 * ((w - MOD0) // 2 + 1))
                for s in range(2):
                    for c in range(2):
                        last = mm(pair[s][:, c * 512:c * 512 + FL], Pu[:, k, c * P:(c + 1) * P], modraw[:, w % 2, s * FL:(s + 1) * FL],
                                  start=(k == 0), stop=(k == NL - 1))
                last.then_inc(S["mod_used"], 1)
            if l == 0:
                w = DFT_FIRST[0] + NL
                pe.wait_ge(mod_in[w % 2], 16 * ((w - MOD0) // 2 + 1))
                tab = modraw[:, w % 2, 0:4 * FC].rearrange("p (s k n) -> p s k n", s=2, k=2)
                for s in range(2):
                    for c in range(2):
                        for k in range(2):
                            last = mm(psS[:, s * 512 + c * 256:s * 512 + c * 256 + FC], Pu[:, NL + k, c * P:(c + 1) * P], tab[:, s, k, :],
                                      start=(k == 0), stop=(k == 1))
                last.then_inc(S["mod_used"], 1)

            def key_values(e0, e1):
                for e in range(e0, e1):
                    t = WALK[e % 2][e // 2]
                    pe.wait_ge(S["kz_ready"], l * NST_E + e + 1)
                    if e >= 8:
                        pe.wait_ge(S["st_ready"], 4 * (l * NST_E + 2 * (e // 2 - 4) + 2))
                    for q in range(2):
                        last = mm(kv_at(e)[:, q * P:(q + 1) * P], kz_at(e)[:, q * P:(q + 1) * P], Pr[:, t, 256 + q * P:256 + (q + 1) * P], start=True, stop=True)
                    if e % 2:
                        last.then_inc(S["kv_ready"], 1)

            if l == 0:
                pe.wait_ge(S["mod_evac"], 10)
            key_values(0, 4)
            pe.wait_ge(S["za_evac"], l + 1)
            pe.wait_ge(S["zb_evac"], l + 1)
            pe.wait_ge(S["prep_wd"], 2 * l + 2)
            for c in range(2):
                for s in range(2):
                    last = mm(psA[:, c * 512:(c + 1) * 512], WCS[:, s, c, :], Zs[:, s, c, :], start=(s == 0), stop=(s == 1))
            last.then_inc(S["y_ready"], 1)
            if l == 0:
                pe.wait_ge(S["zc_evac"], 2)
                for c in range(2):
                    for s in range(2):
                        last = mm(psB[:, c * 256:(c + 1) * 256], WCS[:, s, c, :], Zc[:, s, c, :], start=(s == 0), stop=(s == 1))
                last.then_inc(S["y_ready"], 1)
            key_values(4, NST_E)
            pe.wait_ge(S["y_lo"], 2 * l + (2 if l == 0 else 1))
            n_items = 8 * TT[l]

            def retention(s):
                if s < TT[l]:
                    t, r = s, l * NT + s
                    tc = slice(t * P, (t + 1) * P)
                    if t >= 2:
                        pe.wait_ge(S["md_ready"], 2 * (r - 1))
                    for h in range(4):
                        q = slice(64 * (h % 2), 64 * (h % 2) + 64)
                        c0 = 512 * (h % 2) + P * (h // 2)
                        last = mm(pair[t % 2][:, c0:c0 + P], rkT[q, h // 2, tc], rqT[q, h // 2, tc], start=True, stop=True)
                    last.then_inc(S["sc_ready"], 1)
                    if t == 0:
                        keep_clock(psB, WARM)
                        pe.wait_ge(S["st_ready"], (l + 1) * 4 * NST_E)
                    pe.wait_ge(S["xq_ready"], 2 * r + 2)
                    if t >= 2:
                        pe.wait_ge(S["g_cent"], r - 1)
                    for d in range(2):
                        for q in range(2):
                            c0 = (t % 2) * 512 + d * 256 + q * P
                            mm(psS[:, c0:c0 + P], xq_at(t)[:, (2 * d + q) * P:(2 * d + q + 1) * P], SD[:, d, WALK[d].index(t), q, :], start=(d == 0 and q == 0), stop=False)
                if 1 <= s < TT[l] + 1:
                    t, r = s - 1, l * NT + s - 1
                    pe.wait_ge(S["md_ready"], 2 * r + 2)
                    for d in range(2):
                        for h in range(4):
                            c0 = (t % 2) * 512 + d * 256 + h * HD
                            last = mm(psS[:, c0:c0 + HD], md_at(t, d)[:, HPOS[h] * P:(HPOS[h] + 1) * P], Pr[:, t, 256 + h * HD:256 + (h + 1) * HD],
                                      start=False, stop=(d == 1 and h == 3))
                    last.then_inc(S["ret_ready"], 1)
                if s >= 4:
                    t, r = s - 4, l * NT + s - 4
                    pe.wait_ge(S["ro_ready"], r + 1)
                    if t >= 2:
                        pe.wait_ge(S["rT_lo"], r - 1)
                    for q in range(2):
                        last = tr((ps6, ps7)[t % 2][:, q * P:(q + 1) * P], sum_at(t)[:, q * P:(q + 1) * P])
                    last.then_inc(S["rT_ready"], 1)

            def attention(s):
                if s == 0:
                    pe.wait_ge(S["md_ready"], 2 * (l * NT + TT[l]))
                    pe.wait_ge(S["kl_ready"], 2 * l + 2)
                elif s == 2:
                    pe.wait_ge(S["g_cent"], l * NT + TT[l])
                if s < n_items:
                    it = ITEM_FIRST[l] + s
                    _, b, h, k = ITEMS[it]
                    ks, mprev, mnext = band(b)
                    nb = len(ks)
                    g = h // 4
                    q = qs[:, b % 2, g, h % 4, :]
                    hi_rows = slice(64 * g, 64 * g + 64)
                    if k == 0:
                        pe.wait_ge(S["qb_lo"], 2 * (l * NT + b) + 2)
                    dst = pair[it % 2]
                    if s >= 2:
                        pe.wait_ge(S["s_exp"], it - 1)
                    pieces = [(0, LAT, 2 * P)]
                    if nb:
                        pieces.append((2 * P, ks[0] * P, 2 * P))
                    if nb == 3:
                        pieces.append((4 * P, ks[2] * P, P))
                    for c0, k0, n in pieces:
                        mm(dst[:, c0:c0 + n], q, kh[:, g, k0:k0 + n], start=True, stop=False)
                        for i, mt in ((0, mprev), (1, mnext)):
                            if mt is not None and c0 <= (2 + mt) * P < c0 + n:
                                mm(dst[:, (2 + mt) * P:(3 + mt) * P], identb[:, :], maskb[:, i, :], start=False, stop=False)
                        last = mm(dst[:, c0:c0 + n], q[hi_rows], kl[hi_rows, k0:k0 + n], start=False, stop=True)
                    last.then_inc(S["s_ready"], 1)
                if 2 <= s < n_items + 2:
                    it = ITEM_FIRST[l] + s - 2
                    nk = len(band(ITEMS[it][1])[0]) + 2
                    pe.wait_ge(S["s_exp"], it + 1)
                    if s >= 3:
                        pe.wait_ge(S["pt_evac"], it)
                    for i in range(nk):
                        last = tr(psS[:, i * P:(i + 1) * P], Pb[:, it % 2, i * P:(i + 1) * P])
                    last.then_inc(S["pt_ready"], 1)
                if 3 <= s < n_items + 3:
                    it = ITEM_FIRST[l] + s - 3
                    _, b, h, k = ITEMS[it]
                    keys = [NL, NL + 1] + band(b)[0]
                    pe.wait_ge(S["pt_evac"], it + 1)
                    if k == 0 and b > 1:
                        pe.wait_ge(S["aoT_lo"], l * NT + b - 1)
                    for i, kt in enumerate(keys):
                        last = mm((ps6, ps7)[b % 2][:, h * HD:(h + 1) * HD], PTs[:, it % 2, i * P:(i + 1) * P],
                                  Pk[:, kt, P + (h // 4) * HD:P + (h // 4 + 1) * HD], start=(i == 0), stop=(i == len(keys) - 1))
                    last.then_inc(S["pv_ready"], 1)
                if s >= 12 and (s - 12) % 8 == 0 and (s - 12) // 8 < TT[l]:
                    b = (s - 12) // 8
                    pe.wait_ge(S["ao_ready"], l * NT + b + 1)
                    for q in range(4):
                        last = tr((ps6, ps7)[b % 2][:, q * P:(q + 1) * P], AO[:, q * P:(q + 1) * P])
                    last.then_inc(S["aoT_ready"], 1)

            for s in range(TT[l]):
                retention(s)
            for i in range(2):
                retention(TT[l] + i)
                attention(i)
            retention(TT[l] + 2)
            retention(TT[l] + 3)
            pe.wait_ge(S["rT_lo"], l * NT + TT[l])
            keep_clock(ps7, WARM)
            for s in range(2, n_items + 5):
                attention(s)
            pe.wait_ge(S["aoT_lo"], l * NT + TT[l])

            def tile(dst, slot, offs, hi_, lo_, opens=True, closes=True):
                for i, off in enumerate(offs):
                    wh, wl = Whi[:, slot, off:off + P], Wlo[:, slot, off:off + P]
                    first, fin = opens and i == 0, closes and i == len(offs) - 1
                    for wt, x, f, e in ((wh, hi_, first, False), (wh, lo_, False, False), (wl, hi_, False, fin)):
                        for c0, cn in SPLITS[l]:
                            last = mm(dst[:, c0:c0 + cn], wt, x[:, i, c0:c0 + cn], start=f, stop=e)
                return last

            k8 = [k * P for k in range(KT)]
            for u in range(UO):
                uu = u0 + UP + u
                pe.wait_ge(S["lo_done"], uu + 1)
                if u >= 2:
                    pe.wait_ge(S["resid_done"], 72 * l + u - 1)
                tile(pair[u % 2], uu % 2, k8, Ahi, Alo).then_inc(S["lin_ready"], 1)
                if l == 0 and u in (5, 7):
                    i = u // 2 - 2
                    pe.wait_ge(S["mod_evac"], 10 + i)
                    mod_sums(S["mod_used"], LATE - MOD0 + 4 * i + 3, 32 + 4 * i + 3, maccs[i])
            stats(2 * l + 1, TT[l])
            if l == 0:
                pe.wait_ge(S["mod_evac"], 12)
            spread(2 * l + 1, TT[l])

            pe.wait_ge(S["lo_done"], uf + 2)
            for k in range(KT):
                pe.wait_ge(*a_lo(2 * l + 1, k))
                for i in range(2):
                    last = tile(pair[i], (uf + i) % 2, k8[k:k + 1], Ahi[:, k:k + 1], Alo[:, k:k + 1], k == 0, k == KT - 1)
                    if k == KT - 1:
                        last.then_inc(S["lin_ready"], 1)
            for k in (2, 3):
                uu = uf + k
                pe.wait_ge(S["lo_done"], uu + 1)
                pe.wait_ge(S["relu_done"], 32 * l + k - 1)
                tile(pair[k % 2], uu % 2, k8, Ahi, Alo).then_inc(S["lin_ready"], 1)

            def ff2(c, par, k, uu, slot):
                pe.wait_ge(S["lo_done"], uu + 1)
                for o in range(2):
                    m = 2 * k + o
                    g = c * 8 + m
                    if m < 2:
                        pe.wait_ge(S["relu_done"], 32 * l + c * 4 + 7 + m)
                    else:
                        pe.wait_ge(S["resid_done"], 72 * l + 8 + g - 1)
                    if m == 0:
                        pe.wait_ge(S["h_lo"], 32 * l + c * 4 + 4)
                    offs = [i * 256 + o * P for i in range(CHUNK)]
                    last = tile(pair[m % 2], slot, offs, Hhi[:, par], Hlo[:, par])
                    last.then_inc(S["lin_ready"], 1)

            def half(c, par, mod):
                for k in range(8):
                    uu = uf + 4 + c * 8 + k
                    slot = (uf + k) % 2
                    if k < 4:
                        f = 32 * l + 4 + c * 4 + k
                        pe.wait_ge(S["lo_done"], uu + 1)
                        pe.wait_ge(S["relu_done"], f - 1)
                        if k < 2:
                            pe.wait_ge(S["resid_done"], 72 * l + 7 + c * 8 + k)
                        tile(pair[k % 2], slot, k8, Ahi, Alo).then_inc(S["lin_ready"], 1)
                    else:
                        ff2(c, par, k - 4, uu, slot)
                    if mod and k in (4, 7):
                        pe.wait_ge(S["mod_evac"], c * 2 + 12 + (k == 7))
                        j = 3 if k == 4 else 7
                        mod_sums(S["mod_used"], c * 8 + MOD1 - MOD0 + j, c * 8 + NMOD - 8 + j, macc)

            with pe.Fori(0, 3) as cc:
                half(cc * 2, 0, l == 0)
                half(cc * 2 + 1, 1, l == 0)
            half(6, 0, False)
            if l == 0:
                pe.wait_ge(S["mod_evac"], 24)
                fourier_weights(1)
            for k in range(4):
                uu = uf + 60 + k
                pe.wait_ge(S["lo_done"], uu + 1)
                for o in range(2):
                    m = 2 * k + o
                    pe.wait_ge(S["resid_done"], 72 * l + 8 + 56 + m - 1)
                    if m == 0:
                        pe.wait_ge(S["h_lo"], 32 * l + 32)
                    offs = [i * 256 + o * P for i in range(CHUNK)]
                    tile(pair[m % 2], uu % 2, offs, Hhi[:, 1], Hlo[:, 1]).then_inc(S["lin_ready"], 1)
            if l == 0:
                stats(2, NT)
        pe.wait_ge(S["resid_done"], 144)
        for t in range(NL):
            if t >= 2:
                pe.wait_ge(S["out_a"] if t % 2 == 0 else S["out_d"], t // 2)
            for m in range(KT):
                last = tr(pair[t % 2][:, m * P:(m + 1) * P], X[:, m, t * P:(t + 1) * P])
            last.then_inc(S["out_T"], 1)

    stack.close()


def tables():
    import numpy as np
    f = np.float32
    i = np.arange(P)
    tab = np.zeros((P, TABLE), f)
    tab[:, T_ID:T_ID + P] = np.eye(P)
    q, k = i[:, None], i[None, :]
    tab[:, T_MPREV:T_MPREV + P] = np.where(k >= q, 0.0, -1e30)
    tab[:, T_MNEXT:T_MNEXT + P] = np.where(k <= q, 0.0, -1e30)
    tok = np.arange(LAT)

    def cs(pos, half):
        fr = (f(10000.0) ** (-np.arange(half, dtype=f) / f(half))).astype(f)
        ang = (pos.astype(f)[:, None] * fr[None, :]).astype(f).astype(np.float64)
        return np.cos(ang), np.sin(ang)

    rc, rsn = cs(tok // 64, 16)
    cc, csn = cs(tok % 64, 16)
    tc, tsn = cs(tok, 32)
    rope = np.stack([np.concatenate([rc, rc, cc, cc], 1), np.concatenate([-rsn, rsn, -csn, csn], 1),
                     np.concatenate([tc, tc], 1), np.concatenate([-tsn, tsn], 1)], 1)
    tab[:, T_ROPE:T_TMP] = rope.reshape(NL, P, 4 * HD).transpose(1, 0, 2).reshape(P, -1)
    t0 = tab[:, T_TMP:]
    kq = i[None, :] - i[:, None]
    t0[:, TMP_DPOS:TMP_DPOS + P] = np.maximum(kq, 0)
    t0[:, TMP_DNEG:TMP_DNEG + P] = np.maximum(-kq, 0)
    t0[:, TMP_MPOS:TMP_MPOS + P] = kq >= 0
    t0[:, TMP_MNEG:TMP_MNEG + P] = kq <= 0
    j = np.arange(HD)
    ang = 2 * np.pi * (np.outer(j, j) % HD) / HD
    for s, m in enumerate((np.cos(ang), -np.sin(ang))):
        for b in range(2):
            t0[b * HD:(b + 1) * HD, TMP_C + s * P + b * HD:TMP_C + s * P + (b + 1) * HD] = m
    t0[:, TMP_IDX:TMP_IDX + 2] = np.stack([P - 1 - i, i], 1)
    t0[:, TMP_XI:TMP_XI + 2 * P] = np.concatenate([i + 1, P - i])[None]

    def dft(n):
        w = 2 * np.pi * (np.outer(np.arange(n), np.arange(n)) % n) / n
        w = w[:, :n // 2 + 1]
        return (np.stack([np.cos(w), np.sin(w)]) / np.sqrt(n * HD)).astype(f)

    lat = dft(LAT).reshape(2, NL, P, FL).transpose(1, 2, 0, 3).reshape(NL, P, 2 * FL)
    ctx = dft(CTX).reshape(2, 2, P, FC).transpose(2, 0, 1, 3).reshape(P, 4 * FC)
    return {"table": tab, "dft_lat": np.ascontiguousarray(lat), "dft_ctx": np.ascontiguousarray(ctx)}


_INS = ["x", "c", "ctx", "c_ctx", "w_mod", "b_mod", "norm1_g", "norm2_g", "w_in", "w_out", "q_norm_g", "k_norm_g",
        "attn_sink", "ret_decay_logit", "ret_gn_g", "fourier_w", "w_ff1", "w_ff2"]


def kernel(**inputs):
    import numpy as _np
    import concourse.bacc as _bacc
    from concourse import mybir as _mybir
    from concourse.bass_utils import run_bass_kernel_spmd as _run

    nc = _bacc.Bacc("TRN2", target_bir_lowering=False, num_devices=1)
    arrays, args = {}, {}
    consts = tables()
    for name in _INS + list(consts):
        v = _np.ascontiguousarray(consts[name] if name in consts else inputs[name])
        arrays[f"in_{name}_dram"] = v
        args[name] = nc.dram_tensor(f"in_{name}_dram", v.shape, _mybir.dt.from_np(v.dtype), kind="ExternalInput").ap()
    args["out"] = nc.dram_tensor("out_0_dram", (1, LAT, D), _mybir.dt.float32, kind="ExternalOutput").ap()
    build(nc, args)
    r = _run(nc, [arrays], core_ids=[0])
    return r.results[0]["out_0_dram"]
```
